# Optimizing a Trainium2 kernel written in Bass

```python
import math
import jax
import jax.numpy as jnp
from jax import lax
import numpy as np

D_MODEL = 2048
BATCH = 1
SEQ = 512
DEPTH = 1
DEC_BATCH = 8
DEC_SEQ = 8
PAST_LEN = 4096
PAGE_SIZE = 128

MIX_WIDTH = D_MODEL
GLA_WIDTH = 3 * MIX_WIDTH // 8
ML_WIDTH = 3 * MIX_WIDTH // 8
S5_WIDTH = MIX_WIDTH - GLA_WIDTH - ML_WIDTH
GLA_HEADS = 6
GLA_DV = GLA_WIDTH // GLA_HEADS
GLA_DK = GLA_DV // 2
GLA_RANK = 16
GLA_TAU = 16.0
GLA_CHUNK = 16
ML_HEADS = 6
ML_DH = ML_WIDTH // ML_HEADS
ML_CHUNK = 64
S5_CH = 16
S5_GROUPS = S5_WIDTH // S5_CH
S5_P = 64
PEER_HEADS = 8
PEER_DQ = 256
N_KEYS = 128
N_EXPERTS = N_KEYS * N_KEYS
PEER_TOPK = 16
PEER_BLOCK = 64
NORM_EPS = 1e-6
IN_SPLITS = (GLA_HEADS * GLA_DK, GLA_HEADS * GLA_DK, GLA_WIDTH, GLA_WIDTH, GLA_RANK,
             ML_WIDTH, ML_WIDTH, ML_WIDTH, ML_WIDTH, ML_HEADS, ML_HEADS, S5_WIDTH)
IN_COLS = 2 * GLA_HEADS * GLA_DK + 2 * GLA_WIDTH + GLA_RANK + 4 * ML_WIDTH + 2 * ML_HEADS + S5_WIDTH

kernel_name = 'hymba_gla_mlstm_s5_peer_adaln_step'

def _rms(x, gain=None):
    xf = x.astype(jnp.float32)
    y = xf * lax.rsqrt(jnp.mean(xf * xf, axis=-1, keepdims=True) + NORM_EPS)
    if gain is not None:
        y = y * gain.astype(jnp.float32)
    return y

def _split_cols(z):
    parts = []
    start = 0
    for width in IN_SPLITS:
        parts.append(z[..., start:start + width])
        start += width
    return parts

def _to_chunks(t, n, chunk):
    bsz = t.shape[0]
    return t.reshape(bsz, n, chunk, t.shape[2], t.shape[3]).transpose(1, 0, 3, 2, 4)

def _from_chunks(t):
    n, bsz, heads, chunk, d = t.shape
    return t.transpose(1, 0, 3, 2, 4).reshape(bsz, n * chunk, heads, d)

def _gla(q, k, v, g, r, w_gate_up, b_gate, gain, s0):
    bsz, seq = q.shape[0], q.shape[1]
    q = q.reshape(bsz, seq, GLA_HEADS, GLA_DK) * (GLA_DK ** -0.5)
    k = k.reshape(bsz, seq, GLA_HEADS, GLA_DK)
    v = v.reshape(bsz, seq, GLA_HEADS, GLA_DV)
    log_a = jax.nn.log_sigmoid(r @ w_gate_up.astype(jnp.float32) + b_gate.astype(jnp.float32)) / GLA_TAU
    log_a = log_a.reshape(bsz, seq, GLA_HEADS, GLA_DK)
    chunk = math.gcd(seq, GLA_CHUNK)
    n = seq // chunk
    mask = jnp.tril(jnp.ones((chunk, chunk), dtype=bool))

    def step(s, inp):
        qc, kc, vc, lac = inp
        b = jnp.cumsum(lac, axis=2)
        b_last = b[:, :, -1:, :]
        q_dec = qc * jnp.exp(b)
        k_inv = kc * jnp.exp(-b)
        o_inter = jnp.einsum('bhck,bhkv->bhcv', q_dec, s)
        att = jnp.where(mask, jnp.einsum('bhik,bhjk->bhij', q_dec, k_inv), 0.0)
        o = o_inter + jnp.einsum('bhij,bhjv->bhiv', att, vc)
        k_dec = kc * jnp.exp(b_last - b)
        s_new = jnp.exp(b_last[:, :, 0, :])[..., None] * s + jnp.einsum('bhck,bhcv->bhkv', k_dec, vc)
        return s_new, o

    s_fin, o = lax.scan(step, s0, (_to_chunks(q, n, chunk), _to_chunks(k, n, chunk),
                                  _to_chunks(v, n, chunk), _to_chunks(log_a, n, chunk)))
    o = _rms(_from_chunks(o)).reshape(bsz, seq, GLA_WIDTH)
    o = o * gain.astype(jnp.float32) * jax.nn.silu(g)
    return o, s_fin

def _mlstm(q, k, v, o_pre, i_pre, f_pre, b_i, b_f, gain, c0, n0, m0):
    bsz, seq = q.shape[0], q.shape[1]
    q = q.reshape(bsz, seq, ML_HEADS, ML_DH) * (ML_DH ** -0.5)
    k = k.reshape(bsz, seq, ML_HEADS, ML_DH)
    v = v.reshape(bsz, seq, ML_HEADS, ML_DH)
    log_i = i_pre + b_i.astype(jnp.float32)
    log_f = jax.nn.log_sigmoid(f_pre + b_f.astype(jnp.float32))
    chunk = math.gcd(seq, ML_CHUNK)
    n = seq // chunk
    mask = jnp.tril(jnp.ones((chunk, chunk), dtype=bool))

    def step(carry, inp):
        c_st, n_st, m_st = carry
        qc, kc, vc, ic, fc = inp
        b = jnp.cumsum(fc, axis=-1)
        g_inter = b + m_st[..., None]
        d_log = jnp.where(mask, b[..., :, None] - b[..., None, :] + ic[..., None, :], -jnp.inf)
        m_t = jnp.maximum(g_inter, jnp.max(d_log, axis=-1))
        w_inter = jnp.exp(g_inter - m_t)
        s = jnp.einsum('bhik,bhjk->bhij', qc, kc) * jnp.exp(d_log - m_t[..., None])
        num = w_inter[..., None] * jnp.einsum('bhck,bhkv->bhcv', qc, c_st) + jnp.einsum('bhij,bhjv->bhiv', s, vc)
        den = w_inter * jnp.einsum('bhck,bhk->bhc', qc, n_st) + jnp.sum(s, axis=-1)
        h = num / jnp.maximum(jnp.abs(den), jnp.exp(-m_t))[..., None]
        m_last = m_t[..., -1]
        decay = jnp.exp(b[..., -1] + m_st - m_last)
        w_k = jnp.exp(b[..., -1:] - b + ic - m_last[..., None])
        c_new = decay[..., None, None] * c_st + jnp.einsum('bhc,bhck,bhcv->bhkv', w_k, kc, vc)
        n_new = decay[..., None] * n_st + jnp.einsum('bhc,bhck->bhk', w_k, kc)
        return (c_new, n_new, m_last), h

    gates_i = _to_chunks(log_i[..., None], n, chunk)[..., 0]
    gates_f = _to_chunks(log_f[..., None], n, chunk)[..., 0]
    (c_fin, n_fin, m_fin), h = lax.scan(step, (c0, n0, m0),
                                        (_to_chunks(q, n, chunk), _to_chunks(k, n, chunk),
                                         _to_chunks(v, n, chunk), gates_i, gates_f))
    h = _rms(_from_chunks(h)).reshape(bsz, seq, ML_WIDTH)
    h = h * gain.astype(jnp.float32) * jax.nn.sigmoid(o_pre)
    return h, c_fin, n_fin, m_fin

def _cscan_combine(e1, e2):
    a1r, a1i, b1r, b1i = e1
    a2r, a2i, b2r, b2i = e2
    return (a2r * a1r - a2i * a1i, a2r * a1i + a2i * a1r,
            a2r * b1r - a2i * b1i + b2r, a2r * b1i + a2i * b1r + b2i)

def _s5(u, lam_re, lam_im, log_dt, b_re, b_im, c_re, c_im, d_skip, w_glu, b_glu, gain, h0_re, h0_im):
    f32 = jnp.float32
    bsz, seq = u.shape[0], u.shape[1]
    lam_re = lam_re.astype(f32)
    lam_im = lam_im.astype(f32)
    ug = u.reshape(bsz, seq, S5_GROUPS, S5_CH)
    dt = jnp.exp(log_dt.astype(f32))[:, None]
    mag = jnp.exp(lam_re * dt)
    ar = mag * jnp.cos(lam_im * dt)
    ai = mag * jnp.sin(lam_im * dt)
    den = lam_re * lam_re + lam_im * lam_im
    fr = ((ar - 1.0) * lam_re + ai * lam_im) / den
    fi = (ai * lam_re - (ar - 1.0) * lam_im) / den
    b_re = b_re.astype(f32)
    b_im = b_im.astype(f32)
    bbar_re = fr[..., None] * b_re - fi[..., None] * b_im
    bbar_im = fr[..., None] * b_im + fi[..., None] * b_re
    bu_re = jnp.einsum('blgh,gph->blgp', ug, bbar_re)
    bu_im = jnp.einsum('blgh,gph->blgp', ug, bbar_im)
    bu_re = bu_re.at[:, 0].add(ar * h0_re - ai * h0_im)
    bu_im = bu_im.at[:, 0].add(ar * h0_im + ai * h0_re)
    a_re = jnp.broadcast_to(ar, bu_re.shape)
    a_im = jnp.broadcast_to(ai, bu_im.shape)
    _, _, h_re, h_im = lax.associative_scan(_cscan_combine, (a_re, a_im, bu_re, bu_im), axis=1)
    y = (jnp.einsum('blgp,ghp->blgh', h_re, c_re.astype(f32))
         - jnp.einsum('blgp,ghp->blgh', h_im, c_im.astype(f32))
         + d_skip.astype(f32) * ug)
    y = jax.nn.gelu(y.reshape(bsz, seq, S5_WIDTH))
    out = y * jax.nn.sigmoid(y @ w_glu + b_glu)
    return _rms(out, gain), h_re[:, -1], h_im[:, -1]

def _peer(h, w_q, sub_keys, u_tab, v_tab):
    bsz, seq, dm = h.shape
    n_tok = bsz * seq
    pad = (-n_tok) % PEER_BLOCK
    xt = jnp.pad(h.reshape(n_tok, dm), ((0, pad), (0, 0)))
    blocks = xt.reshape(-1, PEER_BLOCK, dm)

    def one_block(xb):
        q = (xb @ w_q).reshape(PEER_BLOCK, PEER_HEADS, 2, PEER_DQ // 2)
        scores = jnp.einsum('bhsd,hskd->bhsk', q, sub_keys).astype(jnp.float32)
        sv, si = lax.top_k(scores, PEER_TOPK)
        cand = sv[:, :, 0, :, None] + sv[:, :, 1, None, :]
        cidx = si[:, :, 0, :, None] * N_KEYS + si[:, :, 1, None, :]
        cand = cand.reshape(PEER_BLOCK, PEER_HEADS, PEER_TOPK * PEER_TOPK)
        cidx = cidx.reshape(PEER_BLOCK, PEER_HEADS, PEER_TOPK * PEER_TOPK)
        top_v, top_pos = lax.top_k(cand, PEER_TOPK)
        eidx = jnp.take_along_axis(cidx, top_pos, axis=-1)
        gate = jax.nn.softmax(top_v, axis=-1)
        u_sel = jnp.take(u_tab, eidx, axis=0)
        act = jax.nn.gelu(jnp.einsum('bhkd,bd->bhk', u_sel, xb))
        v_sel = jnp.take(v_tab, eidx, axis=0)
        return jnp.einsum('bhk,bhkd->bd', gate * act, v_sel)

    out = lax.map(one_block, blocks).reshape(-1, dm)[:n_tok]
    return out.reshape(bsz, seq, dm)

def _layer(x, c, st, p):
    (w_ada, b_ada, norm_gain, w_in, gla_w_gate_up, gla_b_gate, gla_gain, ml_b_i, ml_b_f, ml_gain,
     s5_lre, s5_lim, s5_logdt, s5_bre, s5_bim, s5_cre, s5_cim, s5_d, s5_wglu, s5_bglu, s5_gain,
     w_out, peer_wq, peer_keys, peer_u, peer_v) = p
    s_gla, m_c, m_n, m_m, h_re, h_im = st
    mod = jax.nn.silu(c.astype(jnp.float32)) @ w_ada + b_ada
    sh1, sc1, g1, sh2, sc2, g2 = jnp.split(mod, 6, axis=-1)
    h = _rms(x, norm_gain[0]) * (1.0 + sc1[:, None]) + sh1[:, None]
    z = h @ w_in
    gq, gk, gv, gg, gr, mq, mk, mv, mo, mi, mf, su = _split_cols(z)
    o_gla, s_gla = _gla(gq, gk, gv, gg, gr, gla_w_gate_up, gla_b_gate, gla_gain, s_gla)
    o_ml, m_c, m_n, m_m = _mlstm(mq, mk, mv, mo, mi, mf, ml_b_i, ml_b_f, ml_gain, m_c, m_n, m_m)
    o_s5, h_re, h_im = _s5(su, s5_lre, s5_lim, s5_logdt, s5_bre, s5_bim, s5_cre, s5_cim, s5_d,
                           s5_wglu, s5_bglu, s5_gain, h_re, h_im)
    mix = jnp.concatenate([o_gla, o_ml, o_s5], axis=-1) @ w_out
    x = x + (g1[:, None] * mix).astype(x.dtype)
    h = _rms(x, norm_gain[1]) * (1.0 + sc2[:, None]) + sh2[:, None]
    x = x + (g2[:, None] * _peer(h, peer_wq, peer_keys, peer_u, peer_v)).astype(x.dtype)
    return x, (s_gla, m_c, m_n, m_m, h_re, h_im)

def _trunk(x, c, states, params, final_gain):
    new_states = []
    for layer in range(DEPTH):
        st = tuple(s[layer].astype(jnp.float32) for s in states)
        pl = tuple(w[layer] for w in params)
        x, st = _layer(x, c, st, pl)
        new_states.append(st)
    y = _rms(x, final_gain).astype(x.dtype)
    stacked = tuple(jnp.stack([ns[i] for ns in new_states]) for i in range(6))
    return y, stacked

def setup_inputs(seed: int = 0) -> dict:
    key = jax.random.key(seed)
    ks = iter(jax.random.split(key, 48))
    f32 = jnp.float32

    def nrm(shape, scale):
        return jax.random.normal(next(ks), shape, f32) * scale

    return {
        'x_prompt': nrm((BATCH, SEQ, D_MODEL), 1.0),
        'x_sample': nrm((DEC_BATCH, DEC_SEQ, D_MODEL), 1.0),
        'state_gla': nrm((DEPTH, DEC_BATCH, GLA_HEADS, GLA_DK, GLA_DV), 0.1),
        'state_mlstm_c': nrm((DEPTH, DEC_BATCH, ML_HEADS, ML_DH, ML_DH), 0.1),
        'state_mlstm_n': nrm((DEPTH, DEC_BATCH, ML_HEADS, ML_DH), 0.3),
        'state_mlstm_m': 2.0 + nrm((DEPTH, DEC_BATCH, ML_HEADS), 0.5),
        'state_s5_re': nrm((DEPTH, DEC_BATCH, S5_GROUPS, S5_P), 0.3),
        'state_s5_im': nrm((DEPTH, DEC_BATCH, S5_GROUPS, S5_P), 0.3),
        'c_prompt': nrm((BATCH, D_MODEL), 1.0),
        'c_sample': nrm((DEC_BATCH, D_MODEL), 1.0),
        'w_ada': nrm((DEPTH, D_MODEL, 6 * D_MODEL), 0.5 * D_MODEL ** -0.5),
        'b_ada': nrm((DEPTH, 6 * D_MODEL), 0.02),
        'norm_gain': 1.0 + nrm((DEPTH, 2, D_MODEL), 0.01),
        'w_in': nrm((DEPTH, D_MODEL, IN_COLS), D_MODEL ** -0.5),
        'gla_w_gate_up': nrm((DEPTH, GLA_RANK, GLA_HEADS * GLA_DK), GLA_RANK ** -0.5),
        'gla_b_gate': 1.0 + nrm((DEPTH, GLA_HEADS * GLA_DK), 0.1),
        'gla_norm_gain': 1.0 + nrm((DEPTH, GLA_WIDTH), 0.01),
        'ml_b_igate': nrm((DEPTH, ML_HEADS), 0.1),
        'ml_b_fgate': jnp.linspace(3.0, 6.0, ML_HEADS, dtype=f32)[None, :] + nrm((DEPTH, ML_HEADS), 0.1),
        'ml_norm_gain': 1.0 + nrm((DEPTH, ML_WIDTH), 0.01),
        's5_lambda_re': -0.5 + nrm((DEPTH, S5_GROUPS, S5_P), 0.01),
        's5_lambda_im': math.pi * jnp.arange(S5_P, dtype=f32)[None, None, :] + nrm((DEPTH, S5_GROUPS, S5_P), 0.01),
        's5_log_dt': jax.random.uniform(next(ks), (DEPTH, S5_GROUPS), f32, math.log(1e-3), math.log(1e-1)),
        's5_b_re': nrm((DEPTH, S5_GROUPS, S5_P, S5_CH), (2 * S5_CH) ** -0.5),
        's5_b_im': nrm((DEPTH, S5_GROUPS, S5_P, S5_CH), (2 * S5_CH) ** -0.5),
        's5_c_re': nrm((DEPTH, S5_GROUPS, S5_CH, S5_P), 0.5),
        's5_c_im': nrm((DEPTH, S5_GROUPS, S5_CH, S5_P), 0.5),
        's5_d': nrm((DEPTH, S5_GROUPS, S5_CH), 0.5),
        's5_w_glu': nrm((DEPTH, S5_WIDTH, S5_WIDTH), S5_WIDTH ** -0.5),
        's5_b_glu': nrm((DEPTH, S5_WIDTH), 0.02),
        's5_norm_gain': 1.0 + nrm((DEPTH, S5_WIDTH), 0.01),
        'w_out': nrm((DEPTH, MIX_WIDTH, D_MODEL), MIX_WIDTH ** -0.5),
        'peer_w_q': nrm((DEPTH, D_MODEL, PEER_HEADS * PEER_DQ), D_MODEL ** -0.5),
        'peer_sub_keys': nrm((DEPTH, PEER_HEADS, 2, N_KEYS, PEER_DQ // 2), (PEER_DQ // 2) ** -0.5),
        'peer_u': nrm((DEPTH, N_EXPERTS, D_MODEL), D_MODEL ** -0.5),
        'peer_v': nrm((DEPTH, N_EXPERTS, D_MODEL), 0.5),
        'final_gain': 1.0 + nrm((D_MODEL,), 0.01),
    }

def reference(x_prompt, x_sample, state_gla, state_mlstm_c, state_mlstm_n, state_mlstm_m,
              state_s5_re, state_s5_im, c_prompt, c_sample,
              w_ada, b_ada, norm_gain, w_in, gla_w_gate_up, gla_b_gate, gla_norm_gain,
              ml_b_igate, ml_b_fgate, ml_norm_gain,
              s5_lambda_re, s5_lambda_im, s5_log_dt, s5_b_re, s5_b_im, s5_c_re, s5_c_im, s5_d,
              s5_w_glu, s5_b_glu, s5_norm_gain, w_out, peer_w_q, peer_sub_keys, peer_u, peer_v,
              final_gain):
    f32 = jnp.float32
    params = (w_ada, b_ada, norm_gain, w_in, gla_w_gate_up, gla_b_gate, gla_norm_gain,
              ml_b_igate, ml_b_fgate, ml_norm_gain,
              s5_lambda_re, s5_lambda_im, s5_log_dt, s5_b_re, s5_b_im, s5_c_re, s5_c_im, s5_d,
              s5_w_glu, s5_b_glu, s5_norm_gain, w_out, peer_w_q, peer_sub_keys, peer_u, peer_v)
    bp = x_prompt.shape[0]
    zero_states = (jnp.zeros((DEPTH, bp, GLA_HEADS, GLA_DK, GLA_DV), f32),
                   jnp.zeros((DEPTH, bp, ML_HEADS, ML_DH, ML_DH), f32),
                   jnp.zeros((DEPTH, bp, ML_HEADS, ML_DH), f32),
                   jnp.zeros((DEPTH, bp, ML_HEADS), f32),
                   jnp.zeros((DEPTH, bp, S5_GROUPS, S5_P), f32),
                   jnp.zeros((DEPTH, bp, S5_GROUPS, S5_P), f32))
    sample_states = (state_gla, state_mlstm_c, state_mlstm_n, state_mlstm_m, state_s5_re, state_s5_im)
    y_prompt, sp = _trunk(x_prompt, c_prompt, zero_states, params, final_gain)
    y_sample, ss = _trunk(x_sample, c_sample, sample_states, params, final_gain)
    return (y_prompt, y_sample,
            sp[0].astype(state_gla.dtype), ss[0].astype(state_gla.dtype),
            sp[1].astype(state_mlstm_c.dtype), ss[1].astype(state_mlstm_c.dtype),
            sp[2].astype(state_mlstm_n.dtype), ss[2].astype(state_mlstm_n.dtype),
            sp[3].astype(state_mlstm_m.dtype), ss[3].astype(state_mlstm_m.dtype),
            sp[4].astype(state_s5_re.dtype), ss[4].astype(state_s5_re.dtype),
            sp[5].astype(state_s5_im.dtype), ss[5].astype(state_s5_im.dtype))


_drawn_inputs = setup_inputs


def setup_inputs(seed=0):
    import zlib

    import numpy as np

    out = dict(_drawn_inputs(seed))
    spreads = {}
    factors = {'gla_norm_gain': 200.0,
     'ml_b_igate': 3.879,
     'ml_norm_gain': 200.0,
     's5_lambda_re': 70.225,
     's5_b_glu': 8.0,
     's5_norm_gain': 200.0,
     'final_gain': 170.395,
     'peer_w_q': 8.0,
     'peer_sub_keys': 8.0,
     'peer_u': 8.0,
     'peer_v': 8.0}
    for name, (base, spread) in spreads.items():
        noise = np.random.default_rng([zlib.crc32(name.encode()), seed]).standard_normal(out[name].shape)
        drawn = base * np.exp(spread * noise) if base else spread * noise
        out[name] = jnp.asarray(drawn.astype(out[name].dtype))
    for name, factor in factors.items():
        out[name] = (out[name] * factor).astype(out[name].dtype)
    return out
```

```python
from contextlib import ExitStack

import numpy as np

import concourse.bass as bass
from concourse import mybir

ALU = mybir.AluOpType
ACT = mybir.ActivationFunctionType
AX = mybir.AxisListType
F32 = mybir.dt.float32
U32 = mybir.dt.uint32
I32 = mybir.dt.int32

P = 128
D = 2048
KC = D // P
NSEQ, SLEN = 8, 8
TP, TS = 512, NSEQ * SLEN
T = TP + TS
HALF = T // 2
NT = 5
EPS = 1e-6
HEADS = 6
GDK, MDH = 64, 128
GC, GMID = 32, 15
SMID = 3
GTAU = 16.0
S5C, S5CH, S5P = 16, 16, 64
PH, NK, TOPK = 8, 128, 16
GRP = 4
ROUNDS = NK // GRP
TBLK = 64
WT = 256
NCOND = 1 + NSEQ

Z_GG, Z_MO, Z_SU, Z_GQ, Z_GK, Z_MQ, Z_MK, Z_N = 0, 6, 12, 16, 19, 22, 28, 34
V_NG1, V_NG2, V_FG, V_BADA, V_GG, V_MG, V_SG, V_BGLU, V_SD, V_BG, V_LRE, V_LIM, V_LDT, V_N = (
    0, 16, 32, 48, 144, 150, 156, 160, 164, 168, 171, 187, 203, 219)

BIG = 1.0e30
TWO_PI_HI = 6.28125
TWO_PI_LO = float(2 * np.pi - 6.28125)
ROUNDER = 12582912.0


class Chain:

    def __init__(self, eng, sem):
        self.eng, self.sem, self.n, self.loop = eng, sem, 0, None

    def value(self):
        return self.n if self.loop is None else self.loop + self.n

    def __call__(self, ins):
        self.n += 1
        ins.then_inc(self.sem, 1)
        self.eng.wait_ge(self.sem, self.value())

    def enter(self, i, per):
        self.loop, self.start, self.per = i * per, self.n, per

    def leave(self, count):
        assert self.n - self.start == self.per, (self.n - self.start, self.per)
        self.n, self.loop = self.start + self.per * count, None


def build(nc, a, o):
    ctx = ExitStack()
    with ctx:
        def sb(name, cols, dt=F32, rows=P):
            return ctx.enter_context(nc.sbuf_tensor(name, [rows, cols], dt))

        def sem(name):
            return ctx.enter_context(nc.semaphore(name))

        ident, ones, iota = sb("ident", P), sb("ones", P), sb("iota", P)
        vec = sb("vec", V_N)
        modT = sb("modT", 96 * NCOND)
        siluc = sb("siluc", KC * NCOND)
        scaleg = sb("scaleg", KC * NCOND)
        gla_mask, gla_smask = sb("gla_mask", P, U32), sb("gla_smask", TS, U32, TS)
        cap, scap = sb("cap", P), sb("scap", TS, F32, TS)
        segm = sb("segm", NSEQ, F32, TS)
        gla_reset, ml_reset = sb("gla_reset", T), sb("ml_reset", T, F32, 32)
        sel = sb("sel", HEADS * P, F32, 32)
        gbias = sb("gbias", 2, F32, HEADS)
        m0 = sb("m0", NSEQ, F32, HEADS)
        rstd = sb("rstd", T)
        gate_tmp = sb("gate_tmp", TS)[:, :]
        attw = sb("attw", 4 * P + 2 * TS)

        AR = 46400
        arena = sb("arena", AR)

        def at(off, n, rows=P):
            assert off + n <= AR
            return arena[0:rows, off:off + n]

        HT, RING, ZF = 0, KC * T, KC * T + 2 * KC * WT
        VT = ZF + Z_N * T
        SM = VT + NT * 1536
        hT = at(HT, KC * T).rearrange("p (c t) -> p c t", t=T)
        ring = [at(RING + s * KC * WT, KC * WT).rearrange("p (c n) -> p c n", c=KC) for s in range(2)]
        zF = at(ZF, Z_N * T).rearrange("p (c t) -> p c t", t=T)
        xT = at(ZF, KC * T).rearrange("p (c t) -> p c t", t=T)
        sq = at(VT, 2 * T).rearrange("p (b t) -> p b t", t=T)
        vT = at(VT, NT * 1536).rearrange("p (n c) -> p n c", c=1536)
        wsmall = at(ZF + Z_N * T - KC * 70, KC * 70).rearrange("p (c n) -> p c n", n=70)
        rows = at(SM, 3 * T).rearrange("p (r t) -> p r t", t=T)
        mixT = zF[:, 0:KC, :]

        SC = 0
        g_la = at(SC, 3 * T).rearrange("p (c t) -> p c t", t=T)
        g_B = at(SC + 3 * T, 3 * T).rearrange("p (c t) -> p c t", t=T)
        g_e1 = at(SC + 6 * T, 3 * T).rearrange("p (c t) -> p c t", t=T)
        g_e2 = at(SC + 9 * T, 3 * T).rearrange("p (c t) -> p c t", t=T)
        g_out = at(SC + 6 * T, 6 * T).rearrange("p (c t) -> p c t", t=T)
        q0 = SC + 12 * T
        g_kd = at(q0, NT * 384).rearrange("p (n c) -> p n c", c=384)
        g_Sm = at(q0 + 1920, 16 * P).rearrange("p (n c) -> p n c", c=P)
        g_S0 = at(q0 + 3968, 8 * P).rearrange("p (n c) -> p n c", c=P)
        g_S0m = at(q0 + 4992, 8 * P).rearrange("p (n c) -> p n c", c=P)
        g_kdm = at(q0 + 6016, 8 * P, TS).rearrange("p (n c) -> p n c", c=P)
        g_S = at(q0 + 7040, 2 * P).rearrange("p (n c) -> p n c", c=P)
        g_wgu = at(q0 + 7296, 384, 16)
        g_sc = at(q0 + 7680, 3 * 3 * 24).rearrange("p (k c n) -> p k c n", k=3, n=24)
        assert q0 + 7680 + 216 <= ZF

        r0 = 0
        m_rows = at(r0, 7 * T, 32).rearrange("p (r t) -> p r t", t=T)
        m_small = at(r0 + 7 * T, 64, 32)
        m_col = at(r0 + 7 * T + 64, 2 * NT * HEADS).rearrange("p (k n h) -> p k n h", k=2, h=HEADS)
        m_dec = at(r0 + 7 * T + 128, HEADS * 12).rearrange("p (h n) -> p h n", n=12)
        r1 = r0 + 7 * T + 256
        m_qw = at(r1, T)
        m_E = at(r1 + T, T)
        m_D = at(r1 + 2 * T, T)
        m_kw = at(r1 + 3 * T, NT * P).rearrange("p (n c) -> p n c", c=P)
        r2 = r1 + 3 * T + NT * P
        m_C = at(r2, 4 * 129).rearrange("p (n c) -> p n c", c=129)
        m_Cs = at(r2 + 516, 2 * NSEQ * 129).rearrange("p (k n c) -> p k n c", k=2, c=129)
        m_nb = at(r2 + 516 + 2064, 3 * P).rearrange("p (n c) -> p n c", c=P)
        m_nbs = at(r2 + 516 + 2064 + 384, NSEQ * P).rearrange("p (n c) -> p n c", c=P)
        m_kwm = at(r2 + 516 + 2064 + 384 + 1024, NSEQ * P, TS).rearrange("p (n c) -> p n c", c=P)
        att_p = attw[:, 0:4 * P].rearrange("p (n h c) -> p n h c", n=2, h=2)
        att_s = attw[:, 4 * P:4 * P + 2 * TS].rearrange("p (h c) -> p h c", h=2)
        m_h = [zF[:, Z_MQ + h, :] for h in range(HEADS)]
        assert r2 + 516 + 2064 + 384 + 2048 <= ZF

        def raw_head(c):
            return zF[:, Z_MQ + c - 6] if c >= 6 else zF[:, (Z_GK if c % 2 else Z_GQ) + c // 2]

        n_sq = at(0, 2 * T).rearrange("p (b t) -> p b t", t=T)
        n_rs = at(2 * T, 2 * T).rearrange("p (b t) -> p b t", t=T)
        n_sg = at(4 * T, 2 * T).rearrange("p (b t) -> p b t", t=T)

        TC = P
        s_tab = at(0, 2 * S5C * TC).rearrange("p (k s t) -> p k s t", k=2, s=S5C)
        s_BT = at(VT, 2 * S5C * P).rearrange("p (k s c) -> p k s c", k=2, c=P)
        s_CT = at(5120, 2 * S5C * 32).rearrange("p (k s c) -> p k s c", k=2, c=32)
        s_t = at(6144, 4 * 4 * TC).rearrange("p (k s t) -> p k s t", k=4, t=TC)
        s_in = at(8192, 2 * 4 * 160).rearrange("p (k s t) -> p k s t", k=2, t=160)
        s_g = at(9472, 2 * 4 * 160).rearrange("p (k s t) -> p k s t", k=2, t=160)
        s_h = at(10752, 2 * 4 * TC).rearrange("p (k s t) -> p k s t", k=2, t=TC)
        s_g0 = at(11776, 2 * S5C).rearrange("p (k s) -> p k s", k=2)
        s_h0 = at(11808, 2 * S5C * NSEQ).rearrange("p (k s b) -> p k s b", k=2, b=NSEQ)
        s_hn = at(12064, 2 * S5C * NSEQ).rearrange("p (k s b) -> p k s b", k=2, b=NSEQ)
        s_hp = at(12320, 2 * S5C).rearrange("p (k s) -> p k s", k=2)
        s_par = at(12352, 16 * S5C).rearrange("p (k s) -> p k s", k=16)
        s_rho = at(12608, TC)
        s_rhos = at(12736, 72)
        s_B = at(12864, 4 * S5C * 32).rearrange("p (k s c) -> p k s c", k=4, c=32)
        s_rhosm = at(4096, 72)
        assert 12864 + 2048 <= ZF
        s_gl = at(ZF + Z_GQ * T, 4 * T).rearrange("p (c t) -> p c t", t=T)
        s_wg = at(ZF + (Z_GQ + 4) * T, 4 * 512).rearrange("p (c n) -> p c n", c=4)
        s_sg = at(ZF + (Z_GQ + 8) * T, 4 * T).rearrange("p (c t) -> p c t", t=T)

        xres = at(ZF + KC * T, KC * T).rearrange("p (c t) -> p c t", t=T)
        sq2 = at(ZF, 2 * T).rearrange("p (b t) -> p b t", t=T)

        R0 = ZF
        p_qT = at(R0, 2 * T).rearrange("p (b t) -> p b t", t=T)
        p_keys = at(R0 + 2 * T, 2 * PH * NK).rearrange("p (c n) -> p c n", n=NK)
        p_sc = at(R0 + 2 * T + 2048, NT * 2 * PH * NK).rearrange("p (n c k) -> p n c k", n=NT, k=NK)
        R1 = R0 + 2 * T + 2048 + NT * 2048
        p_rep = at(R1 + 2048, NK * 2)
        p_sv = at(R1 + 2304, 2 * PH * TOPK).rearrange("p (h s k) -> p h s k", s=2, k=TOPK)
        p_siu = arena[:, R1 + 2560:R1 + 2560 + 256].bitcast(U32).rearrange("p (c k) -> p c k", k=TOPK)
        p_sif = at(R1 + 2816, 2 * PH * TOPK).rearrange("p (h s k) -> p h s k", s=2, k=TOPK)
        p_cand = at(R1 + 3072, 256)
        p_tv = at(R1 + 3328, PH * TOPK).rearrange("p (h k) -> p h k", k=TOPK)
        p_posu = arena[:, R1 + 3456:R1 + 3456 + 128].bitcast(U32)
        p_au = arena[:, R1 + 3584:R1 + 3584 + 128].bitcast(U32)
        p_ab = at(R1 + 3712, 2 * P).rearrange("p (s n) -> p s n", s=2)
        p_oh = at(R1 + 3968, 2048).rearrange("p (n k) -> p n k", k=TOPK)
        p_sel = at(R1 + 6016, 3 * P).rearrange("p (r n) -> p r n", r=3)
        p_sm = at(R1 + 6400, 2 * PH)
        R2 = R1 + 6416
        p_selT = at(R2, 3 * 640).rearrange("p (r t) -> p r t", r=3)
        assert R2 + 1920 <= AR
        o_j = [at(RING + s * 1024, 1024).rearrange("p (t n) -> p t n", n=P) for s in range(2)]
        o_i = [at(RING + 2048 + s * 1024, 1024).rearrange("p (t n) -> p t n", n=P) for s in range(2)]
        o_e = at(RING + 4096, 1024).rearrange("p (t n) -> p t n", n=P)
        stage = [at(R0 + s * 8192, 8192).rearrange("p (i t) -> p i t", t=TBLK) for s in range(2)]
        assert R0 + 2 * 8192 <= R2

        e = RING
        ut = [at(e + s * D, D).rearrange("p (c n) -> p c n", n=P) for s in range(GRP)]
        ev = [at(e + GRP * D + s * D, D) for s in range(GRP)]
        e += 2 * GRP * D
        coef = at(e, GRP * T).rearrange("p (b t) -> p b t", t=T)
        gates = at(e + GRP * T, GRP * T).rearrange("p (n b t) -> p n b t", b=GRP, t=TBLK)
        actv = at(e + 2 * GRP * T, 2 * T).rearrange("p (b t) -> p b t", t=T)
        acc = at(e + (2 * GRP + 2) * T, KC * T).rearrange("p (c t) -> p c t", t=T)
        xfin = at(RING, KC * T).rearrange("p (c t) -> p c t", t=T)
        sqf = coef

        PS = ctx.enter_context(nc.psum_tensor("PS", [P, 4096], F32))

        def bank(n, lo=0, cols=512, rows_=P, base=0):
            return PS[base:base + rows_, 512 * n + lo:512 * n + lo + cols]

        def flat(pair, cols=T):
            return PS[:, 1024 * pair:1024 * pair + cols]

        def split(pair):
            return PS[:, 1024 * pair:1024 * pair + 1024].rearrange("p (b t) -> p b t", b=2)[:, :, 0:HALF]

        def halves(ap):
            return ap.rearrange("p (b t) -> p b t", b=2)

        def seqs(ap):
            return ap.rearrange("p (b t) -> p b t", t=SLEN)

        gd = nc.dram_tensor("gate_scratch", (P, T // TBLK, NK, TBLK), F32, kind="Internal").ap()
        xd = nc.dram_tensor("x_scratch", (P, KC, T), F32, kind="Internal").ap()

        cond_in, x_in, small_in = sem("cond_in"), sem("x_in"), sem("small_in")
        ring_in = [sem(f"ring{s}_in") for s in range(2)]
        consts_made, masks_made = sem("consts_made"), sem("masks_made")
        silu_made = sem("silu_made")
        dve_step, act_step, pool_step = sem("dve_step"), sem("act_step"), sem("pool_step")
        sq_made, sq_used, ms_made, root_made = sem("sq_made"), sem("sq_used"), sem("ms_made"), sem("root_made")
        norm_made, mod_made, ada_made = sem("norm_made"), sem("mod_made"), sem("ada_made")
        prod_made, prod_out = sem("prod_made"), sem("prod_out")
        wsmall_clear, wsmall_in, small_made, small_out = (sem("wsmall_clear"), sem("wsmall_in"), sem("small_made"),
                                                          sem("small_out"))
        v_made, v_out = sem("v_made"), sem("v_out")
        gla_w_in, gla_state_in, gla_stored = sem("gla_w_in"), sem("gla_state_in"), sem("gla_stored")
        gla_lin, gla_ln, gla_dist, gla_exp, gla_kdec = (sem("gla_lin"), sem("gla_ln"), sem("gla_dist"),
                                                        sem("gla_exp"), sem("gla_kdec"))
        gla_tr, gla_ktok, gla_kv, gla_sm, gla_att, gla_attw = (sem("gla_tr"), sem("gla_ktok"), sem("gla_kv"),
                                                               sem("gla_sm"), sem("gla_att"), sem("gla_attw"))
        gla_oout, gla_kvs, gla_states = sem("gla_oout"), sem("gla_kvs"), sem("gla_states")
        ml_state_in = [sem(f"ml_state{k}_in") for k in range(2)]
        ml_stored = [sem(f"ml_state{k}_stored") for k in range(2)]
        m_stored = sem("m_stored")
        ml_ln, ml_pre, ml_rows, ml_cols, ml_colsout = (sem("ml_ln"), sem("ml_pre"), sem("ml_rows"), sem("ml_cols"),
                                                       sem("ml_colsout"))
        ml_bc, ml_kw, ml_floor, ml_spread = sem("ml_bc"), sem("ml_kw"), sem("ml_floor"), sem("ml_spread")
        ml_s, ml_kv, ml_arg, ml_exp, ml_sd, ml_o, ml_kvs, ml_head = (
            sem("ml_s"), sem("ml_kv"), sem("ml_arg"), sem("ml_exp"), sem("ml_sd"), sem("ml_o"), sem("ml_kvs"),
            sem("ml_head"))
        hn_gate, hn_sq, hn_sum, hn_ms, hn_root, hn_out = (sem("hn_gate"), sem("hn_sq"), sem("hn_sum"), sem("hn_ms"),
                                                          sem("hn_root"), sem("hn_out"))
        s5_clear, s5_in, s5_ang, s5_trig, s5_bbar, s5_bt, s5_ready = (
            sem("s5_clear"), sem("s5_in"), sem("s5_ang"), sem("s5_trig"), sem("s5_bbar"), sem("s5_bt"),
            sem("s5_ready"))
        s5_exp, s5_dt, s5_sum = sem("s5_exp"), sem("s5_dt"), sem("s5_sum")
        gla_oatt, s5_ldt = sem("gla_oatt"), sem("s5_ldt")
        s5_bu, s5_buout, s5_h, s5_y, s5_yout = (sem("s5_bu"), sem("s5_buout"), sem("s5_h"), sem("s5_y"),
                                                sem("s5_yout"))
        s5_gelu, s5_glu, s5_sig, s5_mix, s5_stored = (sem("s5_gelu"), sem("s5_glu"), sem("s5_sig"), sem("s5_mix"),
                                                      sem("s5_stored"))
        x_again, res_made, x_saved = sem("x_again"), sem("res_made"), sem("x_saved")
        keys_in, q_out, sc_made, sc_out, sc_clear = (sem("keys_in"), sem("q_out"), sem("sc_made"), sem("sc_out"),
                                                     sem("sc_clear"))
        soft_in, soft_out = sem("soft_in"), sem("soft_out")
        sel_made, sel_tr, sel_out = sem("sel_made"), sem("sel_tr"), sem("sel_out")
        oh_made, g_made, g_out, g_saved = sem("oh_made"), sem("g_made"), sem("g_out"), sem("g_saved")
        ut_in = [sem(f"ut{s}_in") for s in range(GRP)]
        ev_in, gates_in = sem("ev_in"), sem("gates_in")
        u_made, gelu_made, coef_made, vp_made, acc_made, acc_clear = (
            sem("u_made"), sem("gelu_made"), sem("coef_made"), sem("vp_made"), sem("acc_made"), sem("acc_clear"))
        x_back, fin_made, y_made, y_out = sem("x_back"), sem("fin_made"), sem("y_made"), sem("y_out")


        PARTS = {"ada0": ("w_ada", 0, 16, ada_made, 1, 0), "f": ("w_f", 0, 17, prod_made, 2, 0),
                 "v": ("w_v", 0, 6, v_made, NT, 0), "ada1": ("w_ada", 16, 16, ada_made, 1, 16),
                 "ada2": ("w_ada", 32, 16, ada_made, 1, 32), "out": ("w_out", 0, 8, prod_made, 2, 34),
                 "q": ("w_q", 0, 8, prod_made, 2, 50)}

        def fills(name):
            n = [0, 0]
            for k, part in PARTS.items():
                if k == name:
                    return n
                n = [n[0] + (part[2] + 1) // 2, n[1] + part[2] // 2]

        block = ctx.enter_context(nc.Block())

        @block.sync
        def _(sp):
            order = list(PARTS)

            def stream_part(name):
                src, first, tiles, done, per, before = PARTS[name]
                w = a[src]

                def load(s, tile_):
                    sp.dma_start(ring[s], w[tile_].rearrange("p (c n) -> p c n", c=KC)).then_inc(ring_in[s], 16)

                for s in range(2):
                    if order.index(name):
                        _, _, tiles0, done0, per0, before0 = PARTS[order[order.index(name) - 1]]
                        last = tiles0 - 1 - (tiles0 - 1 - s) % 2
                        sp.wait_ge(done0, before0 + per0 * (last + 1))
                    load(s, first + s)
                with sp.Fori(1, tiles // 2) as i:
                    for s in range(2):
                        sp.wait_ge(done, i * (2 * per) + (before + per * (s - 1)))
                        load(s, i * 2 + (first + s))
                if tiles % 2:
                    sp.wait_ge(done, before + per * (tiles - 2))
                    load(0, first + tiles - 1)

            sp.sem_inc(g_saved, 32)
            sp.dma_start(siluc[:, :], a["cT"]).then_inc(cond_in, 16)
            sp.dma_start(vec[:, :], a["vecs"]).then_inc(small_in, 16)
            sp.dma_start(gbias[:, :], a["gate_bias"]).then_inc(small_in, 16)
            sp.dma_start(m0[:, :], a["m0"]).then_inc(small_in, 16)
            sp.dma_start(xT, a["xT"]).then_inc(x_in, 16)
            stream_part("ada0")
            sp.wait_ge(wsmall_clear, 1)
            for lo, n, dst in ((0, 16, 0), (16, 6, 32), (22, 6, 64)):
                sp.dma_start(wsmall[:, :, dst:dst + n],
                             a["w_s"].rearrange("p (c n) -> p c n", c=KC)[:, :, lo:lo + n]).then_inc(wsmall_in, 16)
            stream_part("f")
            stream_part("v")
            stream_part("ada1")
            stream_part("ada2")

            sp.wait_ge(mod_made, 1)
            sp.dma_start(g_wgu, a["w_gate_up"]).then_inc(gla_w_in, 16)
            for p in range(3):
                if p:
                    sp.wait_ge(gla_stored, 32 * p)
                sp.dma_start(g_S0, a["state_gla"].rearrange("b (p q) v -> p q b v", q=P)[p]).then_inc(gla_state_in, 16)
                sp.wait_ge(gla_states, p + 1)
                sp.dma_start(o["gla_p"].rearrange("(p q) v -> p q v", q=P)[p], g_S[:, 0, :]).then_inc(gla_stored, 16)
                sp.dma_start(o["gla_s"].rearrange("b (p q) v -> p q b v", q=P)[p], g_S0).then_inc(gla_stored, 16)
            sp.wait_ge(gla_stored, 96)

            def store_ml(h):
                sp.wait_ge(ml_head, h + 1)
                cs = m_Cs[:, h % 2]
                sp.dma_start(o["c_p"][h], m_C[:, 3, 0:P]).then_inc(ml_stored[h % 2], 16)
                sp.dma_start(o["n_p"][:, h:h + 1], m_C[:, 3, P:P + 1], allow_slow_non_contiguous=True).then_inc(ml_stored[h % 2], 16)
                sp.dma_start(o["c_s"][:, h].rearrange("b k v -> k b v"), cs[:, :, 0:P]).then_inc(ml_stored[h % 2], 16)
                sp.dma_start(o["n_s"][h], cs[:, :, P], allow_slow_non_contiguous=True).then_inc(ml_stored[h % 2], 16)

            sp.wait_ge(gla_oout, 6)
            for h in range(HEADS):
                if h >= 2:
                    sp.wait_ge(ml_stored[h % 2], 64 * (h // 2))
                cs = m_Cs[:, h % 2]
                sp.dma_start(cs[:, :, 0:P], a["state_c"][:, h].rearrange("b k v -> k b v")).then_inc(ml_state_in[h % 2], 16)
                sp.dma_start(cs[:, :, P], a["state_n"][h], allow_slow_non_contiguous=True).then_inc(ml_state_in[h % 2], 16)
                if h >= 1:
                    store_ml(h - 1)
            store_ml(HEADS - 1)
            sp.dma_start(o["m_p"], m_small[0:HEADS, 27:28]).then_inc(m_stored, 16)
            sp.dma_start(o["m_s"], m_small[0:HEADS, 28:36]).then_inc(m_stored, 16)
            for k in range(2):
                sp.wait_ge(ml_stored[k], 64 * HEADS // 2)
            sp.wait_ge(m_stored, 32)

            sp.wait_ge(s5_clear, 1)
            for k in range(2):
                for g in range(2):
                    sp.dma_start(s_B[64 * g:64 * g + 64, k, :, 16 * g:16 * g + 16], a["s5_b"][k, g]).then_inc(s5_in, 16)
                    sp.dma_start(s_CT[64 * g:64 * g + 64, k, :, 16 * g:16 * g + 16], a["s5_c"][k, g]).then_inc(s5_in, 16)
            sp.dma_start(s_h0, a["s5_h0"]).then_inc(s5_in, 16)
            sp.dma_start(s_wg, a["w_glu"].rearrange("p (c n) -> p c n", c=4)).then_inc(s5_in, 16)
            sp.wait_ge(s5_h, 20)
            sp.dma_start(o["s5_s"], s_hn).then_inc(s5_stored, 16)
            sp.dma_start(o["s5_p"], s_hp).then_inc(s5_stored, 16)
            sp.wait_ge(s5_stored, 32)

            sp.wait_ge(s5_mix, 3)
            sp.dma_start(xres, a["xT"]).then_inc(x_again, 16)
            stream_part("out")
            sp.wait_ge(res_made, KC)
            sp.dma_start(xd, xres).then_inc(x_saved, 16)
            sp.wait_ge(x_saved, 16)
            sp.wait_ge(norm_made, 2)
            sp.dma_start(p_keys, a["keysT"].rearrange("p (c n) -> p c n", n=NK)).then_inc(keys_in, 16)
            stream_part("q")

            NB = T // TBLK
            with sp.Fori(0, NB // 2) as i:
                for s in range(2):
                    sp.wait_ge(g_out, i * 16 + 8 * (s + 1))
                    sp.dma_start(gd[:, i * 2 + s], stage[s]).then_inc(g_saved, 16)
            sp.wait_ge(g_out, 8 * NB)
            sp.dma_start(gd[:, NB - 1], stage[0]).then_inc(g_saved, 16)
            sp.wait_ge(g_saved, 16 * (2 + NB))

            def load_round(i, first):
                if not first:
                    sp.wait_ge(coef_made, i * GRP + 2)
                sp.dma_start(gates, gd[:, :, bass.ds(i * GRP, GRP), :]).then_inc(gates_in, 16)
                for b in range(GRP):
                    if not first:
                        sp.wait_ge(u_made, i * GRP + (b + 1 - GRP))
                    sp.dma_start(ut[b], a["peer_ut"][i * GRP + b].rearrange("p (c n) -> p c n", n=P)).then_inc(ut_in[b], 16)
                if not first:
                    sp.wait_ge(vp_made, i * KC + 1)
                for b in range(GRP):
                    sp.dma_start(ev[b], a["peer_v"][i * GRP + b]).then_inc(ev_in, 16)

            load_round(0, True)
            with sp.Fori(1, ROUNDS) as i:
                load_round(i, False)
            sp.wait_ge(vp_made, ROUNDS * KC + 1)
            sp.dma_start(xfin, xd).then_inc(x_back, 16)
            sp.wait_ge(y_made, 1)
            sp.dma_start(o["yT"], xfin).then_inc(y_out, 16)
            sp.wait_ge(y_out, 16)

        @block.gpsimd
        def _(pool):
            step = Chain(pool, pool_step)
            pool.memset(ones[:, :], 1.0).then_inc(consts_made, 1)
            step(pool.memset(ident[:, :], 0.0))
            pool.affine_select(out=ident[:, :], in_=ident[:, :], compare_op=ALU.not_equal, fill=1.0, base=0,
                               pattern=[[-1, P]], channel_multiplier=1).then_inc(consts_made, 1)
            pool.iota(iota[:, :], [[1, P]], base=0, channel_multiplier=0,
                      allow_small_or_imprecise_dtypes=True).then_inc(consts_made, 1)
            pool.memset(wsmall, 0.0).then_inc(wsmall_clear, 1)
            pool.wait_ge(consts_made, 3)
            pool.wait_ge(wsmall_clear, 1)
            step(pool.memset(vT[TS:P, 4], 0.0))

            def keep(ap, pattern, mult, fill=0.0, base=0):
                step(pool.affine_select(out=ap, in_=ap, compare_op=ALU.is_ge, fill=fill, base=base,
                                        pattern=pattern, channel_multiplier=mult))

            step(pool.memset(cap[:, :], 0.0))
            keep(cap[:, :], [[1, P]], -1, -BIG)
            step(pool.memset(scap[:, :], 0.0))
            keep(scap[:, :], [[1, TS]], -1, -BIG)
            keep(seqs(scap[:, :]), [[-SLEN, NSEQ], [0, SLEN]], 1, -BIG)
            gm, gs = gla_mask[:, :].bitcast(F32), gla_smask[:, :].bitcast(F32)
            step(pool.memset(gm, 1.0))
            keep(gm, [[1, P]], -1)
            keep(gm.rearrange("p (b t) -> p b t", t=GC), [[-GC, P // GC], [0, GC]], 1)
            step(pool.memset(gs, 1.0))
            keep(gs, [[1, TS]], -1)
            keep(seqs(gs), [[-SLEN, NSEQ], [0, SLEN]], 1)
            step(pool.memset(segm[:, :], 1.0))
            keep(segm[:, :], [[-SLEN, NSEQ]], 1)
            keep(segm[:, :], [[SLEN, NSEQ]], -1, 0.0, SLEN - 1)
            step(pool.memset(gla_reset[:, :], 1.0))
            step(pool.memset(ml_reset[:, :], 1.0))
            step(pool.memset(gla_reset[:, 0:TP:GC], 0.0))
            step(pool.memset(gla_reset[:, TP:T:SLEN], 0.0))
            step(pool.memset(ml_reset[:, 0:TP:P], 0.0))
            step(pool.memset(ml_reset[:, TP:T:SLEN], 0.0))
            step(pool.memset(sel[:, :], 1.0))
            s3 = sel[:, :].rearrange("p (h n) -> p h n", n=P)
            keep(s3, [[-1, HEADS], [0, P]], 1)
            keep(s3, [[1, HEADS], [0, P]], -1)
            pool.memset(attw[:, :], 0.0).then_inc(masks_made, 1)

            for h in range(HEADS):
                cs = m_Cs[:, h % 2]
                pool.wait_ge(ml_state_in[h % 2], 32 * (h // 2 + 1))
                if h:
                    pool.wait_ge(ml_o, h)
                    pool.wait_ge(ml_kvs, h)
                pool.tensor_copy(m_nbs, cs[:, :, P:P + 1].broadcast_to([P, NSEQ, P])).then_inc(ml_spread, 1)
                pool.wait_ge(ml_kw, h + 1)
                pool.tensor_tensor(m_kwm, m_kw[0:TS, 4:5, :].broadcast_to([TS, NSEQ, P]),
                                   segm[:, :].unsqueeze(2).broadcast_to([TS, NSEQ, P]), ALU.mult).then_inc(ml_spread, 1)

            pool.wait_ge(ml_head, HEADS)
            pool.wait_ge(hn_out, 12)
            for k in range(2):
                pool.wait_ge(ml_stored[k], 64 * HEADS // 2)
            pool.wait_ge(m_stored, 32)
            step(pool.memset(s_B[:, 0:2], 0.0))
            step(pool.memset(s_BT, 0.0))
            pool.memset(s_CT, 0.0).then_inc(s5_clear, 1)

            pool.wait_ge(norm_made, 2)
            pool.wait_ge(x_saved, 16)
            pool.wait_ge(s5_clear, 1)
            pool.memset(p_sc[64:P, 4], 0.0).then_inc(sc_clear, 1)
            pool.wait_ge(g_saved, 16 * (2 + T // TBLK))
            pool.wait_ge(sc_clear, 1)
            pool.memset(acc, 0.0).then_inc(acc_clear, 1)

        @block.scalar
        def _(act):
            step = Chain(act, act_step)

            def square_chunks(src, dst, n0):
                for c in range(KC):
                    if c >= 2:
                        act.wait_ge(sq_used, n0 * KC + c - 1)
                    act.activation(dst[:, c % 2], src[:, c], ACT.Square).then_inc(sq_made, 1)

            def root(n0):
                act.wait_ge(ms_made, n0 + 1)
                act.activation(rstd[:, :], rstd[:, :], ACT.Sqrt).then_inc(root_made, 1)

            for places, n in ((v_out, 2), (q_out, 2), (gelu_made, 2)):
                act.sem_inc(places, n)
            act.wait_ge(cond_in, 16)
            act.activation(siluc[:, :], siluc[:, :], ACT.Silu).then_inc(silu_made, 1)
            act.wait_ge(x_in, 16)
            square_chunks(xT, sq, 0)
            root(0)

            act.wait_ge(small_made, 1)
            act.wait_ge(small_in, 48)
            act.activation(rows[0:16, 0], PS[0:16, 3072:3072 + T], ACT.Copy).then_inc(small_out, 1)
            act.activation(rows[0:HEADS, 1], PS[32:32 + HEADS, 3072:3072 + T], ACT.Identity,
                           bias=gbias[:, 0:1]).then_inc(small_out, 1)
            act.activation(rows[0:HEADS, 2], PS[64:64 + HEADS, 3072:3072 + T], ACT.Identity,
                           bias=gbias[:, 1:2]).then_inc(small_out, 1)

            with act.Fori(0, 8) as i:
                for m in range(4):
                    act.wait_ge(prod_made, i * 4 + m + 1)
                    act.activation(halves(zF[:, bass.ds(i * 4 + m, 1), :].rearrange("p c t -> p (c t)")), split(m),
                                   ACT.Copy).then_inc(prod_out, 1)
            for m in range(2):
                act.wait_ge(prod_made, 32 + m + 1)
                act.activation(halves(zF[:, 32 + m]), split(m), ACT.Copy).then_inc(prod_out, 1)

            with act.Fori(0, 3) as i:
                for s in range(2):
                    for n in range(NT):
                        q = NT * s + n
                        act.wait_ge(v_made, i * 10 + q + 1)
                        nr = P if n < 4 else TS
                        act.activation(vT[0:nr, n, bass.ds((i * 2 + s) * WT, WT)], bank(2 * (q % 2), 0, WT, nr),
                                       ACT.Copy).then_inc(v_out, 1)

            for p in range(3):
                act.wait_ge(gla_lin, p + 1)
                ins = act.activation(g_la[:, p], flat(p), ACT.Identity, bias=vec[:, V_BG + p:V_BG + p + 1])
                step(ins)
            step(act.activation(g_e1, g_la, ACT.Abs))
            step(act.activation(g_e1, g_e1, ACT.Exp, scale=-1.0))
            act.activation(g_e2, g_e1, ACT.Ln, bias=1.0).then_inc(gla_ln, 1)
            act.wait_ge(gla_dist, 1)
            act.activation(g_e1, g_la, ACT.Exp, scale=1.0 / GTAU).then_inc(gla_exp, 1)
            act.activation(g_e2, g_la, ACT.Exp, scale=-1.0 / GTAU).then_inc(gla_exp, 1)
            act.activation(g_sc, g_sc, ACT.Exp, scale=1.0 / GTAU).then_inc(gla_exp, 1)
            for n in range(NT):
                nr = P if n < 4 else TS
                act.wait_ge(gla_tr, n + 1)
                act.activation(g_kd[0:nr, n, :], bank(n, 0, 384, nr), ACT.Copy).then_inc(gla_ktok, 1)
            for p in range(3):
                act.wait_ge(gla_oatt, NT * (p + 1))
                for hh, zc in ((0, Z_GQ), (1, Z_GK)):
                    step(act.activation(zF[:, zc + p, 0:TP], bank(2 + hh), ACT.Copy))
                    act.activation(zF[:, zc + p, TP:T], bank(6 + hh, 0, TS), ACT.Copy).then_inc(gla_oout, 1)

            act.wait_ge(gla_stored, 96)
            act.wait_ge(gla_oout, 6)
            act.wait_ge(small_out, 3)
            act.wait_ge(gla_kvs, 3)
            step(act.activation(m_rows[0:HEADS, 3], rows[0:HEADS, 2], ACT.Abs))
            step(act.activation(m_rows[0:HEADS, 3], m_rows[0:HEADS, 3], ACT.Exp, scale=-1.0))
            act.activation(m_rows[0:HEADS, 4], m_rows[0:HEADS, 3], ACT.Ln, bias=1.0).then_inc(ml_ln, 1)
            act.wait_ge(ml_pre, 1)
            act.activation(m_rows[0:HEADS, 3], m_rows[0:HEADS, 3], ACT.Exp).then_inc(ml_rows, 1)
            act.activation(m_rows[0:HEADS, 4], m_rows[0:HEADS, 1], ACT.Exp, scale=-1.0).then_inc(ml_rows, 1)
            act.activation(m_rows[0:HEADS, 6], m_rows[0:HEADS, 6], ACT.Exp).then_inc(ml_rows, 1)
            act.activation(m_small[0:HEADS, 48:60], m_small[0:HEADS, 48:60], ACT.Exp).then_inc(ml_rows, 1)
            for h in range(HEADS):
                act.wait_ge(ml_bc, h + 1)
                act.activation(m_E, flat(1), ACT.Copy).then_inc(ml_floor, 1)
                act.wait_ge(ml_arg, h + 1)
                act.activation(m_D[:, 0:TP], m_D[:, 0:TP], ACT.Exp).then_inc(ml_exp, 1)
                act.activation(m_D[0:TS, TP:T], m_D[0:TS, TP:T], ACT.Exp).then_inc(ml_exp, 1)

            act.activation(zF[:, Z_GG:Z_GG + 6], zF[:, Z_GG:Z_GG + 6], ACT.Silu).then_inc(hn_gate, 1)
            act.activation(zF[:, Z_MO:Z_MO + 6], zF[:, Z_MO:Z_MO + 6], ACT.Sigmoid).then_inc(hn_gate, 1)
            act.wait_ge(ml_head, HEADS)
            for k in range(2):
                act.wait_ge(ml_stored[k], 64 * HEADS // 2)
            act.wait_ge(m_stored, 32)
            for c in range(12 + 1):
                if c < 12:
                    if c >= 2:
                        act.wait_ge(hn_sum, c - 1)
                    act.activation(n_sq[:, c % 2], raw_head(c), ACT.Square).then_inc(hn_sq, 1)
                if c >= 1:
                    act.wait_ge(hn_ms, c)
                    act.activation(n_rs[:, (c - 1) % 2], n_rs[:, (c - 1) % 2], ACT.Sqrt).then_inc(hn_root, 1)

            act.wait_ge(hn_out, 12)
            act.activation(s_par[:, 0], vec[:, V_LDT:V_LDT + 16], ACT.Exp).then_inc(s5_ldt, 1)
            act.wait_ge(s5_dt, 1)
            act.activation(s_par[:, 3], s_par[:, 1], ACT.Exp).then_inc(s5_exp, 1)
            act.wait_ge(s5_ang, 1)
            act.activation(s_par[:, 4], s_par[:, 4], ACT.Sin).then_inc(s5_trig, 1)
            act.activation(s_par[:, 5], s_par[:, 5], ACT.Sin).then_inc(s5_trig, 1)
            for k in range(2):
                act.wait_ge(s5_bt, k + 1)
                for j in range(4):
                    ins = act.activation(s_BT[32 * j:32 * j + 32, k, j::4, :],
                                         bank(k, 0, 512, 32, 32 * j).rearrange("p (n c) -> p n c", c=P), ACT.Copy)
                ins.then_inc(s5_ready, 1)
            act.wait_ge(s5_yout, 20)
            act.activation(s_gl, s_gl, ACT.Gelu_apprx_tanh).then_inc(s5_gelu, 1)
            for m in range(4):
                act.wait_ge(s5_glu, m + 1)
                act.activation(s_sg[:, m], flat(m), ACT.Sigmoid, bias=vec[:, V_BGLU + m:V_BGLU + m + 1]).then_inc(s5_sig, 1)
            act.wait_ge(s5_mix, 1)
            act.activation(s_gl, s_sg, ACT.Square).then_inc(s5_sig, 1)
            act.wait_ge(s5_mix, 2)
            act.activation(rstd[:, :], rstd[:, :], ACT.Sqrt).then_inc(s5_sig, 1)

            act.wait_ge(res_made, KC)
            square_chunks(xres, sq2, 1)
            root(1)

            with act.Fori(0, 8) as i:
                for m in range(2):
                    act.wait_ge(prod_made, i * 2 + (34 + 16 + m + 1))
                    act.wait_ge(sc_made, i * 2 + m + 1)
                    act.activation(halves(p_qT[:, m]), split(m), ACT.Copy).then_inc(q_out, 1)
            for n in range(NT):
                act.wait_ge(soft_in, n + 1)
                act.activation(p_tv, p_tv, ACT.Exp).then_inc(soft_out, 1)
                act.wait_ge(sel_tr, n + 1)
                act.activation(p_selT[:, :, P * n:P * n + P], bank(0, 0, 384).rearrange("p (r t) -> p r t", r=3),
                               ACT.Copy).then_inc(sel_out, 1)

            def out_g(base, s, u):
                act.wait_ge(g_made, base + (u + 1))
                act.activation(stage[s][:, :, 8 * u:8 * u + 8].rearrange("p i t -> p t i"),
                               PS[:, 1024 * (u % 4):1024 * (u % 4) + 1024].rearrange("p (t i) -> p t i", i=P),
                               ACT.Copy).then_inc(g_out, 1)

            NB = T // TBLK
            with act.Fori(0, NB // 2) as i:
                for s in range(2):
                    act.wait_ge(g_saved, i * 32 + 32)
                    for u in range(8):
                        out_g(i * 16 + 8 * s, s, u)
            act.wait_ge(g_saved, 16 * (2 + NB - 1))
            for u in range(8):
                out_g(8 * (NB - 1), 0, u)

            with act.Fori(0, ROUNDS) as i:
                for b in range(GRP):
                    act.wait_ge(u_made, i * GRP + b + 1)
                    act.wait_ge(coef_made, i * GRP + b + 1)
                    act.activation(halves(actv[:, b % 2]), split(b % 2), ACT.Gelu_apprx_tanh).then_inc(gelu_made, 1)

            act.wait_ge(fin_made, 1)
            square_chunks(xfin, sqf, 2)
            root(2)

        @block.vector
        def _(dve):
            step = Chain(dve, dve_step)
            tt, ts, stt = dve.tensor_tensor, dve.tensor_scalar, dve.scalar_tensor_tensor
            mod = modT[:, :].rearrange("p (c n) -> p c n", n=NCOND)
            sc9 = scaleg[:, :].rearrange("p (c n) -> p c n", n=NCOND)

            def modulation(part):
                dve.wait_ge(ada_made, 16 * (part + 1))
                return tt(mod[:, 32 * part:32 * part + 32],
                          bank(4 + part, 0, 288).rearrange("p (c n) -> p c n", n=NCOND),
                          vec[:, V_BADA + 32 * part:V_BADA + 32 * part + 32].unsqueeze(2).broadcast_to([P, 32, NCOND]),
                          ALU.add)

            def inverse_root(n0, pair):
                dve.wait_ge(sq_used, KC * (n0 + 1))
                ts(rstd[:, :], flat(pair), 1.0 / D, EPS, ALU.mult, ALU.add).then_inc(ms_made, 1)
                dve.wait_ge(root_made, n0 + 1)
                step(dve.reciprocal(rstd[:, :], rstd[:, :]))

            def modulated(src, gain, shift, scale):
                step(stt(sc9, mod[:, scale:scale + KC], 1.0,
                         vec[:, gain:gain + KC].unsqueeze(2).broadcast_to([P, KC, NCOND]), ALU.add, ALU.mult))
                step(tt(hT, src, rstd[:, :].unsqueeze(1).broadcast_to([P, KC, T]), ALU.mult))
                for c in range(KC):
                    ins = ts(hT[:, c, 0:TP], hT[:, c, 0:TP], sc9[:, c, 0:1], mod[:, shift + c, 0:1], ALU.mult, ALU.add)
                step(ins)
                hs = hT[:, :, TP:T].rearrange("p c (b t) -> p c b t", t=SLEN)
                wide = [P, KC, NSEQ, SLEN]
                step(tt(hs, hs, sc9[:, :, 1:NCOND].unsqueeze(3).broadcast_to(wide), ALU.mult))
                return tt(hs, hs, mod[:, shift:shift + KC, 1:NCOND].unsqueeze(3).broadcast_to(wide), ALU.add)

            for places, n in ((prod_out, 4), (sc_out, 4), (coef_made, 2), (acc_made, 2)):
                dve.sem_inc(places, n)

            dve.wait_ge(x_in, 16)
            dve.wait_ge(small_in, 48)
            inverse_root(0, 3)
            ins = modulation(0)
            step(ins)
            modulated(xT, V_NG1, 0, 16).then_inc(norm_made, 1)

            step(modulation(1))
            modulation(2).then_inc(mod_made, 1)

            dve.wait_ge(gla_ln, 1)
            step(stt(g_la, g_la, 0.0, g_e2, ALU.min, ALU.subtract))
            dve.wait_ge(masks_made, 1)
            for p in range(3):
                step(dve.tensor_tensor_scan(g_B[:, p], gla_reset[:, :], g_la[:, p], 0.0, ALU.mult, ALU.add))
            for k, at_p, at_s in ((0, GMID, SMID), (1, GC - 1, SLEN - 1)):
                step(dve.tensor_copy(g_sc[:, k, :, 0:16], g_B[:, :, at_p:TP:GC]))
                step(dve.tensor_copy(g_sc[:, k, :, 16:24], g_B[:, :, TP + at_s:T:SLEN]))
            step(tt(g_sc[:, 2], g_sc[:, 1], g_sc[:, 0], ALU.subtract))

            def per_chunk(out, in_, k, op, p):
                ch = "p (n t) -> p n t"
                step(tt(out[:, p, 0:TP].rearrange(ch, t=GC), in_[:, p, 0:TP].rearrange(ch, t=GC),
                        g_sc[:, k, p, 0:16].unsqueeze(2).broadcast_to([P, 16, GC]), op))
                return tt(out[:, p, TP:T].rearrange(ch, t=SLEN), in_[:, p, TP:T].rearrange(ch, t=SLEN),
                          g_sc[:, k, p, 16:24].unsqueeze(2).broadcast_to([P, NSEQ, SLEN]), op)

            for p in range(3):
                ins = per_chunk(g_la, g_B, 0, ALU.subtract, p)
                if p < 2:
                    step(ins)
            ins.then_inc(gla_dist, 1)
            dve.wait_ge(gla_exp, 3)
            dve.wait_ge(prod_out, 34 + 4)
            gq, gk = zF[:, Z_GQ:Z_GQ + 3], zF[:, Z_GK:Z_GK + 3]
            step(stt(gq, gq, GDK ** -0.5, g_e1, ALU.mult, ALU.mult))
            step(tt(gk, gk, g_e2, ALU.mult))
            for p in range(3):
                ins = per_chunk(g_la, gk, 2, ALU.mult, p)
                if p < 2:
                    step(ins)
            ins.then_inc(gla_kdec, 1)

            for p in range(3):
                dve.wait_ge(gla_kv, p + 1)
                if p:
                    dve.wait_ge(gla_oatt, NT * p)
                    dve.wait_ge(gla_stored, 32 * p)

                def kv(c):
                    return bank(4 + c % 4, P * (c // 4), P)

                step(dve.tensor_copy(g_S[:, 1], kv(0)))
                for c in range(1, 16):
                    ts(g_Sm[:, c], g_S[:, c % 2], g_sc[:, 0, p, c:c + 1], None, ALU.mult)
                    step(stt(g_S[:, (c + 1) % 2], g_S[:, c % 2], g_sc[:, 1, p, c:c + 1], kv(c), ALU.mult, ALU.add))
                dve.wait_ge(gla_state_in, 16 * (p + 1))
                tt(g_S0m, g_S0, g_sc[:, 0, p, 16:24].unsqueeze(2).broadcast_to([P, NSEQ, P]), ALU.mult)
                dve.wait_ge(gla_ktok, NT)
                tt(g_kdm, g_kd[0:TS, 4:5, P * p:P * p + P].broadcast_to([TS, NSEQ, P]),
                   segm[:, :].unsqueeze(2).broadcast_to([TS, NSEQ, P]), ALU.mult).then_inc(gla_sm, 1)
                for n in range(NT):
                    dve.wait_ge(gla_att, NT * p + n + 1)
                    if 2 <= n < 4:
                        dve.wait_ge(gla_oatt, NT * p + n - 1)
                    for hh in range(2):
                        if n < 4:
                            ins = dve.copy_predicated(att_p[:, n % 2, hh], gla_mask[:, :], bank(4 * (n % 2) + hh, 0, P))
                        else:
                            ins = dve.copy_predicated(att_s[0:TS, hh], gla_smask[:, :], bank(hh, 0, TS, TS))
                    ins.then_inc(gla_attw, 1)
                dve.wait_ge(gla_kvs, p + 1)
                step(tt(g_S0, g_S0, g_sc[:, 1, p, 16:24].unsqueeze(2).broadcast_to([P, NSEQ, P]), ALU.mult))
                tt(g_S0, g_S0, PS[:, 2048:3072].rearrange("p (n c) -> p n c", c=P), ALU.add).then_inc(gla_states, 1)

            H6 = HEADS
            dve.wait_ge(ml_ln, 1)
            lf, li = rows[0:H6, 2], rows[0:H6, 1]
            mr = [m_rows[0:H6, k] for k in range(7)]
            step(stt(lf, lf, 0.0, mr[4], ALU.min, ALU.subtract))
            step(dve.tensor_tensor_scan(mr[0], ml_reset[0:H6, :], lf, 0.0, ALU.mult, ALU.add))
            step(dve.tensor_tensor_scan(mr[1][:, 0:TP], lf[:, 0:TP], li[:, 0:TP], 0.0, ALU.add, ALU.max))
            for b in range(NSEQ):
                lo = TP + SLEN * b
                step(dve.tensor_tensor_scan(mr[1][:, lo:lo + SLEN], lf[:, lo:lo + SLEN], li[:, lo:lo + SLEN],
                                            m0[:, b:b + 1], ALU.add, ALU.max))
            ms = m_small[0:H6]
            step(tt(mr[2], mr[0], mr[1], ALU.subtract))
            step(dve.memset(ms[:, 0:1], 0.0))
            step(dve.tensor_copy(ms[:, 1:4], mr[1][:, P - 1:TP - 1:P]))
            step(dve.tensor_copy(ms[:, 4:12], m0[:, :]))
            for k, lo in ((0, 12), (1, 24)):
                step(dve.tensor_copy(ms[:, lo:lo + 4], mr[k][:, P - 1:TP:P]))
                step(dve.tensor_copy(ms[:, lo + 4:lo + 12], mr[k][:, TP + SLEN - 1:T:SLEN]))
            step(tt(ms[:, 36:48], ms[:, 12:24], ms[:, 24:36], ALU.subtract))
            step(tt(ms[:, 48:60], ms[:, 36:48], ms[:, 0:12], ALU.add))
            step(tt(mr[5], li, mr[0], ALU.subtract))
            for dst, src, lo in ((mr[3], mr[2], 0), (mr[6], mr[5], 36)):
                step(tt(dst[:, 0:TP].rearrange("p (n t) -> p n t", t=P), src[:, 0:TP].rearrange("p (n t) -> p n t", t=P),
                        ms[:, lo:lo + 4].unsqueeze(2).broadcast_to([H6, 4, P]), ALU.add))
                step(tt(seqs(dst[:, TP:T]), seqs(src[:, TP:T]),
                        ms[:, lo + 4:lo + 12].unsqueeze(2).broadcast_to([H6, NSEQ, SLEN]), ALU.add))
            mq = zF[:, Z_MQ:Z_MQ + 6]
            ts(mq, mq, MDH ** -0.5, None, ALU.mult).then_inc(ml_pre, 1)
            dve.wait_ge(ml_cols, 1)
            cols = bank(0, 0, 60).rearrange("p (k n h) -> p k n h", k=2, h=H6)
            step(dve.tensor_copy(m_col[:, :, 0:4], cols[:, :, 0:4]))
            step(dve.tensor_copy(m_col[0:TS, :, 4], cols[0:TS, :, 4]))
            dve.tensor_copy(m_dec, bank(0, 64, 72).rearrange("p (h n) -> p h n", n=12)).then_inc(ml_colsout, 1)

            dve.wait_ge(ml_colsout, 1)
            for h in range(HEADS):
                cs = m_Cs[:, h % 2]
                dve.wait_ge(ml_bc, h + 1)
                if h:
                    dve.wait_ge(ml_kvs, h)
                    dve.wait_ge(ml_spread, 2 * h)
                step(tt(m_qw, zF[:, Z_MQ + h], flat(0), ALU.mult))
                for n in range(NT):
                    nr, src = (P, bank(6, P * n, P)) if n < 4 else (TS, bank(5, 384, P, TS))
                    ins = ts(m_kw[0:nr, n], src, m_col[0:nr, 1, n, h:h + 1], None, ALU.mult)
                ins.then_inc(ml_kw, 1)
                for n in range(NT):
                    nr, w, lo = (P, P, P * n) if n < 4 else (TS, TS, TP)
                    ins = stt(m_D[0:nr, lo:lo + w], PS[0:nr, 2048 + lo:2048 + lo + w], m_col[0:nr, 0, n, h:h + 1],
                              (cap if n < 4 else scap)[0:nr, 0:w], ALU.add, ALU.min)
                ins.then_inc(ml_arg, 1)
                dve.wait_ge(ml_kv, h + 1)
                if h:
                    dve.wait_ge(ml_stored[(h - 1) % 2], 64 * ((h - 1) // 2 + 1))
                step(dve.tensor_copy(m_C[:, 0], bank(7, 0, 129)))
                for n in range(1, 4):
                    src = bank(7, 129 * n, 129) if n < 3 else bank(1, P, 129)
                    step(stt(m_C[:, n], m_C[:, n - 1], m_dec[:, h, n:n + 1], src, ALU.mult, ALU.add))
                step(dve.tensor_copy(m_nb, m_C[:, 0:3, P:P + 1].broadcast_to([P, 3, P])))
                dve.wait_ge(ml_s, h + 1)
                dve.wait_ge(ml_exp, 2 * (h + 1))
                step(tt(m_D[:, 0:TP], m_D[:, 0:TP], bank(6), ALU.mult))
                tt(m_D[0:TS, TP:T], m_D[0:TS, TP:T], bank(7, 448, TS, TS), ALU.mult).then_inc(ml_sd, 1)
                dve.wait_ge(ml_o, h + 1)
                dve.wait_ge(ml_floor, h + 1)
                step(tt(m_E, flat(1), m_E, ALU.max))
                step(stt(m_E, flat(1), -1.0, m_E, ALU.mult, ALU.max))
                step(dve.reciprocal(m_E, m_E))
                step(tt(m_h[h], flat(0), m_E, ALU.mult))
                dve.wait_ge(ml_kvs, h + 1)
                dve.wait_ge(ml_spread, 2 * (h + 1))
                for b in range(NSEQ):
                    ins = stt(cs[:, b], cs[:, b], m_dec[:, h, 4 + b:5 + b], bank((4, 6, 7)[b // 3], 129 * (b % 3), 129),
                              ALU.mult, ALU.add)
                ins.then_inc(ml_head, 1)

            dve.wait_ge(hn_gate, 2)

            def head_out(c):
                dve.wait_ge(hn_root, c + 1)
                step(dve.reciprocal(n_rs[:, c % 2], n_rs[:, c % 2]))
                step(stt(n_rs[:, c % 2], raw_head(c), vec[:, V_GG + c:V_GG + c + 1], n_rs[:, c % 2], ALU.mult, ALU.mult))
                ins = tt(zF[:, c], n_rs[:, c % 2], zF[:, c], ALU.mult)
                ins.then_inc(hn_out, 1)
                dve.wait_ge(hn_out, c + 1)

            for c in range(12):
                dve.wait_ge(hn_sum, c + 1)
                ts(n_rs[:, c % 2], flat(c % 2), 1.0 / P, EPS, ALU.mult, ALU.add).then_inc(hn_ms, 1)
                if c:
                    head_out(c - 1)
            head_out(11)

            par = [s_par[:, k] for k in range(16)]
            lre, lim = vec[:, V_LRE:V_LRE + 16], vec[:, V_LIM:V_LIM + 16]
            dve.wait_ge(s5_ldt, 1)
            step(tt(par[2], lim, par[0], ALU.mult))
            tt(par[1], lre, par[0], ALU.mult).then_inc(s5_dt, 1)
            step(ts(par[11], par[2], 1.0 / (2 * np.pi), ROUNDER, ALU.mult, ALU.add))
            step(ts(par[11], par[11], ROUNDER, None, ALU.subtract))
            step(stt(par[12], par[11], -TWO_PI_HI, par[2], ALU.mult, ALU.add))
            step(stt(par[12], par[11], -TWO_PI_LO, par[12], ALU.mult, ALU.add))
            step(ts(par[4], par[12], 3.1415925, -3.1415925, ALU.min, ALU.max))
            step(ts(par[12], par[4], float(np.pi / 2), None, ALU.add))
            step(ts(par[11], par[12], float(np.pi), float(2 * np.pi), ALU.is_gt, ALU.mult))
            step(tt(par[12], par[12], par[11], ALU.subtract))
            ts(par[5], par[12], 3.1415925, -3.1415925, ALU.min, ALU.max).then_inc(s5_ang, 1)
            dve.wait_ge(s5_trig, 2)
            dve.wait_ge(s5_exp, 1)
            step(tt(par[6], par[3], par[5], ALU.mult))
            step(tt(par[7], par[3], par[4], ALU.mult))
            step(tt(par[8], lre, lre, ALU.mult))
            step(tt(par[11], lim, lim, ALU.mult))
            step(tt(par[8], par[8], par[11], ALU.add))
            step(dve.reciprocal(par[8], par[8]))
            step(ts(par[12], par[6], 1.0, None, ALU.subtract))
            step(tt(par[9], par[12], lre, ALU.mult))
            step(tt(par[11], par[7], lim, ALU.mult))
            step(tt(par[9], par[9], par[11], ALU.add))
            step(tt(par[9], par[9], par[8], ALU.mult))
            step(tt(par[10], par[7], lre, ALU.mult))
            step(tt(par[11], par[12], lim, ALU.mult))
            step(tt(par[10], par[10], par[11], ALU.subtract))
            step(tt(par[10], par[10], par[8], ALU.mult))
            dve.wait_ge(s5_in, 16 * 10)
            fr = par[9].unsqueeze(2).broadcast_to([P, S5C, 32])
            fi = par[10].unsqueeze(2).broadcast_to([P, S5C, 32])
            B = [s_B[:, k] for k in range(4)]
            step(tt(B[2], B[0], fr, ALU.mult))
            step(tt(B[3], B[1], fi, ALU.mult))
            step(tt(B[2], B[2], B[3], ALU.subtract))
            step(tt(B[3], B[1], fr, ALU.mult))
            step(tt(B[0], B[0], fi, ALU.mult))
            tt(B[3], B[3], B[0], ALU.add).then_inc(s5_bbar, 1)
            ts(s_CT[:, 1], s_CT[:, 1], -1.0, None, ALU.mult).then_inc(s5_bbar, 1)

            tc_, tsn = s_tab[:, 0], s_tab[:, 1]
            step(dve.tensor_copy(tc_[:, :, 0], par[5]))
            step(dve.tensor_copy(tsn[:, :, 0], par[4]))
            tmp = s_t[:, 0:2].rearrange("p k s t -> p (k s t)").rearrange("p (s t) -> p s t", s=S5C)
            n = 1
            while n < TC:
                cb = tc_[:, :, n - 1:n].broadcast_to([P, S5C, n])
                sb_ = tsn[:, :, n - 1:n].broadcast_to([P, S5C, n])
                step(tt(tc_[:, :, n:2 * n], tc_[:, :, 0:n], cb, ALU.mult))
                step(tt(tmp[:, :, 0:n], tsn[:, :, 0:n], sb_, ALU.mult))
                step(tt(tc_[:, :, n:2 * n], tc_[:, :, n:2 * n], tmp[:, :, 0:n], ALU.subtract))
                step(tt(tsn[:, :, n:2 * n], tc_[:, :, 0:n], sb_, ALU.mult))
                step(tt(tmp[:, :, 0:n], tsn[:, :, 0:n], cb, ALU.mult))
                step(tt(tsn[:, :, n:2 * n], tsn[:, :, n:2 * n], tmp[:, :, 0:n], ALU.add))
                n *= 2
            step(dve.memset(s_g0, 0.0))
            step(dve.memset(s_rhosm, 1.0))
            step(dve.memset(s_rhosm[:, 0:72:9], 0.0))

            def s5_y_out(i):
                c, q = divmod(i, 4)
                w, lo = (TC, TC * c) if c < 4 else (TS, TP)
                dve.wait_ge(s5_y, i + 1)
                stt(s_gl[:, q, lo:lo + w], zF[:, Z_SU + q, lo:lo + w], vec[:, V_SD + q:V_SD + q + 1],
                    bank(4 + q, TC * (c % 4), w), ALU.mult, ALU.add).then_inc(s5_yout, 1)

            for i in range(20):
                c, q = divmod(i, 4)
                sample = c == 4
                w = TS if sample else TC
                dve.wait_ge(s5_bu, i + 1)

                def four(ap):
                    return ap.rearrange("p j (b t) -> p j b t", t=SLEN) if sample else ap

                def table(k):
                    tb = s_tab[:, k, 4 * q:4 * q + 4, 0:(SLEN if sample else TC)]
                    return tb.unsqueeze(2).broadcast_to([P, 4, NSEQ, SLEN]) if sample else tb

                def scan_place(buf, k):
                    if not sample:
                        return buf[:, k, :, 0:TC]
                    return buf[:, k, :, 0:72].rearrange("p j (b t) -> p j b t", t=9)[:, :, :, 1:9]

                bu = [four(bank(2 * (i % 2) + k).rearrange("p (j x) -> p j x", j=4)[:, :, 0:w]) for k in range(2)]
                t4 = [four(s_t[:, k, :, 0:w]) for k in range(4)]
                cosn, sinn = table(0), table(1)
                tt(t4[0], bu[0], cosn, ALU.mult)
                tt(t4[1], bu[1], sinn, ALU.mult)
                tt(t4[2], bu[1], cosn, ALU.mult)
                ins = tt(t4[3], bu[0], sinn, ALU.mult)
                ins.then_inc(s5_buout, 1)
                dve.wait_ge(s5_buout, i + 1)
                step(tt(scan_place(s_in, 0), t4[0], t4[1], ALU.add))
                step(tt(scan_place(s_in, 1), t4[2], t4[3], ALU.subtract))
                if sample:
                    for k in range(2):
                        step(dve.tensor_copy(s_in[:, k, :, 0:72].rearrange("p j (b t) -> p j b t", t=9)[:, :, :, 0],
                                             s_h0[:, k, 4 * q:4 * q + 4, :]))
                for j in range(4):
                    s = 4 * q + j
                    if sample:
                        step(ts(s_rhos, s_rhosm, par[3][:, s:s + 1], None, ALU.mult))
                    for k in range(2):
                        n = 72 if sample else TC
                        ins = dve.tensor_tensor_scan(
                            s_g[:, k, j, 0:n], s_rhos if sample else par[3][:, s:s + 1].broadcast_to([P, TC]),
                            s_in[:, k, j, 0:n], 0.0 if sample else s_g0[:, k, s:s + 1], ALU.mult, ALU.add)
                        if sample:
                            step(ins)
                if not sample:
                    step(ins)
                g = [scan_place(s_g, k) for k in range(2)]
                hh = [four(s_h[:, k, :, 0:w]) for k in range(2)]
                if i:
                    dve.wait_ge(s5_y, i)
                step(tt(hh[0], g[0], cosn, ALU.mult))
                step(tt(t4[0], g[1], sinn, ALU.mult))
                step(tt(hh[0], hh[0], t4[0], ALU.subtract))
                step(tt(hh[1], g[0], sinn, ALU.mult))
                step(tt(t4[1], g[1], cosn, ALU.mult))
                step(tt(hh[1], hh[1], t4[1], ALU.add))
                if sample:
                    step(dve.tensor_copy(s_hn[:, 0, 4 * q:4 * q + 4, :], s_h[:, 0, :, SLEN - 1:TS:SLEN]))
                    dve.tensor_copy(s_hn[:, 1, 4 * q:4 * q + 4, :], s_h[:, 1, :, SLEN - 1:TS:SLEN]).then_inc(s5_h, 1)
                else:
                    if c == 3:
                        step(dve.tensor_copy(s_hp[:, :, 4 * q:4 * q + 4], s_h[:, :, :, TC - 1]))
                    dve.tensor_copy(s_g0[:, :, 4 * q:4 * q + 4], s_h[:, :, :, TC - 1]).then_inc(s5_h, 1)
                if i:
                    s5_y_out(i - 1)
            s5_y_out(19)

            dve.wait_ge(s5_gelu, 1)
            for m in range(4):
                dve.wait_ge(s5_sig, m + 1)
                ins = tt(s_sg[:, m], s_sg[:, m], s_gl[:, m], ALU.mult)
                if m < 3:
                    step(ins)
            ins.then_inc(s5_mix, 1)
            dve.wait_ge(s5_sum, 1)
            ts(rstd[:, :], flat(0), 1.0 / 512, EPS, ALU.mult, ALU.add).then_inc(s5_mix, 1)
            dve.wait_ge(s5_sig, 6)
            step(dve.reciprocal(rstd[:, :], rstd[:, :]))
            for m in range(4):
                ins = stt(zF[:, Z_SU + m], s_sg[:, m], vec[:, V_SG + m:V_SG + m + 1], rstd[:, :], ALU.mult, ALU.mult)
                if m < 3:
                    step(ins)
            ins.then_inc(s5_mix, 1)

            dve.wait_ge(x_again, 16)

            def residual(i, base, m, dst, chunk, gate_chunk):
                xc = dst[:, bass.ds(chunk, 1), :].rearrange("p c t -> p (c t)")
                gcol = modT[:, bass.ds((chunk + gate_chunk) * NCOND, NCOND)]
                dve.wait_ge(prod_made, chunk + (base + 1))
                step(tt(seqs(gate_tmp), seqs(flat(m)[:, TP:T]), gcol[:, 1:NCOND].unsqueeze(2).broadcast_to([P, NSEQ, SLEN]),
                        ALU.mult))
                stt(xc[:, 0:TP], flat(m)[:, 0:TP], gcol[:, 0:1], xc[:, 0:TP], ALU.mult, ALU.add).then_inc(prod_out, 1)
                tt(xc[:, TP:T], xc[:, TP:T], gate_tmp, ALU.add).then_inc(res_made, 1)
                dve.wait_ge(res_made, chunk + 1)

            with dve.Fori(0, 8) as i:
                step.enter(i, 2)
                for m in range(2):
                    residual(i, 34, m, xres, i * 2 + m, 32)
            step.leave(8)

            dve.wait_ge(prod_out, 50 + 4)
            inverse_root(1, 3)
            modulated(xres, V_NG2, 48, 64).then_inc(norm_made, 1)

            dve.wait_ge(sc_clear, 1)
            with dve.Fori(0, 8) as i:
                for m in range(2):
                    dve.wait_ge(sc_made, i * 2 + m + 3)
                    dve.tensor_copy(p_sc[:, 0:4, bass.ds(i * 2 + m, 1), :].rearrange("p n c k -> p n (c k)"),
                                    bank(4 + 2 * m).rearrange("p (n k) -> p n k", k=NK)).then_inc(sc_out, 1)
                    dve.tensor_copy(p_sc[0:TS, 4, bass.ds(i * 2 + m, 1), :].rearrange("p c k -> p (c k)"),
                                    bank(5 + 2 * m, 0, NK, TS)).then_inc(sc_out, 1)

            def best16(vals, idx, scores, work):
                step(dve.max(vals[:, 0:8], scores))
                dve.max_index(idx[:, 0:8], vals[:, 0:8], scores)
                step(dve.match_replace(work, vals[:, 0:8], scores, -3.0e38))
                step(dve.max(vals[:, 8:16], work))
                return dve.max_index(idx[:, 8:16], vals[:, 8:16], work)

            dve.wait_ge(sc_out, 4 * PH + 4)
            for n in range(NT):
                for c in range(2 * PH):
                    ins = best16(p_sv[:, c // 2, c % 2], p_siu[:, c], p_sc[:, n, c], p_rep[:, 0:NK])
                step(ins)
                step(dve.tensor_copy(p_sif.rearrange("p h s k -> p (h s k)"), p_siu.rearrange("p c k -> p (c k)")))
                c3 = p_cand.rearrange("p (a b) -> p a b", b=TOPK)
                for h in range(PH):
                    step(tt(c3, p_sv[:, h, 0].unsqueeze(2).broadcast_to([P, TOPK, TOPK]),
                            p_sv[:, h, 1].unsqueeze(1).broadcast_to([P, TOPK, TOPK]), ALU.add))
                    step(best16(p_tv[:, h], p_posu[:, TOPK * h:TOPK * h + TOPK], p_cand, p_rep))
                mx = p_sm[:, 0:PH]
                step(dve.tensor_copy(mx, p_tv[:, :, 0]))
                tt(p_tv, p_tv, mx.unsqueeze(2).broadcast_to([P, PH, TOPK]), ALU.subtract).then_inc(soft_in, 1)
                step(ts(p_au, p_posu, 4, None, ALU.logical_shift_right))
                step(dve.tensor_copy(p_ab[:, 0], p_au))
                step(ts(p_au, p_posu, 15, None, ALU.bitwise_and))
                step(dve.tensor_copy(p_ab[:, 1], p_au))
                for s in range(2):
                    step(tt(p_oh, p_ab[:, s].unsqueeze(2).broadcast_to([P, P, TOPK]),
                            iota[:, 0:TOPK].unsqueeze(1).broadcast_to([P, P, TOPK]), ALU.is_equal))
                    oh4 = p_oh.rearrange("p (h k) a -> p h k a", k=TOPK)
                    step(tt(oh4, oh4, p_sif[:, :, s].unsqueeze(2).broadcast_to([P, PH, TOPK, TOPK]), ALU.mult))
                    if s == 0 and n:
                        dve.wait_ge(sel_out, n)
                    step(dve.reduce_sum(p_sel[:, s], p_oh, AX.X))
                dve.wait_ge(soft_out, n + 1)
                sm = p_sm[:, PH:2 * PH]
                step(dve.reduce_sum(sm, p_tv, AX.X))
                step(dve.reciprocal(sm, sm))
                tt(p_sel[:, 2].rearrange("p (h k) -> p h k", k=TOPK), p_tv,
                   sm.unsqueeze(2).broadcast_to([P, PH, TOPK]), ALU.mult).then_inc(sel_made, 1)
                dve.wait_ge(sel_made, n + 1)

            dve.wait_ge(sel_out, NT)
            t8 = [P, 8, P]
            io = iota[:, :].unsqueeze(1).broadcast_to(t8)

            def one_hot(i, base, u, first):
                n = base + u
                if not first:
                    dve.wait_ge(g_made, n - 1)
                idx = [p_selT[:, r, bass.ds(n * 8, 8)].unsqueeze(2).broadcast_to(t8) for r in range(3)]
                step(tt(o_e, io, idx[0], ALU.is_equal))
                step(tt(o_i[u % 2], o_e, idx[2], ALU.mult))
                tt(o_j[u % 2], io, idx[1], ALU.is_equal).then_inc(oh_made, 1)

            for u in range(8):
                one_hot(None, 0, u, u < 2)
            with dve.Fori(1, T // TBLK) as i:
                step.enter(i - 1, 16)
                for u in range(8):
                    one_hot(i, i * 8, u, False)
            step.leave(T // TBLK - 1)

            dve.wait_ge(acc_clear, 1)
            with dve.Fori(0, ROUNDS) as i:
                dve.wait_ge(gates_in, i * 16 + 16)
                dve.wait_ge(vp_made, i * KC + 1)
                for b in range(GRP):
                    dve.wait_ge(gelu_made, i * GRP + b + 3)
                    tt(coef[:, b].rearrange("p (n t) -> p n t", t=TBLK), actv[:, b % 2].rearrange("p (n t) -> p n t", t=TBLK),
                       gates[:, :, b, :], ALU.mult).then_inc(coef_made, 1)
                for c in range(KC):
                    dve.wait_ge(vp_made, i * KC + c + 2)
                    tt(halves(acc[:, c]), halves(acc[:, c]), split(2 + c % 2), ALU.add).then_inc(acc_made, 1)

            dve.wait_ge(acc_made, ROUNDS * KC + 2)
            dve.wait_ge(x_back, 16)
            acs = acc[:, :, TP:T].rearrange("p c (b t) -> p c b t", t=SLEN)
            step(tt(acs, acs, mod[:, 80:96, 1:NCOND].unsqueeze(3).broadcast_to([P, KC, NSEQ, SLEN]), ALU.mult))
            for c in range(KC):
                step(stt(xfin[:, c, 0:TP], acc[:, c, 0:TP], mod[:, 80 + c, 0:1], xfin[:, c, 0:TP], ALU.mult, ALU.add))
            tt(xfin[:, :, TP:T], xfin[:, :, TP:T], acc[:, :, TP:T], ALU.add).then_inc(fin_made, 1)
            inverse_root(2, 3)
            for c in range(KC):
                ins = stt(xfin[:, c], xfin[:, c], vec[:, V_FG + c:V_FG + c + 1], rstd[:, :], ALU.mult, ALU.mult)
            ins.then_inc(y_made, 1)

        @block.tensor
        def _(pe):
            mm = pe.matmul

            def sum_squares(src, n0, pair):
                pe.wait_ge(consts_made, 3)
                for c in range(KC):
                    pe.wait_ge(sq_made, n0 * KC + c + 1)
                    for lo, w in ((0, TP), (TP, TS)):
                        ins = mm(flat(pair)[:, lo:lo + w], ones[:, :], src[:, c % 2, lo:lo + w],
                                 start=c == 0, stop=c == KC - 1)
                    ins.then_inc(sq_used, 1)

            sl = siluc[:, :].rearrange("p (c n) -> p c n", n=NCOND)

            def ada_part(part):
                base = fills(f"ada{part}")
                with pe.Fori(0, 8) as i:
                    for s in range(2):
                        pe.wait_ge(ring_in[s], i * 16 + 16 * (base[s] + 1))
                        for m in range(2):
                            out = PS[:, bass.ds(i * (4 * NCOND) + (512 * (4 + part) + (2 * s + m) * NCOND), NCOND)]
                            for c in range(KC):
                                ins = mm(out, ring[s][:, c, P * m:P * m + P], sl[:, c], start=c == 0, stop=c == KC - 1)
                        ins.then_inc(ada_made, 1)

            for places, n in ((sc_made, 2), (vp_made, 1)):
                pe.sem_inc(places, n)

            sum_squares(sq, 0, 3)
            pe.wait_ge(silu_made, 1)
            ada_part(0)

            pe.wait_ge(norm_made, 1)
            pe.wait_ge(wsmall_in, 48)
            for lo, w in ((0, TP), (TP, TS)):
                for c in range(KC):
                    ins = mm(PS[0:70, 3072 + lo:3072 + lo + w], wsmall[:, c, :], hT[:, c, lo:lo + w],
                             start=c == 0, stop=c == KC - 1)
            ins.then_inc(small_made, 1)

            def product(s, m, pair, whole):
                for x in range(2):
                    lo, w = ((0, TP), (TP, TS))[x] if whole else (HALF * x, HALF)
                    out = flat(pair)[:, lo:lo + w] if whole else split(pair)[:, x]
                    for c in range(KC):
                        ins = mm(out, ring[s][:, c, P * m:P * m + P], (mixT if whole else hT)[:, c, lo:lo + w], start=c == 0, stop=c == KC - 1)
                return ins

            base = fills("f")
            pe.wait_ge(small_out, 3)
            with pe.Fori(0, 8) as i:
                for s in range(2):
                    pe.wait_ge(ring_in[s], i * 16 + 16 * (base[s] + 1))
                    for m in range(2):
                        pe.wait_ge(prod_out, i * 4 + (2 * s + m + 1))
                        ins = product(s, m, 2 * s + m, False)
                        ins.then_inc(prod_made, 1)
            pe.wait_ge(ring_in[0], 16 * (base[0] + 9))
            for m in range(2):
                pe.wait_ge(prod_out, 32 + m + 1)
                product(0, m, m, False).then_inc(prod_made, 1)

            base = fills("v")
            pe.wait_ge(prod_out, 34 + 4)
            with pe.Fori(0, 3) as i:
                for s in range(2):
                    pe.wait_ge(ring_in[s], i * 16 + 16 * (base[s] + 1))
                    for n in range(NT):
                        q = NT * s + n
                        nr = P if n < 4 else TS
                        pe.wait_ge(v_out, i * 10 + q + 1)
                        for c in range(KC):
                            ins = mm(bank(2 * (q % 2), 0, WT, nr), hT[:, c, P * n:P * n + nr], ring[s][:, c, :],
                                     start=c == 0, stop=c == KC - 1)
                        ins.then_inc(v_made, 1)
            ada_part(1)
            ada_part(2)

            pe.wait_ge(gla_w_in, 16)
            pe.wait_ge(v_out, 30 + 2)
            pe.wait_ge(masks_made, 1)
            for p in range(3):
                for lo, w in ((0, TP), (TP, TS)):
                    ins = mm(flat(p)[:, lo:lo + w], g_wgu[:, P * p:P * p + P], rows[0:16, 0, lo:lo + w],
                             start=True, stop=True)
                ins.then_inc(gla_lin, 1)
            pe.wait_ge(gla_kdec, 1)
            for n in range(NT):
                nr = P if n < 4 else TS
                for p in range(3):
                    ins = pe.transpose(bank(n, P * p, P, nr), g_la[:, p, P * n:P * n + nr], ident[:, :])
                ins.then_inc(gla_tr, 1)
            pe.wait_ge(gla_ktok, NT)
            for p in range(3):
                if p:
                    pe.wait_ge(gla_states, p)
                    pe.wait_ge(gla_oout, 2 * p)
                for c in range(16):
                    r = GC * (c % 4)
                    for hh in range(2):
                        ins = mm(bank(4 + c % 4, P * (c // 4), P, GDK, GDK * hh),
                                 g_kd[r:r + GC, c // 4, P * p + GDK * hh:P * p + GDK * hh + GDK],
                                 vT[r:r + GC, c // 4, P * (2 * p + hh):P * (2 * p + hh) + P], start=True, stop=True)
                ins.then_inc(gla_kv, 1)
                gq, gk = zF[:, Z_GQ + p], zF[:, Z_GK + p]

                def scores(n):
                    if n >= 2:
                        pe.wait_ge(gla_attw, NT * p + n - 1)
                    w = P if n < 4 else TS
                    for hh in range(2):
                        r = slice(GDK * hh, GDK * hh + GDK)
                        lo = P * n
                        ins = mm(bank(4 * (n % 2) + hh, 0, w, w), gk[r, lo:lo + w], gq[r, lo:lo + w], start=True, stop=True)
                    ins.then_inc(gla_att, 1)

                def outputs(n):
                    pe.wait_ge(gla_attw, NT * p + n + 1)
                    for hh in range(2):
                        r = slice(GDK * hh, GDK * hh + GDK)
                        v = slice(P * (2 * p + hh), P * (2 * p + hh) + P)
                        if n < 4:
                            out = bank(2 + hh, P * n, P)
                            ins = mm(out, vT[:, n, v], att_p[:, n % 2, hh], start=True, stop=True)
                            for k in range(4):
                                c = 4 * n + k
                                if c:
                                    ins = mm(out[:, GC * k:GC * k + GC], g_Sm[r, c], gq[r, GC * c:GC * c + GC],
                                             start=False, stop=True, skip_group_check=True)
                        else:
                            out = bank(6 + hh, 0, TS)
                            ins = mm(out, vT[:, n, v], att_s[:, hh], start=True, stop=True)
                            for b in range(NSEQ):
                                ins = mm(out[:, SLEN * b:SLEN * b + SLEN], g_S0m[r, b],
                                         gq[r, TP + SLEN * b:TP + SLEN * b + SLEN], start=False, stop=True,
                                         skip_group_check=True)
                    ins.then_inc(gla_oatt, 1)

                scores(0)
                pe.wait_ge(gla_sm, p + 1)
                scores(1)
                outputs(0)
                scores(2)
                outputs(1)
                scores(3)
                outputs(2)
                scores(4)
                outputs(3)
                outputs(4)
                for b in range(NSEQ):
                    for hh in range(2):
                        ins = mm(PS[GDK * hh:GDK * hh + GDK, 2048 + P * b:2048 + P * b + P],
                                 g_kdm[:, b, GDK * hh:GDK * hh + GDK], vT[0:TS, 4, P * (2 * p + hh):P * (2 * p + hh) + P],
                                 start=True, stop=True)
                ins.then_inc(gla_kvs, 1)

            pe.wait_ge(ml_rows, 4)
            pe.wait_ge(gla_oout, 6)
            for k, r in ((0, 5), (1, 6)):
                for n in range(NT):
                    nr = P if n < 4 else TS
                    pe.transpose(bank(0, (k * NT + n) * HEADS, HEADS, nr), m_rows[0:HEADS, r, P * n:P * n + nr],
                                 ident[0:HEADS, 0:HEADS])
            for h in range(HEADS):
                ins = mm(bank(0, 64 + 12 * h, 12), sel[0:HEADS, P * h:P * h + P], m_small[0:HEADS, 48:60],
                         start=True, stop=True)
            ins.then_inc(ml_cols, 1)
            pe.wait_ge(ml_colsout, 1)
            pe.wait_ge(gla_states, 3)
            for h in range(HEADS):
                if h:
                    pe.wait_ge(ml_head, h)
                q_, k_ = zF[:, Z_MQ + h], zF[:, Z_MK + h]
                v = slice(768 + P * h, 768 + P * h + P)
                for pair, r in ((0, 3), (1, 4), (2, 2)):
                    for lo, w in ((0, TP), (TP, TS)):
                        mm(flat(pair)[:, lo:lo + w], sel[0:HEADS, P * h:P * h + P], m_rows[0:HEADS, r, lo:lo + w],
                           start=True, stop=True)
                for n in range(4):
                    pe.transpose(bank(6, P * n, P), k_[:, P * n:P * n + P], ident[:, :])
                pe.transpose(bank(5, 384, P, TS), k_[:, TP:T], ident[:, :]).then_inc(ml_bc, 1)
                pe.wait_ge(ml_kw, h + 1)
                for n in range(4):
                    mm(bank(6, P * n, P), k_[:, P * n:P * n + P], q_[:, P * n:P * n + P], start=True, stop=True)
                mm(bank(7, 448, TS, TS), k_[:, TP:T], q_[:, TP:T], start=True, stop=True).then_inc(ml_s, 1)
                for n in range(4):
                    b_, lo = (7, 129 * n) if n < 3 else (1, P)
                    mm(bank(b_, lo, P), m_kw[:, n], vT[:, n, v], start=True, stop=True)
                    ins = mm(bank(b_, lo + P, 1), m_kw[:, n], ones[:, 0:1], start=True, stop=True)
                ins.then_inc(ml_kv, 1)
                pe.wait_ge(ml_sd, h + 1)
                pe.wait_ge(ml_floor, h + 1)
                pe.wait_ge(ml_spread, 2 * h + 2)
                for n in range(4):
                    lo = P * n
                    for pair, vv, st in ((0, vT[:, n, v], lambda n: m_C[:, n, 0:P]), (1, ones[:, :], lambda n: m_nb[:, n])):
                        out = flat(pair)[:, lo:lo + P]
                        mm(out, vv, m_D[:, lo:lo + P], start=True, stop=n == 0)
                        if n:
                            mm(out, st(n - 1), m_qw[:, lo:lo + P], start=False, stop=True)
                for pair, vv, st in ((0, vT[0:TS, 4, v], lambda b: m_Cs[:, h % 2, b, 0:P]),
                                     (1, ones[0:TS, :], lambda b: m_nbs[:, b])):
                    out = flat(pair)[:, TP:T]
                    mm(out, vv, m_D[0:TS, TP:T], start=True, stop=True)
                    for b in range(NSEQ):
                        ins = mm(out[:, SLEN * b:SLEN * b + SLEN], st(b), m_qw[:, TP + SLEN * b:TP + SLEN * b + SLEN],
                                 start=False, stop=True, skip_group_check=True)
                ins.then_inc(ml_o, 1)
                for b in range(NSEQ):
                    b_, lo = (4, 6, 7)[b // 3], 129 * (b % 3)
                    mm(bank(b_, lo, P), m_kwm[:, b], vT[0:TS, 4, v], start=True, stop=True)
                    ins = mm(bank(b_, lo + P, 1), m_kwm[:, b], ones[0:TS, 0:1], start=True, stop=True)
                ins.then_inc(ml_kvs, 1)

            pe.wait_ge(ml_head, HEADS)
            for c in range(12):
                pe.wait_ge(hn_sq, c + 1)
                if c >= 2:
                    pe.wait_ge(hn_ms, c - 1)
                for lo, w in ((0, TP), (TP, TS)):
                    ins = mm(flat(c % 2)[:, lo:lo + w], ones[:, :], n_sq[:, c % 2, lo:lo + w], start=True, stop=True)
                ins.then_inc(hn_sum, 1)

            pe.wait_ge(hn_ms, 12)
            pe.wait_ge(s5_bbar, 1)
            for k in range(2):
                for n in range(4):
                    ins = pe.transpose(bank(k, P * n, P), s_B[:, 2 + k, 4 * n:4 * n + 4, :].rearrange("p s c -> p (s c)"),
                                       ident[:, :])
                ins.then_inc(s5_bt, 1)
            pe.wait_ge(s5_ready, 2)
            pe.wait_ge(s5_bbar, 2)

            def s5_inputs(i):
                c, q = divmod(i, 4)
                w, lo = (TC, TC * c) if c < 4 else (TS, TP)
                if i >= 2:
                    pe.wait_ge(s5_buout, i - 1)
                for k in range(2):
                    for j in range(4):
                        ins = mm(bank(2 * (i % 2) + k, P * j, w), s_BT[:, k, 4 * q + j], zF[:, Z_SU + q, lo:lo + w],
                                 start=True, stop=True)
                ins.then_inc(s5_bu, 1)

            s5_inputs(0)
            for i in range(20):
                if i < 19:
                    s5_inputs(i + 1)
                c, q = divmod(i, 4)
                w = TC if c < 4 else TS
                pe.wait_ge(s5_h, i + 1)
                if c == 4:
                    pe.wait_ge(s5_yout, i - 15)
                for j in range(4):
                    for k in range(2):
                        ins = mm(bank(4 + q, TC * (c % 4), w, 32, 32 * j), s_CT[:, k, 4 * q + j, :], s_h[:, k, j, 0:w],
                                 start=k == 0, stop=k == 1)
                ins.then_inc(s5_y, 1)
            pe.wait_ge(s5_gelu, 1)
            for m in range(4):
                for lo, w in ((0, TP), (TP, TS)):
                    for c in range(4):
                        ins = mm(flat(m)[:, lo:lo + w], s_wg[:, c, P * m:P * m + P], s_gl[:, c, lo:lo + w],
                                 start=c == 0, stop=c == 3)
                ins.then_inc(s5_glu, 1)
            pe.wait_ge(s5_sig, 5)
            for lo, w in ((0, TP), (TP, TS)):
                for c in range(4):
                    ins = mm(flat(0)[:, lo:lo + w], ones[:, :], s_gl[:, c, lo:lo + w], start=c == 0, stop=c == 3)
            ins.then_inc(s5_sum, 1)

            pe.wait_ge(s5_mix, 3)
            pe.wait_ge(hn_out, 12)
            base = fills("out")
            with pe.Fori(0, 4) as i:
                for s in range(2):
                    pe.wait_ge(ring_in[s], i * 16 + 16 * (base[s] + 1))
                    for m in range(2):
                        pe.wait_ge(prod_out, i * 4 + (34 + 2 * s + m - 1 + 4))
                        product(s, m, m, True).then_inc(prod_made, 1)

            sum_squares(sq2, 1, 3)

            pe.wait_ge(norm_made, 2)
            pe.wait_ge(keys_in, 16)
            base = fills("q")
            with pe.Fori(0, 4) as i:
                for s in range(2):
                    pe.wait_ge(ring_in[s], i * 16 + 16 * (base[s] + 1))
                    for m in range(2):
                        pe.wait_ge(prod_out, 50 + 4)
                        pe.wait_ge(q_out, i * 4 + (2 * s + m + 1))
                        product(s, m, m, False).then_inc(prod_made, 1)
                    for m in range(2):
                        pe.wait_ge(q_out, i * 4 + (2 * s + m + 3))
                        pe.wait_ge(sc_out, i * 8 + 2 * (2 * s + m + 1))
                        for n in range(NT):
                            nr = P if n < 4 else TS
                            dst = bank(4 + 2 * m, P * n, NK) if n < 4 else bank(5 + 2 * m, 0, NK, TS)
                            ins = mm(dst, p_qT[:, m, P * n:P * n + nr],
                                     p_keys[:, bass.ds(i * 4 + (2 * s + m), 1), :].rearrange("p c k -> p (c k)"),
                                     start=True, stop=True)
                        ins.then_inc(sc_made, 1)

            for n in range(NT):
                pe.wait_ge(sel_made, n + 1)
                if n:
                    pe.wait_ge(sel_out, n)
                for r in range(3):
                    ins = pe.transpose(bank(0, P * r, P), p_sel[:, r], ident[:, :])
                ins.then_inc(sel_tr, 1)

            pe.wait_ge(sel_out, NT)

            def gate_products(n, u):
                pe.wait_ge(oh_made, n + 1)
                if not isinstance(n, int) or n >= 4:
                    pe.wait_ge(g_out, n - 3)
                for t in range(8):
                    ins = mm(PS[:, 1024 * (u % 4) + P * t:1024 * (u % 4) + P * t + P], o_j[u % 2][:, t], o_i[u % 2][:, t],
                             start=True, stop=True)
                ins.then_inc(g_made, 1)

            for u in range(8):
                gate_products(u, u)
            with pe.Fori(1, T // TBLK) as i:
                for u in range(8):
                    gate_products(i * 8 + u, u)

            pe.wait_ge(g_out, T // 8)
            with pe.Fori(0, ROUNDS) as i:
                for b in range(GRP):
                    pe.wait_ge(ut_in[b], i * 16 + 16)
                    pe.wait_ge(gelu_made, i * GRP + b + 1)
                    for x in range(2):
                        for c in range(KC):
                            ins = mm(split(b % 2)[:, x], ut[b][:, c], hT[:, c, HALF * x:HALF * x + HALF],
                                     start=c == 0, stop=c == KC - 1)
                    ins.then_inc(u_made, 1)
                pe.wait_ge(ev_in, i * (16 * GRP) + 16 * GRP)
                for c in range(KC):
                    pe.wait_ge(acc_made, i * KC + c + 1)
                    for x in range(2):
                        for b in range(GRP):
                            if c == 0 and x == 0:
                                pe.wait_ge(coef_made, i * GRP + b + 3)
                            ins = mm(split(2 + c % 2)[:, x], ev[b][:, P * c:P * c + P],
                                     coef[:, b, HALF * x:HALF * x + HALF], start=b == 0, stop=b == GRP - 1)
                    ins.then_inc(vp_made, 1)

            sum_squares(sqf, 2, 3)



def kernel(**inputs):
    from concourse import bacc
    from concourse.bass_utils import run_bass_kernel_spmd

    g = {k: np.ascontiguousarray(v) for k, v in inputs.items()}
    g = {k: v[0] if k not in ("x_prompt", "x_sample", "c_prompt", "c_sample", "final_gain") else v for k, v in g.items()}

    def chunks(w, rows_last=False):
        return w.reshape(-1, P, *w.shape[1:]).swapaxes(0, 1)

    def tiles(w):
        return w.reshape(KC, P, -1, WT).transpose(2, 1, 0, 3).reshape(-1, P, KC * WT)

    def vecs(*vs):
        return np.concatenate([chunks(v.reshape(-1)) for v in vs], axis=1)

    w_in = g["w_in"]
    c = np.concatenate([g["c_prompt"], g["c_sample"]])
    x = np.concatenate([g["x_prompt"].reshape(TP, D), g["x_sample"].reshape(TS, D)])
    ins = {
        "cT": chunks(c.T).reshape(P, -1),
        "xT": chunks(x.T),
        "vecs": vecs(g["norm_gain"][0], g["norm_gain"][1], g["final_gain"], g["b_ada"], g["gla_norm_gain"],
                     g["ml_norm_gain"], g["s5_norm_gain"], g["s5_b_glu"], g["s5_d"], g["gla_b_gate"],
                     g["s5_lambda_re"], g["s5_lambda_im"], np.repeat(g["s5_log_dt"], S5P)),
        "gate_bias": np.stack([g["ml_b_igate"], g["ml_b_fgate"]], axis=1),
        "m0": g["state_mlstm_m"].T,
        "w_ada": tiles(g["w_ada"]),
        "w_f": tiles(np.concatenate([w_in[:, lo:hi] for lo, hi in (
            (1536, 2304), (4624, 5392), (5404, 5916), (0, 384), (384, 768), (2320, 3088), (3088, 3856))], axis=1)),
        "w_v": tiles(np.concatenate([w_in[:, 768:1536], w_in[:, 3856:4624]], axis=1)),
        "w_s": chunks(np.concatenate([w_in[:, 2304:2320], w_in[:, 5392:5404]], axis=1)).reshape(P, -1),
        "w_gate_up": g["gla_w_gate_up"],
        "state_gla": g["state_gla"].reshape(NSEQ, HEADS * GDK, MDH),
        "state_c": g["state_mlstm_c"],
        "state_n": g["state_mlstm_n"].transpose(1, 2, 0),
        "s5_b": np.stack([g[k].reshape(S5C, 2, S5P, S5CH).transpose(1, 2, 0, 3) for k in ("s5_b_re", "s5_b_im")]),
        "s5_c": np.stack([g[k].reshape(S5C, 2, S5CH, S5P).transpose(1, 3, 0, 2) for k in ("s5_c_re", "s5_c_im")]),
        "s5_h0": np.stack([g[k].reshape(NSEQ, S5C, P).transpose(2, 1, 0) for k in ("state_s5_re", "state_s5_im")], axis=1),
        "w_glu": chunks(g["s5_w_glu"]).reshape(P, -1),
        "w_out": tiles(g["w_out"]),
        "w_q": tiles(g["peer_w_q"]),
        "keysT": g["peer_sub_keys"].transpose(3, 0, 1, 2).reshape(P, -1),
        "peer_ut": g["peer_u"].reshape(NK, NK, KC, P).transpose(0, 3, 2, 1).reshape(NK, P, D),
        "peer_v": g["peer_v"].reshape(NK, P, D),
    }
    outs = {
        "yT": (P, KC, T), "gla_p": (HEADS * GDK, MDH), "gla_s": (NSEQ, HEADS * GDK, MDH),
        "c_p": (HEADS, P, P), "n_p": (P, HEADS), "c_s": (NSEQ, HEADS, P, P), "n_s": (HEADS, P, NSEQ),
        "m_p": (HEADS, 1), "m_s": (HEADS, NSEQ), "s5_s": (P, 2, S5C, NSEQ), "s5_p": (P, 2, S5C),
    }
    nc = bacc.Bacc("TRN2", target_bir_lowering=False, num_devices=1)
    arrays = {f"in_{k}": np.ascontiguousarray(v) for k, v in ins.items()}
    a = {k: nc.dram_tensor(f"in_{k}", arrays[f"in_{k}"].shape, F32, kind="ExternalInput").ap() for k in ins}
    o = {k: nc.dram_tensor(f"out_{k}", s, F32, kind="ExternalOutput").ap() for k, s in outs.items()}
    build(nc, a, o)
    r = run_bass_kernel_spmd(nc, [arrays], core_ids=[0]).results[0]
    r = {k: np.asarray(r[f"out_{k}"]) for k in outs}

    y = r["yT"].transpose(2, 1, 0).reshape(T, D)
    s5_s = r["s5_s"].transpose(1, 3, 2, 0).reshape(2, 1, NSEQ, 2 * S5C, S5P)
    s5_p = r["s5_p"].transpose(1, 2, 0).reshape(2, 1, 1, 2 * S5C, S5P)
    return (y[:TP].reshape(1, TP, D), y[TP:].reshape(NSEQ, SLEN, D),
            r["gla_p"].reshape(1, 1, HEADS, GDK, MDH), r["gla_s"].reshape(1, NSEQ, HEADS, GDK, MDH),
            r["c_p"].reshape(1, 1, HEADS, P, P), r["c_s"].reshape(1, NSEQ, HEADS, P, P),
            r["n_p"].T.reshape(1, 1, HEADS, P), r["n_s"].transpose(2, 0, 1).reshape(1, NSEQ, HEADS, P),
            r["m_p"].reshape(1, 1, HEADS), r["m_s"].T.reshape(1, NSEQ, HEADS),
            s5_p[0], s5_s[0], s5_p[1], s5_s[1])
```

```python
from contextlib import ExitStack

import numpy as np

import concourse.bass as bass
from concourse import mybir

ALU = mybir.AluOpType
ACT = mybir.ActivationFunctionType
AX = mybir.AxisListType
F32 = mybir.dt.float32
F32R = mybir.dt.float32r
U32 = mybir.dt.uint32
I32 = mybir.dt.int32

P = 128
D = 2048
KC = D // P
NSEQ, SLEN = 8, 8
TP, TS = 512, NSEQ * SLEN
T = TP + TS
HALF = T // 2
NT = 5
EPS = 1e-6
HEADS = 6
GDK, MDH = 64, 128
GC, GMID = 32, 15
SMID = 3
GTAU = 16.0
S5C, S5CH, S5P = 16, 16, 64
PH, NK, TOPK = 8, 128, 16
GRP = 2
ROUNDS = NK // GRP
TBLK = 32
WT = 256
NCOND = 1 + NSEQ

Z_GG, Z_MO, Z_SU, Z_GQ, Z_GK, Z_MQ, Z_MK, Z_N = 0, 6, 12, 16, 19, 22, 28, 34
V_NG1, V_NG2, V_FG, V_BADA, V_GG, V_MG, V_SG, V_BGLU, V_SD, V_BG, V_LRE, V_LIM, V_LDT, V_N = (
    0, 16, 32, 48, 144, 150, 156, 160, 164, 168, 171, 187, 203, 219)

BIG = 1.0e30
TWO_PI_HI = 6.28125
TWO_PI_LO = float(2 * np.pi - 6.28125)
ROUNDER = 12582912.0


class Chain:

    def __init__(self, eng, sem):
        self.eng, self.sem, self.n, self.loop = eng, sem, 0, None

    def value(self):
        return self.n if self.loop is None else self.loop + self.n

    def __call__(self, ins):
        self.n += 1
        ins.then_inc(self.sem, 1)
        self.eng.wait_ge(self.sem, self.value())

    def enter(self, i, per):
        self.loop, self.start, self.per = i * per, self.n, per

    def leave(self, count):
        assert self.n - self.start == self.per, (self.n - self.start, self.per)
        self.n, self.loop = self.start + self.per * count, None


def build(nc, a, o):
    ctx = ExitStack()
    with ctx:
        def sb(name, cols, dt=F32, rows=P):
            return ctx.enter_context(nc.sbuf_tensor(name, [rows, cols], dt))

        def sem(name):
            return ctx.enter_context(nc.semaphore(name))

        ident, ones, iota = sb("ident", P), sb("ones", P), sb("iota", P)
        vec = sb("vec", V_N)
        modT = sb("modT", 96 * NCOND)
        siluc = sb("siluc", KC * NCOND)
        scaleg = sb("scaleg", KC * NCOND)
        gla_mask, gla_smask = sb("gla_mask", P, U32), sb("gla_smask", TS, U32, TS)
        cap, scap = sb("cap", P), sb("scap", TS, F32, TS)
        segm = sb("segm", NSEQ, F32, TS)
        gla_reset, ml_reset = sb("gla_reset", T), sb("ml_reset", T, F32, 32)
        sel_all = sb("sel", HEADS * P)
        sel = sel_all[0:32, :]
        gbias = sb("gbias", 2, F32, HEADS)
        m0 = sb("m0", NSEQ, F32, HEADS)
        rstd = sb("rstd", T)
        gate_tmp = sb("gate_tmp", TS)[:, :]
        attw = sb("attw", 4 * P + 2 * TS)
        ada_rows = sb("ada_rows", 2 * WT, F32, NCOND)

        AR = 46720
        arena_at = nc.sbuf_base
        arena = sb("arena", AR)

        def rounded(name, off, n):
            assert off + n <= AR
            return nc.alloc_sbuf_tensor_at(name, [P, n], F32R, offset=arena_at + 4 * off)

        def at(off, n, rows=P):
            assert off + n <= AR
            return arena[0:rows, off:off + n]

        HT, RING, ZF = 0, KC * T, KC * T + 2 * KC * WT
        VT = ZF + Z_N * T
        SM = VT + NT * 1536
        hT = at(HT, KC * T).rearrange("p (c t) -> p c t", t=T)
        ring = [at(RING + s * KC * WT, KC * WT).rearrange("p (c n) -> p c n", c=KC) for s in range(2)]
        zF = at(ZF, Z_N * T).rearrange("p (c t) -> p c t", t=T)
        xT = at(ZF, KC * T).rearrange("p (c t) -> p c t", t=T)
        sq = at(VT, 2 * T).rearrange("p (b t) -> p b t", t=T)
        vT = at(VT, NT * 1536).rearrange("p (n c) -> p n c", c=1536)
        wsmall = at(ZF + Z_N * T - KC * 70, KC * 70).rearrange("p (c n) -> p c n", n=70)
        rows = at(SM, 3 * T).rearrange("p (r t) -> p r t", t=T)
        mixT = zF[:, 0:KC, :]

        SC = 0
        g_la = at(SC, 3 * T).rearrange("p (c t) -> p c t", t=T)
        g_B = at(SC + 3 * T, 3 * T).rearrange("p (c t) -> p c t", t=T)
        g_e1 = at(SC + 6 * T, 3 * T).rearrange("p (c t) -> p c t", t=T)
        g_e2 = at(SC + 9 * T, 3 * T).rearrange("p (c t) -> p c t", t=T)
        q0 = SC + 12 * T
        g_kd = at(q0, NT * 384).rearrange("p (n c) -> p n c", c=384)
        g_Sm = at(q0 + 1920, 16 * P).rearrange("p (n c) -> p n c", c=P)
        g_S0 = at(q0 + 3968, 8 * P).rearrange("p (n c) -> p n c", c=P)
        g_S0m = at(q0 + 4992, 8 * P).rearrange("p (n c) -> p n c", c=P)
        g_kdm = at(q0 + 6016, 8 * P, TS).rearrange("p (n c) -> p n c", c=P)
        g_S = at(q0 + 7040, 2 * P).rearrange("p (n c) -> p n c", c=P)
        g_wgu = at(q0 + 7296, 384, 16)
        g_sc = at(q0 + 7680, 3 * 3 * 24).rearrange("p (k c n) -> p k c n", k=3, n=24)
        assert q0 + 7680 + 216 <= ZF

        r0 = 0
        m_rows = at(r0, 7 * T, 32).rearrange("p (r t) -> p r t", t=T)
        m_small = at(r0 + 7 * T, 64, 32)
        m_col = at(r0 + 7 * T + 64, 2 * NT * HEADS).rearrange("p (k n h) -> p k n h", k=2, h=HEADS)
        m_dec = at(r0 + 7 * T + 128, HEADS * 12).rearrange("p (h n) -> p h n", n=12)
        r1 = r0 + 7 * T + 256
        m_qw = at(r1, T)
        m_E = at(r1 + T, T)
        m_D = at(r1 + 2 * T, T)
        m_kw = at(r1 + 3 * T, NT * P).rearrange("p (n c) -> p n c", c=P)
        r2 = r1 + 3 * T + NT * P
        m_C = at(r2, 4 * 129).rearrange("p (n c) -> p n c", c=129)
        m_Cs = at(r2 + 516, 2 * NSEQ * 129).rearrange("p (k n c) -> p k n c", k=2, c=129)
        m_nb = at(r2 + 516 + 2064, 3 * P).rearrange("p (n c) -> p n c", c=P)
        m_nbs = at(r2 + 516 + 2064 + 384, NSEQ * P).rearrange("p (n c) -> p n c", c=P)
        m_kwm = at(r2 + 516 + 2064 + 384 + 1024, NSEQ * P, TS).rearrange("p (n c) -> p n c", c=P)
        att_p = attw[:, 0:4 * P].rearrange("p (n h c) -> p n h c", n=2, h=2)
        att_s = attw[:, 4 * P:4 * P + 2 * TS].rearrange("p (h c) -> p h c", h=2)
        m_h = [zF[:, Z_MQ + h, :] for h in range(HEADS)]
        assert r2 + 516 + 2064 + 384 + 2048 <= ZF

        def raw_head(c):
            return zF[:, Z_MQ + c - 6] if c >= 6 else zF[:, (Z_GK if c % 2 else Z_GQ) + c // 2]

        n_sq = at(0, 2 * T).rearrange("p (b t) -> p b t", t=T)
        n_rs = at(2 * T, 2 * T).rearrange("p (b t) -> p b t", t=T)

        TC = P
        s_tab = at(0, 2 * S5C * TC).rearrange("p (k s t) -> p k s t", k=2, s=S5C)
        s_BT = at(VT, 2 * S5C * P).rearrange("p (k s c) -> p k s c", k=2, c=P)
        s_CT = at(5120, 2 * S5C * 32).rearrange("p (k s c) -> p k s c", k=2, c=32)
        s_t = at(6144, 4 * 4 * TC).rearrange("p (k s t) -> p k s t", k=4, t=TC)
        s_in = at(8192, 2 * 4 * 160).rearrange("p (k s t) -> p k s t", k=2, t=160)
        s_g = at(9472, 2 * 4 * 160).rearrange("p (k s t) -> p k s t", k=2, t=160)
        s_h = at(10752, 2 * 4 * TC).rearrange("p (k s t) -> p k s t", k=2, t=TC)
        s_g0 = at(11776, 2 * S5C).rearrange("p (k s) -> p k s", k=2)
        s_h0 = at(11808, 2 * S5C * NSEQ).rearrange("p (k s b) -> p k s b", k=2, b=NSEQ)
        s_hn = at(12064, 2 * S5C * NSEQ).rearrange("p (k s b) -> p k s b", k=2, b=NSEQ)
        s_hp = at(12320, 2 * S5C).rearrange("p (k s) -> p k s", k=2)
        s_par = at(12352, 16 * S5C).rearrange("p (k s) -> p k s", k=16)
        s_rhos = at(12736, 72)
        s_B = at(6144, 4 * S5C * 32).rearrange("p (k s c) -> p k s c", k=4, c=32)
        s_rhosm = at(4096, 72)
        assert 12736 + 72 <= RING + KC * WT
        ada_ring = [at(x, KC * WT).rearrange("p (c n) -> p c n", c=KC) for x in (VT + 2 * S5C * P, RING + KC * WT)]
        s_gl = at(ZF + Z_GQ * T, 4 * T).rearrange("p (c t) -> p c t", t=T)
        s_wg = at(ZF + (Z_GQ + 4) * T, 4 * 512).rearrange("p (c n) -> p c n", c=4)
        s_sg = at(ZF + (Z_GQ + 8) * T, 4 * T).rearrange("p (c t) -> p c t", t=T)

        xres = at(ZF + KC * T, KC * T).rearrange("p (c t) -> p c t", t=T)
        sq2 = at(ZF, 2 * T).rearrange("p (b t) -> p b t", t=T)

        h2T = nc.alloc_sbuf_tensor_at("h2T", [P, KC * T], F32, offset=arena_at)
        h_hi, h_lo = rounded("h_hi", KC * T, KC * T), rounded("h_lo", 0, KC * T)
        h_part = [t[:, :].rearrange("p (c t) -> p c t", t=T) for t in (h_hi, h_lo)]
        U0 = 2 * KC * T
        blk_raw = [at(U0 + 2 * D * s, D) for s in range(3)]
        blk_lo = [rounded(f"blk_lo{s}", U0 + 2 * D * s, D) for s in range(3)]
        blk_hi = [rounded(f"blk_hi{s}", U0 + 2 * D * s + D, D) for s in range(3)]
        A0 = U0 + 6 * D
        actv = at(A0, 3 * T).rearrange("p (b t) -> p b t", t=T)
        p_qT = actv
        C0 = A0 + 3 * T
        p_sc = at(C0, NT * 2 * PH * NK).rearrange("p (n c k) -> p n c k", n=NT, k=NK)
        R1 = C0 + NT * 2 * PH * NK
        p_keys = at(R1, 2 * PH * NK).rearrange("p (c n) -> p c n", n=NK)
        p_rep, p_cand = at(R1, 256), at(R1 + 256, 256)
        p_au = arena[:, R1 + 512:R1 + 640].bitcast(U32)
        p_oh = at(R1 + 640, 1024).rearrange("p (n k) -> p n k", k=TOPK)
        p_sel = at(R1 + 1664, 3 * P).rearrange("p (r n) -> p r n", r=3)
        p_sm = at(R1 + 2048, 2 * PH)
        p_selT = at(R1 + 2064, 3 * 640).rearrange("p (r t) -> p r t", r=3)
        p_sv = sel_all[:, 0:256].rearrange("p (h s k) -> p h s k", s=2, k=TOPK)
        p_siu = sel_all[:, 256:512].bitcast(U32).rearrange("p (c k) -> p c k", k=TOPK)
        p_sif = sel_all[:, 512:768].rearrange("p (h s k) -> p h s k", s=2, k=TOPK)
        p_ab = gla_reset[:, 0:256].rearrange("p (s n) -> p s n", s=2)
        p_tv = gla_reset[:, 256:384].rearrange("p (h k) -> p h k", k=TOPK)
        p_posu = gla_reset[:, 384:512].bitcast(U32)
        stage = [at(C0 + s * NK * TBLK, NK * TBLK).rearrange("p (i t) -> p i t", t=TBLK) for s in range(2)]
        o_j = [at(C0 + 8192 + s * 512, 512).rearrange("p (t n) -> p t n", n=P) for s in range(2)]
        o_i = [at(C0 + 9216 + s * 512, 512).rearrange("p (t n) -> p t n", n=P) for s in range(2)]
        o_e = p_oh[:, 0:32].rearrange("p n k -> p (n k)").rearrange("p (t n) -> p t n", n=P)

        V_AT = (C0, 0)
        C_AT = (C0 + 4 * D, 4 * D)
        ev_raw = [at(x, 2 * D) for x in V_AT]
        ev_lo = [rounded(f"ev_lo{k}", x, 2 * D) for k, x in enumerate(V_AT)]
        ev_hi = [rounded(f"ev_hi{k}", x + 2 * D, 2 * D) for k, x in enumerate(V_AT)]
        co_hi = [rounded(f"co_hi{k}", x, GRP * T) for k, x in enumerate(C_AT)]
        co_lo = [rounded(f"co_lo{k}", x + GRP * T, GRP * T) for k, x in enumerate(C_AT)]
        acts = [at(x + 2 * GRP * T, GRP * T) for x in C_AT]
        gates = [at(x + 3 * GRP * T, GRP * T).rearrange("p (n b t) -> p n b t", b=GRP, t=TBLK) for x in C_AT]
        acc = at(U0, KC * T).rearrange("p (c t) -> p c t", t=T)
        xfin = at(0, KC * T).rearrange("p (c t) -> p c t", t=T)
        sqf = at(KC * T, 2 * T).rearrange("p (b t) -> p b t", t=T)

        PS = ctx.enter_context(nc.psum_tensor("PS", [P, 4096], F32))

        def bank(n, lo=0, cols=512, rows_=P, base=0):
            return PS[base:base + rows_, 512 * n + lo:512 * n + lo + cols]

        def flat(pair, cols=T):
            return PS[:, 1024 * pair:1024 * pair + cols]

        def split(pair):
            return PS[:, 1024 * pair:1024 * pair + 1024].rearrange("p (b t) -> p b t", b=2)[:, :, 0:HALF]

        def halves(ap):
            return ap.rearrange("p (b t) -> p b t", b=2)

        def seqs(ap):
            return ap.rearrange("p (b t) -> p b t", t=SLEN)

        gd = nc.dram_tensor("gate_scratch", (P, T // TBLK, NK, TBLK), F32, kind="Internal").ap()
        ad = nc.dram_tensor("activation_scratch", (P, NK, T), F32, kind="Internal").ap()
        xd = nc.dram_tensor("x_scratch", (P, KC, T), F32, kind="Internal").ap()

        cond_in, x_in, small_in = sem("cond_in"), sem("x_in"), sem("small_in")
        ring_in = [sem(f"ring{s}_in") for s in range(2)]
        consts_made, masks_made = sem("consts_made"), sem("masks_made")
        silu_made = sem("silu_made")
        dve_step, act_step, pool_step = sem("dve_step"), sem("act_step"), sem("pool_step")
        sq_made, sq_used, ms_made, root_made = sem("sq_made"), sem("sq_used"), sem("ms_made"), sem("root_made")
        norm_made, mod_made = sem("norm_made"), sem("mod_made")
        ada_in = [sem(f"ada{s}_in") for s in range(2)]
        mod1_made = sem("mod1_made")
        ada_made, ada_out, ada_turned = sem("ada_made"), sem("ada_out"), sem("ada_turned")
        prod_made, prod_out = sem("prod_made"), sem("prod_out")
        wsmall_clear, wsmall_in, small_made, small_out = (sem("wsmall_clear"), sem("wsmall_in"), sem("small_made"),
                                                          sem("small_out"))
        v_made, v_out = sem("v_made"), sem("v_out")
        gla_w_in, gla_state_in, gla_stored = sem("gla_w_in"), sem("gla_state_in"), sem("gla_stored")
        gla_lin, gla_ln, gla_dist, gla_exp, gla_kdec = (sem("gla_lin"), sem("gla_ln"), sem("gla_dist"),
                                                        sem("gla_exp"), sem("gla_kdec"))
        gla_tr, gla_ktok, gla_kv, gla_sm, gla_att, gla_attw = (sem("gla_tr"), sem("gla_ktok"), sem("gla_kv"),
                                                               sem("gla_sm"), sem("gla_att"), sem("gla_attw"))
        gla_oout, gla_kvs, gla_states = sem("gla_oout"), sem("gla_kvs"), sem("gla_states")
        ml_state_in = [sem(f"ml_state{k}_in") for k in range(2)]
        ml_stored = [sem(f"ml_state{k}_stored") for k in range(2)]
        m_stored = sem("m_stored")
        ml_ln, ml_pre, ml_rows, ml_cols, ml_colsout = (sem("ml_ln"), sem("ml_pre"), sem("ml_rows"), sem("ml_cols"),
                                                       sem("ml_colsout"))
        ml_bc, ml_kw, ml_floor, ml_spread = sem("ml_bc"), sem("ml_kw"), sem("ml_floor"), sem("ml_spread")
        ml_s, ml_kv, ml_arg, ml_exp, ml_sd, ml_o, ml_kvs, ml_head = (
            sem("ml_s"), sem("ml_kv"), sem("ml_arg"), sem("ml_exp"), sem("ml_sd"), sem("ml_o"), sem("ml_kvs"),
            sem("ml_head"))
        hn_gate, hn_sq, hn_sum, hn_ms, hn_root, hn_out = (sem("hn_gate"), sem("hn_sq"), sem("hn_sum"), sem("hn_ms"),
                                                          sem("hn_root"), sem("hn_out"))
        s5_clear, s5_in, s5_ang, s5_trig, s5_bbar, s5_bt, s5_ready = (
            sem("s5_clear"), sem("s5_in"), sem("s5_ang"), sem("s5_trig"), sem("s5_bbar"), sem("s5_bt"),
            sem("s5_ready"))
        s5_exp, s5_dt, s5_sum = sem("s5_exp"), sem("s5_dt"), sem("s5_sum")
        gla_oatt, s5_ldt = sem("gla_oatt"), sem("s5_ldt")
        s5_bu, s5_buout, s5_h, s5_y, s5_yout = (sem("s5_bu"), sem("s5_buout"), sem("s5_h"), sem("s5_y"),
                                                sem("s5_yout"))
        s5_gelu, s5_glu, s5_sig, s5_mix, s5_stored = (sem("s5_gelu"), sem("s5_glu"), sem("s5_sig"), sem("s5_mix"),
                                                      sem("s5_stored"))
        x_again, res_made, x_saved = sem("x_again"), sem("res_made"), sem("x_saved")
        keys_in, sc_made, sc_out, sc_clear = sem("keys_in"), sem("sc_made"), sem("sc_out"), sem("sc_clear")
        h_hi_made, h_lo_made = sem("h_hi_made"), sem("h_lo_made")
        soft_in, soft_out = sem("soft_in"), sem("soft_out")
        sel_made, sel_tr, sel_out = sem("sel_made"), sem("sel_tr"), sem("sel_out")
        oh_made, g_made, g_out = sem("oh_made"), sem("g_made"), sem("g_out")
        g_saved = [sem(f"stage{k}_saved") for k in range(2)]
        blk_in = [sem(f"blk{k}_in") for k in range(3)]
        blk_hi_made, blk_lo_made, blk_made, blk_out = (sem("blk_hi_made"), sem("blk_lo_made"), sem("blk_made"),
                                                       sem("blk_out"))
        a_saved = [sem(f"a{k}_saved") for k in range(3)]
        ev_in = [sem(f"ev{k}_in") for k in range(2)]
        ag_in = [sem(f"ag{k}_in") for k in range(2)]
        ev_hi_made, ev_lo_made, co_made, co_hi_made, co_lo_made = (sem("ev_hi_made"), sem("ev_lo_made"), sem("co_made"),
                                                                   sem("co_hi_made"), sem("co_lo_made"))
        vp_made, acc_made, acc_clear = sem("vp_made"), sem("acc_made"), sem("acc_clear")
        x_back, fin_made, y_made, y_out = sem("x_back"), sem("fin_made"), sem("y_made"), sem("y_out")


        NQ, NB_ALL = KC, KC + NK
        TB = 9
        GB, GL = NQ + 2 + TB * NT, T // (2 * TBLK)

        PARTS = {"ada0": ("w_ada", 0, 16, ada_made, 1, 0), "f": ("w_f", 0, 17, prod_made, 2, 0),
                 "v": ("w_v", 0, 6, v_made, NT, 0), "out": ("w_out", 0, 8, prod_made, 2, 34),
                 }

        def fills(name):
            n = [0, 0]
            for k, part in PARTS.items():
                if k == name:
                    return n
                n = [n[0] + (part[2] + 1) // 2, n[1] + part[2] // 2]

        block = ctx.enter_context(nc.Block())

        @block.sync
        def _(sp):
            order = list(PARTS)

            def stream_part(name, after_first=None):
                src, first, tiles, done, per, before = PARTS[name]
                w = a[src]

                def load(s, tile_):
                    sp.dma_start(ring[s], w[tile_].rearrange("p (c n) -> p c n", c=KC)).then_inc(ring_in[s], 16)

                for s in range(2):
                    if order.index(name):
                        _, _, tiles0, done0, per0, before0 = PARTS[order[order.index(name) - 1]]
                        last = tiles0 - 1 - (tiles0 - 1 - s) % 2
                        sp.wait_ge(done0, before0 + per0 * (last + 1))
                    load(s, first + s)
                if after_first:
                    after_first()
                with sp.Fori(1, tiles // 2) as i:
                    for s in range(2):
                        sp.wait_ge(done, i * (2 * per) + (before + per * (s - 1)))
                        load(s, i * 2 + (first + s))
                if tiles % 2:
                    sp.wait_ge(done, before + per * (tiles - 2))
                    load(0, first + tiles - 1)

            sp.dma_start(siluc[:, :], a["cT"]).then_inc(cond_in, 16)
            sp.dma_start(vec[:, :], a["vecs"]).then_inc(small_in, 16)
            sp.dma_start(gbias[:, :], a["gate_bias"]).then_inc(small_in, 16)
            sp.dma_start(m0[:, :], a["m0"]).then_inc(small_in, 16)
            sp.dma_start(xT, a["xT"]).then_inc(x_in, 16)
            stream_part("ada0")
            sp.wait_ge(wsmall_clear, 1)
            for lo, n, dst in ((0, 16, 0), (16, 6, 32), (22, 6, 64)):
                sp.dma_start(wsmall[:, :, dst:dst + n],
                             a["w_s"].rearrange("p (c n) -> p c n", c=KC)[:, :, lo:lo + n]).then_inc(wsmall_in, 16)
            stream_part("f")
            stream_part("v")

            sp.wait_ge(v_made, 6 * NT)
            sp.dma_start(g_wgu, a["w_gate_up"]).then_inc(gla_w_in, 16)
            for p in range(3):
                if p:
                    sp.wait_ge(gla_stored, 32 * p)
                sp.dma_start(g_S0, a["state_gla"].rearrange("b (p q) v -> p q b v", q=P)[p]).then_inc(gla_state_in, 16)
                sp.wait_ge(gla_states, p + 1)
                sp.dma_start(o["gla_p"].rearrange("(p q) v -> p q v", q=P)[p], g_S[:, 0, :]).then_inc(gla_stored, 16)
                sp.dma_start(o["gla_s"].rearrange("b (p q) v -> p q b v", q=P)[p], g_S0).then_inc(gla_stored, 16)
            sp.wait_ge(gla_stored, 96)

            def store_ml(h):
                sp.wait_ge(ml_head, h + 1)
                cs = m_Cs[:, h % 2]
                sp.dma_start(o["c_p"][h], m_C[:, 3, 0:P]).then_inc(ml_stored[h % 2], 16)
                sp.dma_start(o["n_p"][:, h:h + 1], m_C[:, 3, P:P + 1], allow_slow_non_contiguous=True).then_inc(ml_stored[h % 2], 16)
                sp.dma_start(o["c_s"][:, h].rearrange("b k v -> k b v"), cs[:, :, 0:P]).then_inc(ml_stored[h % 2], 16)
                sp.dma_start(o["n_s"][h], cs[:, :, P], allow_slow_non_contiguous=True).then_inc(ml_stored[h % 2], 16)

            sp.wait_ge(gla_oout, 6)
            for h in range(HEADS):
                if h >= 2:
                    sp.wait_ge(ml_stored[h % 2], 64 * (h // 2))
                cs = m_Cs[:, h % 2]
                sp.dma_start(cs[:, :, 0:P], a["state_c"][:, h].rearrange("b k v -> k b v")).then_inc(ml_state_in[h % 2], 16)
                sp.dma_start(cs[:, :, P], a["state_n"][h], allow_slow_non_contiguous=True).then_inc(ml_state_in[h % 2], 16)
                if h >= 1:
                    store_ml(h - 1)
            store_ml(HEADS - 1)

            def load_ada(u):
                if u >= 2:
                    sp.wait_ge(ada_made, 16 + u - 1)
                sp.dma_start(ada_ring[u % 2], a["w_ada"][16 + u].rearrange("p (c n) -> p c n", c=KC)
                             ).then_inc(ada_in[u % 2], 16)

            for u in range(2):
                load_ada(u)
            sp.dma_start(o["m_p"], m_small[0:HEADS, 27:28]).then_inc(m_stored, 16)
            sp.dma_start(o["m_s"], m_small[0:HEADS, 28:36]).then_inc(m_stored, 16)
            for k in range(2):
                sp.wait_ge(ml_stored[k], 64 * HEADS // 2)
            sp.wait_ge(m_stored, 32)

            for u in range(2, 14):
                load_ada(u)

            sp.wait_ge(s5_clear, 1)
            for k in range(2):
                for g in range(2):
                    sp.dma_start(s_B[64 * g:64 * g + 64, k, :, 16 * g:16 * g + 16], a["s5_b"][k, g]).then_inc(s5_in, 16)
                    sp.dma_start(s_CT[64 * g:64 * g + 64, k, :, 16 * g:16 * g + 16], a["s5_c"][k, g]).then_inc(s5_in, 16)
            sp.dma_start(s_h0, a["s5_h0"]).then_inc(s5_in, 16)
            sp.dma_start(s_wg, a["w_glu"].rearrange("p (c n) -> p c n", c=4)).then_inc(s5_in, 16)
            for u in range(14, 32):
                load_ada(u)
            sp.wait_ge(s5_h, 20)
            sp.dma_start(o["s5_s"], s_hn).then_inc(s5_stored, 16)
            sp.dma_start(o["s5_p"], s_hp).then_inc(s5_stored, 16)
            sp.wait_ge(s5_stored, 32)

            sp.wait_ge(s5_yout, 20)
            sp.wait_ge(ada_made, 48)

            def load_x_again():
                sp.wait_ge(s5_mix, 3)
                sp.dma_start(xres, a["xT"]).then_inc(x_again, 16)

            stream_part("out", load_x_again)
            sp.wait_ge(res_made, KC)
            sp.dma_start(xd, xres).then_inc(x_saved, 16)
            sp.wait_ge(x_saved, 16)
            sp.wait_ge(norm_made, 2)
            sp.dma_start(p_keys, a["keysT"].rearrange("p (c n) -> p c n", n=NK)).then_inc(keys_in, 16)

            def load_block(src, n, k):
                sp.dma_start(blk_raw[k], src).then_inc(blk_in[k], 16)

            for n in range(3):
                load_block(a["w_q"][n], n, n)
            for n in range(3, NQ + 2):
                sp.wait_ge(blk_made, n - 2)
                load_block(a["w_q"][n] if n < NQ else a["peer_ut"][n - NQ], n, n % 3)
            with sp.Fori(0, (NB_ALL - NQ - 2) // 3) as i:
                for k in range(3):
                    sp.wait_ge(blk_made, i * 3 + (NQ + k))
                    load_block(a["peer_ut"][i * 3 + (2 + k)], None, (NQ + 2 + k) % 3)

            def load_values(r, p):
                sp.dma_start(ev_raw[p].rearrange("p (b n) -> p b n", b=GRP),
                             a["peer_v"][bass.ds(r * GRP, GRP)].rearrange("b p n -> p b n")).then_inc(ev_in[p], 16)

            def load_factors(r, p):
                sp.dma_start(acts[p].rearrange("p (b t) -> p b t", t=T), ad[:, bass.ds(r * GRP, GRP), :]).then_inc(ag_in[p], 16)
                sp.dma_start(gates[p], gd[:, :, bass.ds(r * GRP, GRP), :]).then_inc(ag_in[p], 16)

            for k in range(2):
                sp.wait_ge(g_saved[k], 16 * (GL + 1))
            load_values(0, 0)
            for k in range(3):
                sp.wait_ge(a_saved[k], 16 * (1 + len([n for n in range(NQ, NB_ALL) if n % 3 == k])))
            load_factors(0, 0)
            load_factors(1, 1)
            load_values(1, 1)
            with sp.Fori(1, ROUNDS // 2) as i:
                for p in range(2):
                    sp.wait_ge(vp_made, i * (2 * KC) + (KC * (p - 1) + 1))
                    load_factors(i * 2 + p, p)
                    load_values(i * 2 + p, p)
            sp.wait_ge(vp_made, ROUNDS * KC + 1)
            sp.dma_start(xfin, xd).then_inc(x_back, 16)
            sp.wait_ge(y_made, 1)
            sp.dma_start(o["yT"], xfin).then_inc(y_out, 16)
            sp.wait_ge(y_out, 16)

        @block.gpsimd
        def _(pool):
            step = Chain(pool, pool_step)
            pool.memset(ones[:, :], 1.0).then_inc(consts_made, 1)
            step(pool.memset(ident[:, :], 0.0))
            pool.affine_select(out=ident[:, :], in_=ident[:, :], compare_op=ALU.not_equal, fill=1.0, base=0,
                               pattern=[[-1, P]], channel_multiplier=1).then_inc(consts_made, 1)
            pool.iota(iota[:, :], [[1, P]], base=0, channel_multiplier=0,
                      allow_small_or_imprecise_dtypes=True).then_inc(consts_made, 1)
            pool.memset(wsmall, 0.0).then_inc(wsmall_clear, 1)
            pool.wait_ge(consts_made, 3)
            pool.wait_ge(wsmall_clear, 1)
            step(pool.memset(vT[TS:P, 4], 0.0))

            def keep(ap, pattern, mult, fill=0.0, base=0):
                step(pool.affine_select(out=ap, in_=ap, compare_op=ALU.is_ge, fill=fill, base=base,
                                        pattern=pattern, channel_multiplier=mult))

            step(pool.memset(cap[:, :], 0.0))
            keep(cap[:, :], [[1, P]], -1, -BIG)
            step(pool.memset(scap[:, :], 0.0))
            keep(scap[:, :], [[1, TS]], -1, -BIG)
            keep(seqs(scap[:, :]), [[-SLEN, NSEQ], [0, SLEN]], 1, -BIG)
            gm, gs = gla_mask[:, :].bitcast(F32), gla_smask[:, :].bitcast(F32)
            step(pool.memset(gm, 1.0))
            keep(gm, [[1, P]], -1)
            keep(gm.rearrange("p (b t) -> p b t", t=GC), [[-GC, P // GC], [0, GC]], 1)
            step(pool.memset(gs, 1.0))
            keep(gs, [[1, TS]], -1)
            keep(seqs(gs), [[-SLEN, NSEQ], [0, SLEN]], 1)
            step(pool.memset(segm[:, :], 1.0))
            keep(segm[:, :], [[-SLEN, NSEQ]], 1)
            keep(segm[:, :], [[SLEN, NSEQ]], -1, 0.0, SLEN - 1)
            step(pool.memset(gla_reset[:, :], 1.0))
            step(pool.memset(ml_reset[:, :], 1.0))
            step(pool.memset(gla_reset[:, 0:TP:GC], 0.0))
            step(pool.memset(gla_reset[:, TP:T:SLEN], 0.0))
            step(pool.memset(ml_reset[:, 0:TP:P], 0.0))
            step(pool.memset(ml_reset[:, TP:T:SLEN], 0.0))
            step(pool.memset(sel[:, :], 1.0))
            s3 = sel[:, :].rearrange("p (h n) -> p h n", n=P)
            keep(s3, [[-1, HEADS], [0, P]], 1)
            keep(s3, [[1, HEADS], [0, P]], -1)
            pool.memset(attw[:, :], 0.0).then_inc(masks_made, 1)

            for h in range(HEADS):
                cs = m_Cs[:, h % 2]
                pool.wait_ge(ml_state_in[h % 2], 32 * (h // 2 + 1))
                if h:
                    pool.wait_ge(ml_o, h)
                    pool.wait_ge(ml_kvs, h)
                pool.tensor_copy(m_nbs, cs[:, :, P:P + 1].broadcast_to([P, NSEQ, P])).then_inc(ml_spread, 1)
                pool.wait_ge(ml_kw, h + 1)
                pool.tensor_tensor(m_kwm, m_kw[0:TS, 4:5, :].broadcast_to([TS, NSEQ, P]),
                                   segm[:, :].unsqueeze(2).broadcast_to([TS, NSEQ, P]), ALU.mult).then_inc(ml_spread, 1)

            pool.wait_ge(ml_head, HEADS)
            pool.wait_ge(hn_out, 12)
            for k in range(2):
                pool.wait_ge(ml_stored[k], 64 * HEADS // 2)
            pool.wait_ge(m_stored, 32)
            step(pool.memset(s_B[:, 0:2], 0.0))
            step(pool.memset(s_BT, 0.0))
            pool.memset(s_CT, 0.0).then_inc(s5_clear, 1)

            pool.wait_ge(norm_made, 2)
            pool.wait_ge(x_saved, 16)
            pool.wait_ge(s5_clear, 1)
            pool.memset(p_sc[64:P, 4], 0.0).then_inc(sc_clear, 1)
            pool.wait_ge(blk_made, NB_ALL)
            pool.memset(acc, 0.0).then_inc(acc_clear, 1)

        @block.scalar
        def _(act):
            step = Chain(act, act_step)

            def square_chunks(src, dst, n0):
                for c in range(KC):
                    if c >= 2:
                        act.wait_ge(sq_used, n0 * KC + c - 1)
                    act.activation(dst[:, c % 2], src[:, c], ACT.Square).then_inc(sq_made, 1)

            def ada_first_out():
                with act.Fori(0, 8) as i:
                    for s in range(2):
                        act.wait_ge(ada_made, i * 2 + (s + 1))
                        act.wait_ge(ada_turned, i * 2 + (s + 1))
                        act.activation(ada_rows[:, WT * s:WT * s + WT], bank(2 * s + 1, 0, WT, NCOND),
                                       ACT.Copy).then_inc(ada_out, 1)

            def ada_tile_out(u):
                act.wait_ge(ada_made, 16 + u + 1)
                act.wait_ge(ada_turned, 16 + u + 1)
                act.activation(ada_rows[:, WT * (u % 2):WT * (u % 2) + WT], bank(6, 0, WT, NCOND),
                               ACT.Copy).then_inc(ada_out, 1)

            def root(n0):
                act.wait_ge(ms_made, n0 + 1)
                act.activation(rstd[:, :], rstd[:, :], ACT.Sqrt).then_inc(root_made, 1)

            for places, n in [(ada_out, 2), (v_out, 2), (blk_out, 3), (g_out, 2)] + [(x, 16) for x in g_saved + a_saved]:
                act.sem_inc(places, n)
            act.wait_ge(cond_in, 16)
            act.activation(siluc[:, :], siluc[:, :], ACT.Silu).then_inc(silu_made, 1)
            act.wait_ge(x_in, 16)
            square_chunks(xT, sq, 0)
            root(0)

            ada_first_out()

            act.wait_ge(small_made, 1)
            act.wait_ge(small_in, 48)
            act.activation(rows[0:16, 0], PS[0:16, 3072:3072 + T], ACT.Copy).then_inc(small_out, 1)
            act.activation(rows[0:HEADS, 1], PS[32:32 + HEADS, 3072:3072 + T], ACT.Identity,
                           bias=gbias[:, 0:1]).then_inc(small_out, 1)
            act.activation(rows[0:HEADS, 2], PS[64:64 + HEADS, 3072:3072 + T], ACT.Identity,
                           bias=gbias[:, 1:2]).then_inc(small_out, 1)

            with act.Fori(0, 8) as i:
                for m in range(4):
                    act.wait_ge(prod_made, i * 4 + m + 1)
                    act.activation(halves(zF[:, bass.ds(i * 4 + m, 1), :].rearrange("p c t -> p (c t)")), split(m),
                                   ACT.Copy).then_inc(prod_out, 1)
            for m in range(2):
                act.wait_ge(prod_made, 32 + m + 1)
                act.activation(halves(zF[:, 32 + m]), split(m), ACT.Copy).then_inc(prod_out, 1)

            with act.Fori(0, 3) as i:
                for s in range(2):
                    for n in range(NT):
                        q = NT * s + n
                        act.wait_ge(v_made, i * 10 + q + 1)
                        nr = P if n < 4 else TS
                        act.activation(vT[0:nr, n, bass.ds((i * 2 + s) * WT, WT)], bank(2 * (q % 2), 0, WT, nr),
                                       ACT.Copy).then_inc(v_out, 1)

            for p in range(3):
                act.wait_ge(gla_lin, p + 1)
                ins = act.activation(g_la[:, p], flat(p), ACT.Identity, bias=vec[:, V_BG + p:V_BG + p + 1])
                step(ins)
            step(act.activation(g_e1, g_la, ACT.Abs))
            step(act.activation(g_e1, g_e1, ACT.Exp, scale=-1.0))
            act.activation(g_e2, g_e1, ACT.Ln, bias=1.0).then_inc(gla_ln, 1)
            act.wait_ge(gla_dist, 1)
            act.activation(g_e1, g_la, ACT.Exp, scale=1.0 / GTAU).then_inc(gla_exp, 1)
            act.activation(g_e2, g_la, ACT.Exp, scale=-1.0 / GTAU).then_inc(gla_exp, 1)
            act.activation(g_sc, g_sc, ACT.Exp, scale=1.0 / GTAU).then_inc(gla_exp, 1)
            for n in range(NT):
                nr = P if n < 4 else TS
                act.wait_ge(gla_tr, n + 1)
                act.activation(g_kd[0:nr, n, :], bank(n, 0, 384, nr), ACT.Copy).then_inc(gla_ktok, 1)
            for p in range(3):
                act.wait_ge(gla_oatt, NT * (p + 1))
                for hh, zc in ((0, Z_GQ), (1, Z_GK)):
                    step(act.activation(zF[:, zc + p, 0:TP], bank(2 + hh), ACT.Copy))
                    act.activation(zF[:, zc + p, TP:T], bank(6 + hh, 0, TS), ACT.Copy).then_inc(gla_oout, 1)

            act.wait_ge(gla_stored, 96)
            act.wait_ge(gla_oout, 6)
            act.wait_ge(small_out, 3)
            act.wait_ge(gla_kvs, 3)
            step(act.activation(m_rows[0:HEADS, 3], rows[0:HEADS, 2], ACT.Abs))
            step(act.activation(m_rows[0:HEADS, 3], m_rows[0:HEADS, 3], ACT.Exp, scale=-1.0))
            act.activation(m_rows[0:HEADS, 4], m_rows[0:HEADS, 3], ACT.Ln, bias=1.0).then_inc(ml_ln, 1)
            act.wait_ge(ml_pre, 1)
            act.activation(m_rows[0:HEADS, 3], m_rows[0:HEADS, 3], ACT.Exp).then_inc(ml_rows, 1)
            act.activation(m_rows[0:HEADS, 4], m_rows[0:HEADS, 1], ACT.Exp, scale=-1.0).then_inc(ml_rows, 1)
            act.activation(m_rows[0:HEADS, 6], m_rows[0:HEADS, 6], ACT.Exp).then_inc(ml_rows, 1)
            act.activation(m_small[0:HEADS, 48:60], m_small[0:HEADS, 48:60], ACT.Exp).then_inc(ml_rows, 1)
            for h in range(HEADS):
                act.wait_ge(ml_bc, h + 1)
                act.activation(m_E, flat(1), ACT.Copy).then_inc(ml_floor, 1)
                act.wait_ge(ml_arg, h + 1)
                act.activation(m_D[:, 0:TP], m_D[:, 0:TP], ACT.Exp).then_inc(ml_exp, 1)
                act.activation(m_D[0:TS, TP:T], m_D[0:TS, TP:T], ACT.Exp).then_inc(ml_exp, 1)

            act.activation(zF[:, Z_GG:Z_GG + 6], zF[:, Z_GG:Z_GG + 6], ACT.Silu).then_inc(hn_gate, 1)
            act.activation(zF[:, Z_MO:Z_MO + 6], zF[:, Z_MO:Z_MO + 6], ACT.Sigmoid).then_inc(hn_gate, 1)
            act.wait_ge(ml_head, HEADS)
            for k in range(2):
                act.wait_ge(ml_stored[k], 64 * HEADS // 2)
            act.wait_ge(m_stored, 32)
            for c in range(12 + 1):
                if c < 12:
                    if c >= 2:
                        act.wait_ge(hn_sum, c - 1)
                    act.activation(n_sq[:, c % 2], raw_head(c), ACT.Square).then_inc(hn_sq, 1)
                if c >= 1:
                    act.wait_ge(hn_ms, c)
                    act.activation(n_rs[:, (c - 1) % 2], n_rs[:, (c - 1) % 2], ACT.Sqrt).then_inc(hn_root, 1)
                    ada_tile_out(c - 1)

            act.wait_ge(hn_out, 12)
            act.activation(s_par[:, 0], vec[:, V_LDT:V_LDT + 16], ACT.Exp).then_inc(s5_ldt, 1)
            act.wait_ge(s5_dt, 1)
            act.activation(s_par[:, 3], s_par[:, 1], ACT.Exp).then_inc(s5_exp, 1)
            act.wait_ge(s5_ang, 1)
            act.activation(s_par[:, 4], s_par[:, 4], ACT.Sin).then_inc(s5_trig, 1)
            act.activation(s_par[:, 5], s_par[:, 5], ACT.Sin).then_inc(s5_trig, 1)
            for k in range(2):
                act.wait_ge(s5_bt, k + 1)
                for j in range(4):
                    ins = act.activation(s_BT[32 * j:32 * j + 32, k, j::4, :],
                                         bank(k, 0, 512, 32, 32 * j).rearrange("p (n c) -> p n c", c=P), ACT.Copy)
                ins.then_inc(s5_ready, 1)
            for u in range(12, 32):
                ada_tile_out(u)
            act.wait_ge(s5_yout, 20)
            act.activation(s_gl, s_gl, ACT.Gelu_apprx_tanh).then_inc(s5_gelu, 1)
            for m in range(4):
                act.wait_ge(s5_glu, m + 1)
                act.activation(s_sg[:, m], flat(m), ACT.Sigmoid, bias=vec[:, V_BGLU + m:V_BGLU + m + 1]).then_inc(s5_sig, 1)
            act.wait_ge(s5_mix, 1)
            act.activation(s_gl, s_sg, ACT.Square).then_inc(s5_sig, 1)
            act.wait_ge(s5_mix, 2)
            act.activation(rstd[:, :], rstd[:, :], ACT.Sqrt).then_inc(s5_sig, 1)

            act.wait_ge(res_made, KC)
            square_chunks(xres, sq2, 1)
            root(1)

            act.wait_ge(norm_made, 2)
            act.activation(h_hi[:, :], h2T[:, :], ACT.Copy).then_inc(h_hi_made, 1)

            def high(n, k, fills):
                act.wait_ge(blk_in[k], fills)
                act.activation(blk_hi[k][:, :], blk_raw[k], ACT.Copy).then_inc(blk_hi_made, 1)

            def query_out(n, k):
                act.wait_ge(blk_made, n + 1)
                act.wait_ge(sc_made, n + 1)
                act.activation(halves(p_qT[:, k]), split(k), ACT.Copy).then_inc(blk_out, 1)

            def gelu_out(n, k, uses):
                act.wait_ge(blk_made, n + 1)
                act.wait_ge(a_saved[k], uses)
                act.activation(halves(actv[:, k]), split(k), ACT.Gelu_apprx_tanh).then_inc(blk_out, 1)

            def save(n, k):
                act.wait_ge(blk_out, n + 4)
                act.dma_start(ad[:, n - NQ] if isinstance(n, int) else ad[:, bass.ds(n - NQ, 1), :].rearrange("p b t -> p (b t)"),
                              actv[:, k]).then_inc(a_saved[k], 16)

            def uses(n):
                return 16 * (1 + len([m for m in range(NQ, n) if m % 3 == n % 3]))

            def step_block(n):
                if n <= NQ:
                    query_out(n - 1, (n - 1) % 3)
                else:
                    gelu_out(n - 1, (n - 1) % 3, uses(n - 1))
                if n + 1 < NB_ALL:
                    high(n + 1, (n + 1) % 3, 16 * ((n + 1) // 3 + 1))
                if n > NQ:
                    save(n - 1, (n - 1) % 3)

            high(0, 0, 16)
            high(1, 1, 16)
            with act.Fori(0, NQ // 3) as i:
                for k in range(3):
                    query_out(i * 3 + k, k)
                    high(None, (k + 2) % 3, i * 16 + 16 * ((k + 2) // 3 + 1))
            step_block(NQ)
            for n in range(NQ + 1, GB + 1):
                step_block(n)
                t, at_ = divmod(n - NQ - TB + 1, TB)
                if at_ == 0 and 0 <= t < NT:
                    act.wait_ge(soft_in, t + 1)
                    act.activation(p_tv, p_tv, ACT.Exp).then_inc(soft_out, 1)
                t, at_ = divmod(n - NQ - TB - 2, TB)
                if at_ == 0 and 0 <= t < NT:
                    act.wait_ge(sel_tr, t + 1)
                    act.activation(p_selT[:, :, P * t:P * t + P], bank(6, 0, 384).rearrange("p (r t) -> p r t", r=3),
                                   ACT.Copy).then_inc(sel_out, 1)

            with act.Fori(0, GL) as w:
                for u in range(16):
                    k = u // 8
                    if u % 8 == 0:
                        act.wait_ge(g_saved[k], w * 16 + 16)
                    act.wait_ge(g_made, w * 16 + u + 3)
                    act.activation(stage[k][:, :, 4 * (u % 8):4 * (u % 8) + 4].rearrange("p i t -> p t i"),
                                   bank(6 + u % 2).rearrange("p (t i) -> p t i", i=P), ACT.Copy).then_inc(g_out, 1)
                    if u % 8 == 7:
                        act.wait_ge(g_out, w * 16 + u + 3)
                        act.dma_start(gd[:, bass.ds(w * 2 + k, 1)].rearrange("p b i t -> p (b i) t"),
                                      stage[k]).then_inc(g_saved[k], 16)
                    if u in (4, 9, 15):
                        b = (4, 9, 15).index(u)
                        n0 = GB + 1 + b
                        gelu_out(w * 3 + (n0 - 1), (n0 - 1) % 3, w * 16 + uses(n0 - 1))
                        high(None, (n0 + 1) % 3, w * 16 + 16 * ((n0 + 1) // 3 + 1))
                        save(w * 3 + (n0 - 1), (n0 - 1) % 3)

            n0 = GB + 3 * GL + 1
            with act.Fori(0, (NB_ALL - n0 - 1) // 3) as i:
                for k in range(3):
                    n = n0 + k
                    gelu_out(i * 3 + (n - 1), (n - 1) % 3, i * 16 + uses(n - 1))
                    high(None, (n + 1) % 3, i * 16 + 16 * ((n + 1) // 3 + 1))
                    save(i * 3 + (n - 1), (n - 1) % 3)
            for n in range(n0 + 3 * ((NB_ALL - n0 - 1) // 3), NB_ALL + 1):
                step_block(n)

            def values_high(p, fills):
                act.wait_ge(ev_in[p], fills)
                act.activation(ev_hi[p][:, :], ev_raw[p], ACT.Copy).then_inc(ev_hi_made, 1)

            def coefficients_high(r, p):
                act.wait_ge(co_made, r + 1)
                act.activation(co_hi[p][:, :], acts[p], ACT.Copy).then_inc(co_hi_made, 1)

            values_high(0, 16)
            coefficients_high(0, 0)
            coefficients_high(1, 1)
            values_high(1, 16)
            with act.Fori(1, ROUNDS // 2) as i:
                for p in range(2):
                    coefficients_high(i * 2 + p, p)
                    values_high(p, i * 16 + 16)

            act.wait_ge(fin_made, 1)
            square_chunks(xfin, sqf, 2)
            root(2)

        @block.vector
        def _(dve):
            step = Chain(dve, dve_step)
            tt, ts, stt = dve.tensor_tensor, dve.tensor_scalar, dve.scalar_tensor_tensor
            mod = modT[:, :].rearrange("p (c n) -> p c n", n=NCOND)
            sc9 = scaleg[:, :].rearrange("p (c n) -> p c n", n=NCOND)

            def modulation(part):
                dve.wait_ge(ada_turned, 16 * (part + 1) + 2)
                return tt(mod[:, 32 * part:32 * part + 32],
                          bank(7 if part else 4, 0, 288).rearrange("p (c n) -> p c n", n=NCOND),
                          vec[:, V_BADA + 32 * part:V_BADA + 32 * part + 32].unsqueeze(2).broadcast_to([P, 32, NCOND]),
                          ALU.add)

            def inverse_root(n0, pair):
                dve.wait_ge(sq_used, KC * (n0 + 1))
                ts(rstd[:, :], flat(pair), 1.0 / D, EPS, ALU.mult, ALU.add).then_inc(ms_made, 1)
                dve.wait_ge(root_made, n0 + 1)
                step(dve.reciprocal(rstd[:, :], rstd[:, :]))

            def modulated(hT, src, gain, shift, scale):
                step(stt(sc9, mod[:, scale:scale + KC], 1.0,
                         vec[:, gain:gain + KC].unsqueeze(2).broadcast_to([P, KC, NCOND]), ALU.add, ALU.mult))
                step(tt(hT, src, rstd[:, :].unsqueeze(1).broadcast_to([P, KC, T]), ALU.mult))
                for c in range(KC):
                    ins = ts(hT[:, c, 0:TP], hT[:, c, 0:TP], sc9[:, c, 0:1], mod[:, shift + c, 0:1], ALU.mult, ALU.add)
                step(ins)
                hs = hT[:, :, TP:T].rearrange("p c (b t) -> p c b t", t=SLEN)
                wide = [P, KC, NSEQ, SLEN]
                step(tt(hs, hs, sc9[:, :, 1:NCOND].unsqueeze(3).broadcast_to(wide), ALU.mult))
                return tt(hs, hs, mod[:, shift:shift + KC, 1:NCOND].unsqueeze(3).broadcast_to(wide), ALU.add)

            for places, n in ((prod_out, 4), (sc_out, 2), (acc_made, 4)):
                dve.sem_inc(places, n)

            dve.wait_ge(x_in, 16)
            dve.wait_ge(small_in, 48)
            inverse_root(0, 3)
            ins = modulation(0)
            step(ins)
            modulated(hT, xT, V_NG1, 0, 16).then_inc(norm_made, 1)

            dve.wait_ge(gla_ln, 1)
            step(stt(g_la, g_la, 0.0, g_e2, ALU.min, ALU.subtract))
            dve.wait_ge(masks_made, 1)
            for p in range(3):
                step(dve.tensor_tensor_scan(g_B[:, p], gla_reset[:, :], g_la[:, p], 0.0, ALU.mult, ALU.add))
            for k, at_p, at_s in ((0, GMID, SMID), (1, GC - 1, SLEN - 1)):
                step(dve.tensor_copy(g_sc[:, k, :, 0:16], g_B[:, :, at_p:TP:GC]))
                step(dve.tensor_copy(g_sc[:, k, :, 16:24], g_B[:, :, TP + at_s:T:SLEN]))
            step(tt(g_sc[:, 2], g_sc[:, 1], g_sc[:, 0], ALU.subtract))

            def per_chunk(out, in_, k, op, p):
                ch = "p (n t) -> p n t"
                step(tt(out[:, p, 0:TP].rearrange(ch, t=GC), in_[:, p, 0:TP].rearrange(ch, t=GC),
                        g_sc[:, k, p, 0:16].unsqueeze(2).broadcast_to([P, 16, GC]), op))
                return tt(out[:, p, TP:T].rearrange(ch, t=SLEN), in_[:, p, TP:T].rearrange(ch, t=SLEN),
                          g_sc[:, k, p, 16:24].unsqueeze(2).broadcast_to([P, NSEQ, SLEN]), op)

            for p in range(3):
                ins = per_chunk(g_la, g_B, 0, ALU.subtract, p)
                if p < 2:
                    step(ins)
            ins.then_inc(gla_dist, 1)
            dve.wait_ge(gla_exp, 3)
            dve.wait_ge(prod_out, 34 + 4)
            gq, gk = zF[:, Z_GQ:Z_GQ + 3], zF[:, Z_GK:Z_GK + 3]
            step(stt(gq, gq, GDK ** -0.5, g_e1, ALU.mult, ALU.mult))
            step(tt(gk, gk, g_e2, ALU.mult))
            for p in range(3):
                ins = per_chunk(g_la, gk, 2, ALU.mult, p)
                if p < 2:
                    step(ins)
            ins.then_inc(gla_kdec, 1)

            for p in range(3):
                dve.wait_ge(gla_kv, p + 1)
                if p:
                    dve.wait_ge(gla_oatt, NT * p)
                    dve.wait_ge(gla_stored, 32 * p)

                def kv(c):
                    return bank(4 + c % 4, P * (c // 4), P)

                step(dve.tensor_copy(g_S[:, 1], kv(0)))
                for c in range(1, 16):
                    ts(g_Sm[:, c], g_S[:, c % 2], g_sc[:, 0, p, c:c + 1], None, ALU.mult)
                    step(stt(g_S[:, (c + 1) % 2], g_S[:, c % 2], g_sc[:, 1, p, c:c + 1], kv(c), ALU.mult, ALU.add))
                dve.wait_ge(gla_state_in, 16 * (p + 1))
                tt(g_S0m, g_S0, g_sc[:, 0, p, 16:24].unsqueeze(2).broadcast_to([P, NSEQ, P]), ALU.mult)
                dve.wait_ge(gla_ktok, NT)
                tt(g_kdm, g_kd[0:TS, 4:5, P * p:P * p + P].broadcast_to([TS, NSEQ, P]),
                   segm[:, :].unsqueeze(2).broadcast_to([TS, NSEQ, P]), ALU.mult).then_inc(gla_sm, 1)
                for n in range(NT):
                    dve.wait_ge(gla_att, NT * p + n + 1)
                    if 2 <= n < 4:
                        dve.wait_ge(gla_oatt, NT * p + n - 1)
                    for hh in range(2):
                        if n < 4:
                            ins = dve.copy_predicated(att_p[:, n % 2, hh], gla_mask[:, :], bank(4 * (n % 2) + hh, 0, P))
                        else:
                            ins = dve.copy_predicated(att_s[0:TS, hh], gla_smask[:, :], bank(hh, 0, TS, TS))
                    ins.then_inc(gla_attw, 1)
                dve.wait_ge(gla_kvs, p + 1)
                step(tt(g_S0, g_S0, g_sc[:, 1, p, 16:24].unsqueeze(2).broadcast_to([P, NSEQ, P]), ALU.mult))
                tt(g_S0, g_S0, PS[:, 2048:3072].rearrange("p (n c) -> p n c", c=P), ALU.add).then_inc(gla_states, 1)

            H6 = HEADS
            dve.wait_ge(ml_ln, 1)
            lf, li = rows[0:H6, 2], rows[0:H6, 1]
            mr = [m_rows[0:H6, k] for k in range(7)]
            step(stt(lf, lf, 0.0, mr[4], ALU.min, ALU.subtract))
            step(dve.tensor_tensor_scan(mr[0], ml_reset[0:H6, :], lf, 0.0, ALU.mult, ALU.add))
            step(dve.tensor_tensor_scan(mr[1][:, 0:TP], lf[:, 0:TP], li[:, 0:TP], 0.0, ALU.add, ALU.max))
            for b in range(NSEQ):
                lo = TP + SLEN * b
                step(dve.tensor_tensor_scan(mr[1][:, lo:lo + SLEN], lf[:, lo:lo + SLEN], li[:, lo:lo + SLEN],
                                            m0[:, b:b + 1], ALU.add, ALU.max))
            ms = m_small[0:H6]
            step(tt(mr[2], mr[0], mr[1], ALU.subtract))
            step(dve.memset(ms[:, 0:1], 0.0))
            step(dve.tensor_copy(ms[:, 1:4], mr[1][:, P - 1:TP - 1:P]))
            step(dve.tensor_copy(ms[:, 4:12], m0[:, :]))
            for k, lo in ((0, 12), (1, 24)):
                step(dve.tensor_copy(ms[:, lo:lo + 4], mr[k][:, P - 1:TP:P]))
                step(dve.tensor_copy(ms[:, lo + 4:lo + 12], mr[k][:, TP + SLEN - 1:T:SLEN]))
            step(tt(ms[:, 36:48], ms[:, 12:24], ms[:, 24:36], ALU.subtract))
            step(tt(ms[:, 48:60], ms[:, 36:48], ms[:, 0:12], ALU.add))
            step(tt(mr[5], li, mr[0], ALU.subtract))
            for dst, src, lo in ((mr[3], mr[2], 0), (mr[6], mr[5], 36)):
                step(tt(dst[:, 0:TP].rearrange("p (n t) -> p n t", t=P), src[:, 0:TP].rearrange("p (n t) -> p n t", t=P),
                        ms[:, lo:lo + 4].unsqueeze(2).broadcast_to([H6, 4, P]), ALU.add))
                step(tt(seqs(dst[:, TP:T]), seqs(src[:, TP:T]),
                        ms[:, lo + 4:lo + 12].unsqueeze(2).broadcast_to([H6, NSEQ, SLEN]), ALU.add))
            mq = zF[:, Z_MQ:Z_MQ + 6]
            ts(mq, mq, MDH ** -0.5, None, ALU.mult).then_inc(ml_pre, 1)
            dve.wait_ge(ml_cols, 1)
            cols = bank(0, 0, 60).rearrange("p (k n h) -> p k n h", k=2, h=H6)
            step(dve.tensor_copy(m_col[:, :, 0:4], cols[:, :, 0:4]))
            step(dve.tensor_copy(m_col[0:TS, :, 4], cols[0:TS, :, 4]))
            dve.tensor_copy(m_dec, bank(0, 64, 72).rearrange("p (h n) -> p h n", n=12)).then_inc(ml_colsout, 1)

            dve.wait_ge(ml_colsout, 1)
            for h in range(HEADS):
                cs = m_Cs[:, h % 2]
                dve.wait_ge(ml_bc, h + 1)
                if h:
                    dve.wait_ge(ml_kvs, h)
                    dve.wait_ge(ml_spread, 2 * h)
                step(tt(m_qw, zF[:, Z_MQ + h], flat(0), ALU.mult))
                for n in range(NT):
                    nr, src = (P, bank(6, P * n, P)) if n < 4 else (TS, bank(5, 384, P, TS))
                    ins = ts(m_kw[0:nr, n], src, m_col[0:nr, 1, n, h:h + 1], None, ALU.mult)
                ins.then_inc(ml_kw, 1)
                for n in range(NT):
                    nr, w, lo = (P, P, P * n) if n < 4 else (TS, TS, TP)
                    ins = stt(m_D[0:nr, lo:lo + w], PS[0:nr, 2048 + lo:2048 + lo + w], m_col[0:nr, 0, n, h:h + 1],
                              (cap if n < 4 else scap)[0:nr, 0:w], ALU.add, ALU.min)
                ins.then_inc(ml_arg, 1)
                dve.wait_ge(ml_kv, h + 1)
                if h:
                    dve.wait_ge(ml_stored[(h - 1) % 2], 64 * ((h - 1) // 2 + 1))
                step(dve.tensor_copy(m_C[:, 0], bank(7, 0, 129)))
                for n in range(1, 4):
                    src = bank(7, 129 * n, 129) if n < 3 else bank(1, P, 129)
                    step(stt(m_C[:, n], m_C[:, n - 1], m_dec[:, h, n:n + 1], src, ALU.mult, ALU.add))
                step(dve.tensor_copy(m_nb, m_C[:, 0:3, P:P + 1].broadcast_to([P, 3, P])))
                dve.wait_ge(ml_s, h + 1)
                dve.wait_ge(ml_exp, 2 * (h + 1))
                step(tt(m_D[:, 0:TP], m_D[:, 0:TP], bank(6), ALU.mult))
                tt(m_D[0:TS, TP:T], m_D[0:TS, TP:T], bank(7, 448, TS, TS), ALU.mult).then_inc(ml_sd, 1)
                dve.wait_ge(ml_o, h + 1)
                dve.wait_ge(ml_floor, h + 1)
                step(tt(m_E, flat(1), m_E, ALU.max))
                step(stt(m_E, flat(1), -1.0, m_E, ALU.mult, ALU.max))
                step(dve.reciprocal(m_E, m_E))
                step(tt(m_h[h], flat(0), m_E, ALU.mult))
                dve.wait_ge(ml_kvs, h + 1)
                dve.wait_ge(ml_spread, 2 * (h + 1))
                for b in range(NSEQ):
                    ins = stt(cs[:, b], cs[:, b], m_dec[:, h, 4 + b:5 + b], bank((4, 6, 7)[b // 3], 129 * (b % 3), 129),
                              ALU.mult, ALU.add)
                ins.then_inc(ml_head, 1)

            dve.wait_ge(hn_gate, 2)

            def head_out(c):
                dve.wait_ge(hn_root, c + 1)
                step(dve.reciprocal(n_rs[:, c % 2], n_rs[:, c % 2]))
                step(stt(n_rs[:, c % 2], raw_head(c), vec[:, V_GG + c:V_GG + c + 1], n_rs[:, c % 2], ALU.mult, ALU.mult))
                ins = tt(zF[:, c], n_rs[:, c % 2], zF[:, c], ALU.mult)
                ins.then_inc(hn_out, 1)
                dve.wait_ge(hn_out, c + 1)

            for c in range(12):
                dve.wait_ge(hn_sum, c + 1)
                ts(n_rs[:, c % 2], flat(c % 2), 1.0 / P, EPS, ALU.mult, ALU.add).then_inc(hn_ms, 1)
                if c:
                    head_out(c - 1)
            head_out(11)

            par = [s_par[:, k] for k in range(16)]
            lre, lim = vec[:, V_LRE:V_LRE + 16], vec[:, V_LIM:V_LIM + 16]
            dve.wait_ge(s5_ldt, 1)
            step(tt(par[2], lim, par[0], ALU.mult))
            tt(par[1], lre, par[0], ALU.mult).then_inc(s5_dt, 1)
            step(ts(par[11], par[2], 1.0 / (2 * np.pi), ROUNDER, ALU.mult, ALU.add))
            step(ts(par[11], par[11], ROUNDER, None, ALU.subtract))
            step(stt(par[12], par[11], -TWO_PI_HI, par[2], ALU.mult, ALU.add))
            step(stt(par[12], par[11], -TWO_PI_LO, par[12], ALU.mult, ALU.add))
            step(ts(par[4], par[12], 3.1415925, -3.1415925, ALU.min, ALU.max))
            step(ts(par[12], par[4], float(np.pi / 2), None, ALU.add))
            step(ts(par[11], par[12], float(np.pi), float(2 * np.pi), ALU.is_gt, ALU.mult))
            step(tt(par[12], par[12], par[11], ALU.subtract))
            ts(par[5], par[12], 3.1415925, -3.1415925, ALU.min, ALU.max).then_inc(s5_ang, 1)
            dve.wait_ge(s5_trig, 2)
            dve.wait_ge(s5_exp, 1)
            step(tt(par[6], par[3], par[5], ALU.mult))
            step(tt(par[7], par[3], par[4], ALU.mult))
            step(tt(par[8], lre, lre, ALU.mult))
            step(tt(par[11], lim, lim, ALU.mult))
            step(tt(par[8], par[8], par[11], ALU.add))
            step(dve.reciprocal(par[8], par[8]))
            step(ts(par[12], par[6], 1.0, None, ALU.subtract))
            step(tt(par[9], par[12], lre, ALU.mult))
            step(tt(par[11], par[7], lim, ALU.mult))
            step(tt(par[9], par[9], par[11], ALU.add))
            step(tt(par[9], par[9], par[8], ALU.mult))
            step(tt(par[10], par[7], lre, ALU.mult))
            step(tt(par[11], par[12], lim, ALU.mult))
            step(tt(par[10], par[10], par[11], ALU.subtract))
            step(tt(par[10], par[10], par[8], ALU.mult))
            dve.wait_ge(s5_in, 16 * 10)
            fr = par[9].unsqueeze(2).broadcast_to([P, S5C, 32])
            fi = par[10].unsqueeze(2).broadcast_to([P, S5C, 32])
            B = [s_B[:, k] for k in range(4)]
            step(tt(B[2], B[0], fr, ALU.mult))
            step(tt(B[3], B[1], fi, ALU.mult))
            step(tt(B[2], B[2], B[3], ALU.subtract))
            step(tt(B[3], B[1], fr, ALU.mult))
            step(tt(B[0], B[0], fi, ALU.mult))
            tt(B[3], B[3], B[0], ALU.add).then_inc(s5_bbar, 1)
            ts(s_CT[:, 1], s_CT[:, 1], -1.0, None, ALU.mult).then_inc(s5_bbar, 1)

            tc_, tsn = s_tab[:, 0], s_tab[:, 1]
            step(dve.tensor_copy(tc_[:, :, 0], par[5]))
            step(dve.tensor_copy(tsn[:, :, 0], par[4]))
            tmp = s_t[:, 0:2].rearrange("p k s t -> p (k s t)").rearrange("p (s t) -> p s t", s=S5C)
            n = 1
            while n < TC:
                cb = tc_[:, :, n - 1:n].broadcast_to([P, S5C, n])
                sb_ = tsn[:, :, n - 1:n].broadcast_to([P, S5C, n])
                step(tt(tc_[:, :, n:2 * n], tc_[:, :, 0:n], cb, ALU.mult))
                step(tt(tmp[:, :, 0:n], tsn[:, :, 0:n], sb_, ALU.mult))
                step(tt(tc_[:, :, n:2 * n], tc_[:, :, n:2 * n], tmp[:, :, 0:n], ALU.subtract))
                step(tt(tsn[:, :, n:2 * n], tc_[:, :, 0:n], sb_, ALU.mult))
                step(tt(tmp[:, :, 0:n], tsn[:, :, 0:n], cb, ALU.mult))
                step(tt(tsn[:, :, n:2 * n], tsn[:, :, n:2 * n], tmp[:, :, 0:n], ALU.add))
                n *= 2
            step(dve.memset(s_g0, 0.0))
            step(dve.memset(s_rhosm, 1.0))
            step(dve.memset(s_rhosm[:, 0:72:9], 0.0))

            def s5_y_out(i):
                c, q = divmod(i, 4)
                w, lo = (TC, TC * c) if c < 4 else (TS, TP)
                dve.wait_ge(s5_y, i + 1)
                stt(s_gl[:, q, lo:lo + w], zF[:, Z_SU + q, lo:lo + w], vec[:, V_SD + q:V_SD + q + 1],
                    bank(4 + i % 2, 0, w), ALU.mult, ALU.add).then_inc(s5_yout, 1)

            for i in range(20):
                c, q = divmod(i, 4)
                sample = c == 4
                w = TS if sample else TC
                if i == 5:
                    modulation(1).then_inc(mod1_made, 1)
                dve.wait_ge(s5_bu, i + 1)

                def four(ap):
                    return ap.rearrange("p j (b t) -> p j b t", t=SLEN) if sample else ap

                def table(k):
                    tb = s_tab[:, k, 4 * q:4 * q + 4, 0:(SLEN if sample else TC)]
                    return tb.unsqueeze(2).broadcast_to([P, 4, NSEQ, SLEN]) if sample else tb

                def scan_place(buf, k):
                    if not sample:
                        return buf[:, k, :, 0:TC]
                    return buf[:, k, :, 0:72].rearrange("p j (b t) -> p j b t", t=9)[:, :, :, 1:9]

                bu = [four(bank(2 * (i % 2) + k).rearrange("p (j x) -> p j x", j=4)[:, :, 0:w]) for k in range(2)]
                t4 = [four(s_t[:, k, :, 0:w]) for k in range(4)]
                cosn, sinn = table(0), table(1)
                tt(t4[0], bu[0], cosn, ALU.mult)
                tt(t4[1], bu[1], sinn, ALU.mult)
                tt(t4[2], bu[1], cosn, ALU.mult)
                ins = tt(t4[3], bu[0], sinn, ALU.mult)
                ins.then_inc(s5_buout, 1)
                dve.wait_ge(s5_buout, i + 1)
                step(tt(scan_place(s_in, 0), t4[0], t4[1], ALU.add))
                step(tt(scan_place(s_in, 1), t4[2], t4[3], ALU.subtract))
                if sample:
                    for k in range(2):
                        step(dve.tensor_copy(s_in[:, k, :, 0:72].rearrange("p j (b t) -> p j b t", t=9)[:, :, :, 0],
                                             s_h0[:, k, 4 * q:4 * q + 4, :]))
                for j in range(4):
                    s = 4 * q + j
                    if sample:
                        step(ts(s_rhos, s_rhosm, par[3][:, s:s + 1], None, ALU.mult))
                    for k in range(2):
                        n = 72 if sample else TC
                        ins = dve.tensor_tensor_scan(
                            s_g[:, k, j, 0:n], s_rhos if sample else par[3][:, s:s + 1].broadcast_to([P, TC]),
                            s_in[:, k, j, 0:n], 0.0 if sample else s_g0[:, k, s:s + 1], ALU.mult, ALU.add)
                        if sample:
                            step(ins)
                if not sample:
                    step(ins)
                g = [scan_place(s_g, k) for k in range(2)]
                hh = [four(s_h[:, k, :, 0:w]) for k in range(2)]
                if i:
                    dve.wait_ge(s5_y, i)
                step(tt(hh[0], g[0], cosn, ALU.mult))
                step(tt(t4[0], g[1], sinn, ALU.mult))
                step(tt(hh[0], hh[0], t4[0], ALU.subtract))
                step(tt(hh[1], g[0], sinn, ALU.mult))
                step(tt(t4[1], g[1], cosn, ALU.mult))
                step(tt(hh[1], hh[1], t4[1], ALU.add))
                if sample:
                    step(dve.tensor_copy(s_hn[:, 0, 4 * q:4 * q + 4, :], s_h[:, 0, :, SLEN - 1:TS:SLEN]))
                    dve.tensor_copy(s_hn[:, 1, 4 * q:4 * q + 4, :], s_h[:, 1, :, SLEN - 1:TS:SLEN]).then_inc(s5_h, 1)
                else:
                    if c == 3:
                        step(dve.tensor_copy(s_hp[:, :, 4 * q:4 * q + 4], s_h[:, :, :, TC - 1]))
                    dve.tensor_copy(s_g0[:, :, 4 * q:4 * q + 4], s_h[:, :, :, TC - 1]).then_inc(s5_h, 1)
                if i:
                    s5_y_out(i - 1)
            s5_y_out(19)
            modulation(2).then_inc(mod_made, 1)

            dve.wait_ge(s5_gelu, 1)
            for m in range(4):
                dve.wait_ge(s5_sig, m + 1)
                ins = tt(s_sg[:, m], s_sg[:, m], s_gl[:, m], ALU.mult)
                if m < 3:
                    step(ins)
            ins.then_inc(s5_mix, 1)
            dve.wait_ge(s5_sum, 1)
            ts(rstd[:, :], flat(0), 1.0 / 512, EPS, ALU.mult, ALU.add).then_inc(s5_mix, 1)
            dve.wait_ge(s5_sig, 6)
            step(dve.reciprocal(rstd[:, :], rstd[:, :]))
            for m in range(4):
                ins = stt(zF[:, Z_SU + m], s_sg[:, m], vec[:, V_SG + m:V_SG + m + 1], rstd[:, :], ALU.mult, ALU.mult)
                if m < 3:
                    step(ins)
            ins.then_inc(s5_mix, 1)

            dve.wait_ge(x_again, 16)

            def residual(i, base, m, dst, chunk, gate_chunk):
                xc = dst[:, bass.ds(chunk, 1), :].rearrange("p c t -> p (c t)")
                gcol = modT[:, bass.ds((chunk + gate_chunk) * NCOND, NCOND)]
                dve.wait_ge(prod_made, chunk + (base + 1))
                step(tt(seqs(gate_tmp), seqs(flat(m)[:, TP:T]), gcol[:, 1:NCOND].unsqueeze(2).broadcast_to([P, NSEQ, SLEN]),
                        ALU.mult))
                stt(xc[:, 0:TP], flat(m)[:, 0:TP], gcol[:, 0:1], xc[:, 0:TP], ALU.mult, ALU.add).then_inc(prod_out, 1)
                tt(xc[:, TP:T], xc[:, TP:T], gate_tmp, ALU.add).then_inc(res_made, 1)
                dve.wait_ge(res_made, chunk + 1)

            with dve.Fori(0, 8) as i:
                step.enter(i, 2)
                for m in range(2):
                    residual(i, 34, m, xres, i * 2 + m, 32)
            step.leave(8)

            dve.wait_ge(prod_out, 50 + 4)
            inverse_root(1, 3)
            modulated(h2T[:, :].rearrange("p (c t) -> p c t", t=T), xres, V_NG2, 48, 64).then_inc(norm_made, 1)

            dve.wait_ge(h_hi_made, 1)
            tt(h_lo[:, :], h2T[:, :], h_hi[:, :].bitcast(F32), ALU.subtract).then_inc(h_lo_made, 1)

            def low(n, k):
                dve.wait_ge(blk_hi_made, n + 1)
                tt(blk_lo[k][:, :], blk_raw[k], blk_hi[k][:, :].bitcast(F32), ALU.subtract).then_inc(blk_lo_made, 1)

            def score_out(c):
                dve.wait_ge(sc_made, c + 4)
                cs = slice(c, c + 1) if isinstance(c, int) else bass.ds(c, 1)
                dve.tensor_copy(p_sc[:, 0:4, cs, :].rearrange("p n c k -> p n (c k)"),
                                bank(6).rearrange("p (n k) -> p n k", k=NK)).then_inc(sc_out, 1)
                dve.tensor_copy(p_sc[0:TS, 4, cs, :].rearrange("p c k -> p (c k)"), bank(7, 0, NK, TS)).then_inc(sc_out, 1)

            low(0, 0)
            low(1, 1)
            dve.wait_ge(sc_clear, 1)
            with dve.Fori(0, NQ // 3) as i:
                for k in range(3):
                    low(i * 3 + (k + 2), (k + 2) % 3)
                    score_out(i * 3 + k)
            score_out(NQ - 1)

            def best16(vals, idx, scores, work):
                step(dve.max(vals[:, 0:8], scores))
                dve.max_index(idx[:, 0:8], vals[:, 0:8], scores)
                step(dve.match_replace(work, vals[:, 0:8], scores, -3.0e38))
                step(dve.max(vals[:, 8:16], work))
                return dve.max_index(idx[:, 8:16], vals[:, 8:16], work)

            dve.wait_ge(sc_out, 4 * PH + 2)
            lows = iter(range(NQ + 1, NB_ALL))

            def next_low():
                n = next(lows)
                low(n, n % 3)

            for n in range(NT):
                for c in range(2 * PH):
                    ins = best16(p_sv[:, c // 2, c % 2], p_siu[:, c], p_sc[:, n, c], p_rep[:, 0:NK])
                    if c in (2, 5, 8, 11, 15):
                        step(ins)
                        next_low()
                step(dve.tensor_copy(p_sif.rearrange("p h s k -> p (h s k)"), p_siu.rearrange("p c k -> p (c k)")))
                c3 = p_cand.rearrange("p (a b) -> p a b", b=TOPK)
                for h in range(PH):
                    step(tt(c3, p_sv[:, h, 0].unsqueeze(2).broadcast_to([P, TOPK, TOPK]),
                            p_sv[:, h, 1].unsqueeze(1).broadcast_to([P, TOPK, TOPK]), ALU.add))
                    step(best16(p_tv[:, h], p_posu[:, TOPK * h:TOPK * h + TOPK], p_cand, p_rep))
                    if h in (1, 3, 6):
                        next_low()
                mx = p_sm[:, 0:PH]
                step(dve.tensor_copy(mx, p_tv[:, :, 0]))
                tt(p_tv, p_tv, mx.unsqueeze(2).broadcast_to([P, PH, TOPK]), ALU.subtract).then_inc(soft_in, 1)
                step(ts(p_au, p_posu, 4, None, ALU.logical_shift_right))
                step(dve.tensor_copy(p_ab[:, 0], p_au))
                step(ts(p_au, p_posu, 15, None, ALU.bitwise_and))
                step(dve.tensor_copy(p_ab[:, 1], p_au))
                for s in range(2):
                    for x in range(2):
                        step(tt(p_oh, p_ab[:, s, 64 * x:64 * x + 64].unsqueeze(2).broadcast_to([P, 64, TOPK]),
                                iota[:, 0:TOPK].unsqueeze(1).broadcast_to([P, 64, TOPK]), ALU.is_equal))
                        oh4 = p_oh.rearrange("p (h k) a -> p h k a", k=TOPK)
                        step(tt(oh4, oh4, p_sif[:, 4 * x:4 * x + 4, s].unsqueeze(2).broadcast_to([P, 4, TOPK, TOPK]),
                                ALU.mult))
                        if s == 0 and x == 0 and n:
                            dve.wait_ge(sel_out, n)
                        step(dve.reduce_sum(p_sel[:, s, 64 * x:64 * x + 64], p_oh, AX.X))
                    if s == 0:
                        next_low()
                dve.wait_ge(soft_out, n + 1)
                sm = p_sm[:, PH:2 * PH]
                step(dve.reduce_sum(sm, p_tv, AX.X))
                step(dve.reciprocal(sm, sm))
                tt(p_sel[:, 2].rearrange("p (h k) -> p h k", k=TOPK), p_tv,
                   sm.unsqueeze(2).broadcast_to([P, PH, TOPK]), ALU.mult).then_inc(sel_made, 1)
                dve.wait_ge(sel_made, n + 1)

            assert next(lows) == GB - 1
            low(GB - 1, (GB - 1) % 3)
            low(GB, GB % 3)
            dve.wait_ge(sel_out, NT)
            t4_ = [P, 4, P]
            io = iota[:, :].unsqueeze(1).broadcast_to(t4_)
            with dve.Fori(0, GL) as w:
                step.enter(w, 32)
                for u in range(16):
                    n = w * 16 + u
                    dve.wait_ge(g_made, n + 1)
                    idx = [p_selT[:, r, bass.ds(n * 4, 4)].unsqueeze(2).broadcast_to(t4_) for r in range(3)]
                    step(tt(o_e, io, idx[0], ALU.is_equal))
                    step(tt(o_i[u % 2], o_e, idx[2], ALU.mult))
                    tt(o_j[u % 2], io, idx[1], ALU.is_equal).then_inc(oh_made, 1)
                    if u in (2, 7, 12):
                        b = (2, 7, 12).index(u)
                        low(w * 3 + (GB + 1 + b), (GB + 1 + b) % 3)
            step.leave(GL)

            n0 = GB + 3 * GL + 1
            with dve.Fori(0, (NB_ALL - n0) // 3) as i:
                for k in range(3):
                    low(i * 3 + (n0 + k), (n0 + k) % 3)
            for n in range(n0 + 3 * ((NB_ALL - n0) // 3), NB_ALL):
                low(n, n % 3)

            def coefficients(r, p, fills):
                dve.wait_ge(ag_in[p], fills)
                x4 = acts[p].rearrange("p (b n t) -> p n b t", b=GRP, t=TBLK)
                tt(x4, x4, gates[p], ALU.mult).then_inc(co_made, 1)

            def values_low(r, p, b):
                dve.wait_ge(ev_hi_made, r + 1)
                w = slice(D * b, D * b + D)
                tt(ev_lo[p][:, w], ev_raw[p][:, w], ev_hi[p][:, w].bitcast(F32), ALU.subtract).then_inc(ev_lo_made, 1)

            def coefficients_low(r, p):
                dve.wait_ge(co_hi_made, r + 1)
                tt(co_lo[p][:, :], acts[p], co_hi[p][:, :].bitcast(F32), ALU.subtract).then_inc(co_lo_made, 1)

            def add(r, c):
                dve.wait_ge(vp_made, r * KC + c + 2)
                tt(halves(acc[:, c]), halves(acc[:, c]), split(c % 4), ALU.add).then_inc(acc_made, 1)

            def round_(r, p, fills):
                for c in range(KC):
                    add(r, c)
                    if fills is None:
                        continue
                    if c == 4:
                        coefficients(r + 1, 1 - p, fills)
                    if c in (9, 12):
                        values_low(r + 1, 1 - p, (c - 9) // 3)
                    if c == 6:
                        coefficients_low(r + 1, 1 - p)

            for b in range(GRP):
                values_low(0, 0, b)
            coefficients(0, 0, 32)
            coefficients_low(0, 0)
            dve.wait_ge(acc_clear, 1)
            with dve.Fori(0, ROUNDS // 2 - 1) as i:
                round_(i * 2, 0, i * 32 + 32)
                round_(i * 2 + 1, 1, i * 32 + 64)
            round_(ROUNDS - 2, 0, 32 * (ROUNDS // 2))
            round_(ROUNDS - 1, 1, None)

            dve.wait_ge(acc_made, ROUNDS * KC + 4)
            dve.wait_ge(x_back, 16)
            acs = acc[:, :, TP:T].rearrange("p c (b t) -> p c b t", t=SLEN)
            step(tt(acs, acs, mod[:, 80:96, 1:NCOND].unsqueeze(3).broadcast_to([P, KC, NSEQ, SLEN]), ALU.mult))
            for c in range(KC):
                step(stt(xfin[:, c, 0:TP], acc[:, c, 0:TP], mod[:, 80 + c, 0:1], xfin[:, c, 0:TP], ALU.mult, ALU.add))
            tt(xfin[:, :, TP:T], xfin[:, :, TP:T], acc[:, :, TP:T], ALU.add).then_inc(fin_made, 1)
            inverse_root(2, 3)
            for c in range(KC):
                ins = stt(xfin[:, c], xfin[:, c], vec[:, V_FG + c:V_FG + c + 1], rstd[:, :], ALU.mult, ALU.mult)
            ins.then_inc(y_made, 1)

        @block.tensor
        def _(pe):
            mm = pe.matmul

            def sum_squares(src, n0, pair):
                pe.wait_ge(consts_made, 3)
                for c in range(KC):
                    pe.wait_ge(sq_made, n0 * KC + c + 1)
                    for lo, w in ((0, TP), (TP, TS)):
                        ins = mm(flat(pair)[:, lo:lo + w], ones[:, :], src[:, c % 2, lo:lo + w],
                                 start=c == 0, stop=c == KC - 1)
                    ins.then_inc(sq_used, 1)

            sl = siluc[:, :].rearrange("p (c n) -> p c n", n=NCOND)

            def turn_ada(out, s):
                for m in range(2):
                    ins = mm(out(m), ada_rows[:, WT * s + P * m:WT * s + P * m + P], ident[0:NCOND, 0:NCOND],
                             start=True, stop=True)
                ins.then_inc(ada_turned, 1)

            def ada_product(b, w):
                for c in range(KC):
                    ins = mm(bank(b, 0, WT, NCOND), sl[:, c], w[:, c, :], start=c == 0, stop=c == KC - 1)
                ins.then_inc(ada_made, 1)

            def ada_tile(u):
                if u:
                    pe.wait_ge(ada_out, 16 + u - 1 + 3)
                    if u - 1 == 16:
                        pe.wait_ge(mod1_made, 1)
                    turn_ada(lambda m: bank(7, NCOND * (2 * ((u - 1) % 16) + m), NCOND), (u - 1) % 2)
                if u < 32:
                    pe.wait_ge(ada_in[u % 2], 16 * (u // 2 + 1))
                    ada_product(6, ada_ring[u % 2])

            for places, n in ((sc_made, 3), (vp_made, 1), (g_made, 2), (ada_turned, 2)):
                pe.sem_inc(places, n)

            sum_squares(sq, 0, 3)
            pe.wait_ge(silu_made, 1)
            with pe.Fori(0, 8) as i:
                for s in range(2):
                    pe.wait_ge(ring_in[s], i * 16 + 16)
                    pe.wait_ge(ada_out, i * 2 + (s + 1))
                    ada_product(2 * s + 1, ring[s])
                for s in range(2):
                    pe.wait_ge(ada_out, i * 2 + (s + 3))
                    turn_ada(lambda m: PS[:, bass.ds(i * (4 * NCOND) + (512 * 4 + (2 * s + m) * NCOND), NCOND)], s)

            pe.wait_ge(norm_made, 1)
            pe.wait_ge(wsmall_in, 48)
            for lo, w in ((0, TP), (TP, TS)):
                for c in range(KC):
                    ins = mm(PS[0:70, 3072 + lo:3072 + lo + w], wsmall[:, c, :], hT[:, c, lo:lo + w],
                             start=c == 0, stop=c == KC - 1)
            ins.then_inc(small_made, 1)

            def product(s, m, pair, whole):
                for x in range(2):
                    lo, w = ((0, TP), (TP, TS))[x] if whole else (HALF * x, HALF)
                    out = flat(pair)[:, lo:lo + w] if whole else split(pair)[:, x]
                    for c in range(KC):
                        ins = mm(out, ring[s][:, c, P * m:P * m + P], (mixT if whole else hT)[:, c, lo:lo + w], start=c == 0, stop=c == KC - 1)
                return ins

            base = fills("f")
            pe.wait_ge(small_out, 3)
            with pe.Fori(0, 8) as i:
                for s in range(2):
                    pe.wait_ge(ring_in[s], i * 16 + 16 * (base[s] + 1))
                    for m in range(2):
                        pe.wait_ge(prod_out, i * 4 + (2 * s + m + 1))
                        ins = product(s, m, 2 * s + m, False)
                        ins.then_inc(prod_made, 1)
            pe.wait_ge(ring_in[0], 16 * (base[0] + 9))
            for m in range(2):
                pe.wait_ge(prod_out, 32 + m + 1)
                product(0, m, m, False).then_inc(prod_made, 1)

            base = fills("v")
            pe.wait_ge(prod_out, 34 + 4)
            with pe.Fori(0, 3) as i:
                for s in range(2):
                    pe.wait_ge(ring_in[s], i * 16 + 16 * (base[s] + 1))
                    for n in range(NT):
                        q = NT * s + n
                        nr = P if n < 4 else TS
                        pe.wait_ge(v_out, i * 10 + q + 1)
                        for c in range(KC):
                            ins = mm(bank(2 * (q % 2), 0, WT, nr), hT[:, c, P * n:P * n + nr], ring[s][:, c, :],
                                     start=c == 0, stop=c == KC - 1)
                        ins.then_inc(v_made, 1)

            pe.wait_ge(gla_w_in, 16)
            pe.wait_ge(v_out, 30 + 2)
            pe.wait_ge(masks_made, 1)
            for p in range(3):
                for lo, w in ((0, TP), (TP, TS)):
                    ins = mm(flat(p)[:, lo:lo + w], g_wgu[:, P * p:P * p + P], rows[0:16, 0, lo:lo + w],
                             start=True, stop=True)
                ins.then_inc(gla_lin, 1)
            pe.wait_ge(gla_kdec, 1)
            for n in range(NT):
                nr = P if n < 4 else TS
                for p in range(3):
                    ins = pe.transpose(bank(n, P * p, P, nr), g_la[:, p, P * n:P * n + nr], ident[:, :])
                ins.then_inc(gla_tr, 1)
            pe.wait_ge(gla_ktok, NT)
            for p in range(3):
                if p:
                    pe.wait_ge(gla_states, p)
                    pe.wait_ge(gla_oout, 2 * p)
                for c in range(16):
                    r = GC * (c % 4)
                    for hh in range(2):
                        ins = mm(bank(4 + c % 4, P * (c // 4), P, GDK, GDK * hh),
                                 g_kd[r:r + GC, c // 4, P * p + GDK * hh:P * p + GDK * hh + GDK],
                                 vT[r:r + GC, c // 4, P * (2 * p + hh):P * (2 * p + hh) + P], start=True, stop=True)
                ins.then_inc(gla_kv, 1)
                gq, gk = zF[:, Z_GQ + p], zF[:, Z_GK + p]

                def scores(n):
                    if n >= 2:
                        pe.wait_ge(gla_attw, NT * p + n - 1)
                    w = P if n < 4 else TS
                    for hh in range(2):
                        r = slice(GDK * hh, GDK * hh + GDK)
                        lo = P * n
                        ins = mm(bank(4 * (n % 2) + hh, 0, w, w), gk[r, lo:lo + w], gq[r, lo:lo + w], start=True, stop=True)
                    ins.then_inc(gla_att, 1)

                def outputs(n):
                    pe.wait_ge(gla_attw, NT * p + n + 1)
                    for hh in range(2):
                        r = slice(GDK * hh, GDK * hh + GDK)
                        v = slice(P * (2 * p + hh), P * (2 * p + hh) + P)
                        if n < 4:
                            out = bank(2 + hh, P * n, P)
                            ins = mm(out, vT[:, n, v], att_p[:, n % 2, hh], start=True, stop=True)
                            for k in range(4):
                                c = 4 * n + k
                                if c:
                                    ins = mm(out[:, GC * k:GC * k + GC], g_Sm[r, c], gq[r, GC * c:GC * c + GC],
                                             start=False, stop=True, skip_group_check=True)
                        else:
                            out = bank(6 + hh, 0, TS)
                            ins = mm(out, vT[:, n, v], att_s[:, hh], start=True, stop=True)
                            for b in range(NSEQ):
                                ins = mm(out[:, SLEN * b:SLEN * b + SLEN], g_S0m[r, b],
                                         gq[r, TP + SLEN * b:TP + SLEN * b + SLEN], start=False, stop=True,
                                         skip_group_check=True)
                    ins.then_inc(gla_oatt, 1)

                scores(0)
                pe.wait_ge(gla_sm, p + 1)
                scores(1)
                outputs(0)
                scores(2)
                outputs(1)
                scores(3)
                outputs(2)
                scores(4)
                outputs(3)
                outputs(4)
                for b in range(NSEQ):
                    for hh in range(2):
                        ins = mm(PS[GDK * hh:GDK * hh + GDK, 2048 + P * b:2048 + P * b + P],
                                 g_kdm[:, b, GDK * hh:GDK * hh + GDK], vT[0:TS, 4, P * (2 * p + hh):P * (2 * p + hh) + P],
                                 start=True, stop=True)
                ins.then_inc(gla_kvs, 1)

            pe.wait_ge(ml_rows, 4)
            pe.wait_ge(gla_oout, 6)
            for k, r in ((0, 5), (1, 6)):
                for n in range(NT):
                    nr = P if n < 4 else TS
                    pe.transpose(bank(0, (k * NT + n) * HEADS, HEADS, nr), m_rows[0:HEADS, r, P * n:P * n + nr],
                                 ident[0:HEADS, 0:HEADS])
            for h in range(HEADS):
                ins = mm(bank(0, 64 + 12 * h, 12), sel[0:HEADS, P * h:P * h + P], m_small[0:HEADS, 48:60],
                         start=True, stop=True)
            ins.then_inc(ml_cols, 1)
            pe.wait_ge(ml_colsout, 1)
            pe.wait_ge(gla_states, 3)
            for h in range(HEADS):
                if h:
                    pe.wait_ge(ml_head, h)
                q_, k_ = zF[:, Z_MQ + h], zF[:, Z_MK + h]
                v = slice(768 + P * h, 768 + P * h + P)
                for pair, r in ((0, 3), (1, 4), (2, 2)):
                    for lo, w in ((0, TP), (TP, TS)):
                        mm(flat(pair)[:, lo:lo + w], sel[0:HEADS, P * h:P * h + P], m_rows[0:HEADS, r, lo:lo + w],
                           start=True, stop=True)
                for n in range(4):
                    pe.transpose(bank(6, P * n, P), k_[:, P * n:P * n + P], ident[:, :])
                pe.transpose(bank(5, 384, P, TS), k_[:, TP:T], ident[:, :]).then_inc(ml_bc, 1)
                pe.wait_ge(ml_kw, h + 1)
                for n in range(4):
                    mm(bank(6, P * n, P), k_[:, P * n:P * n + P], q_[:, P * n:P * n + P], start=True, stop=True)
                mm(bank(7, 448, TS, TS), k_[:, TP:T], q_[:, TP:T], start=True, stop=True).then_inc(ml_s, 1)
                for n in range(4):
                    b_, lo = (7, 129 * n) if n < 3 else (1, P)
                    mm(bank(b_, lo, P), m_kw[:, n], vT[:, n, v], start=True, stop=True)
                    ins = mm(bank(b_, lo + P, 1), m_kw[:, n], ones[:, 0:1], start=True, stop=True)
                ins.then_inc(ml_kv, 1)
                pe.wait_ge(ml_sd, h + 1)
                pe.wait_ge(ml_floor, h + 1)
                pe.wait_ge(ml_spread, 2 * h + 2)
                for n in range(4):
                    lo = P * n
                    for pair, vv, st in ((0, vT[:, n, v], lambda n: m_C[:, n, 0:P]), (1, ones[:, :], lambda n: m_nb[:, n])):
                        out = flat(pair)[:, lo:lo + P]
                        mm(out, vv, m_D[:, lo:lo + P], start=True, stop=n == 0)
                        if n:
                            mm(out, st(n - 1), m_qw[:, lo:lo + P], start=False, stop=True)
                for pair, vv, st in ((0, vT[0:TS, 4, v], lambda b: m_Cs[:, h % 2, b, 0:P]),
                                     (1, ones[0:TS, :], lambda b: m_nbs[:, b])):
                    out = flat(pair)[:, TP:T]
                    mm(out, vv, m_D[0:TS, TP:T], start=True, stop=True)
                    for b in range(NSEQ):
                        ins = mm(out[:, SLEN * b:SLEN * b + SLEN], st(b), m_qw[:, TP + SLEN * b:TP + SLEN * b + SLEN],
                                 start=False, stop=True, skip_group_check=True)
                ins.then_inc(ml_o, 1)
                for b in range(NSEQ):
                    b_, lo = (4, 6, 7)[b // 3], 129 * (b % 3)
                    mm(bank(b_, lo, P), m_kwm[:, b], vT[0:TS, 4, v], start=True, stop=True)
                    ins = mm(bank(b_, lo + P, 1), m_kwm[:, b], ones[0:TS, 0:1], start=True, stop=True)
                ins.then_inc(ml_kvs, 1)

            pe.wait_ge(ml_head, HEADS)
            for c in range(12):
                pe.wait_ge(hn_sq, c + 1)
                if c >= 2:
                    pe.wait_ge(hn_ms, c - 1)
                for lo, w in ((0, TP), (TP, TS)):
                    ins = mm(flat(c % 2)[:, lo:lo + w], ones[:, :], n_sq[:, c % 2, lo:lo + w], start=True, stop=True)
                ins.then_inc(hn_sum, 1)
                ada_tile(c)

            pe.wait_ge(hn_ms, 12)
            pe.wait_ge(s5_bbar, 1)
            for k in range(2):
                for n in range(4):
                    ins = pe.transpose(bank(k, P * n, P), s_B[:, 2 + k, 4 * n:4 * n + 4, :].rearrange("p s c -> p (s c)"),
                                       ident[:, :])
                ins.then_inc(s5_bt, 1)
            pe.wait_ge(s5_ready, 2)
            pe.wait_ge(s5_bbar, 2)

            def s5_inputs(i):
                c, q = divmod(i, 4)
                w, lo = (TC, TC * c) if c < 4 else (TS, TP)
                if i >= 2:
                    pe.wait_ge(s5_buout, i - 1)
                for k in range(2):
                    for j in range(4):
                        ins = mm(bank(2 * (i % 2) + k, P * j, w), s_BT[:, k, 4 * q + j], zF[:, Z_SU + q, lo:lo + w],
                                 start=True, stop=True)
                ins.then_inc(s5_bu, 1)

            s5_inputs(0)
            for i in range(20):
                if i < 19:
                    s5_inputs(i + 1)
                c, q = divmod(i, 4)
                w = TC if c < 4 else TS
                pe.wait_ge(s5_h, i + 1)
                if i >= 2:
                    pe.wait_ge(s5_yout, i - 1)
                for j in range(4):
                    for k in range(2):
                        ins = mm(bank(4 + i % 2, 0, w, 32, 32 * j), s_CT[:, k, 4 * q + j, :], s_h[:, k, j, 0:w],
                                 start=k == 0, stop=k == 1)
                ins.then_inc(s5_y, 1)
                ada_tile(12 + i)
            ada_tile(32)
            pe.wait_ge(mod_made, 1)
            pe.wait_ge(s5_gelu, 1)
            for m in range(4):
                for lo, w in ((0, TP), (TP, TS)):
                    for c in range(4):
                        ins = mm(flat(m)[:, lo:lo + w], s_wg[:, c, P * m:P * m + P], s_gl[:, c, lo:lo + w],
                                 start=c == 0, stop=c == 3)
                ins.then_inc(s5_glu, 1)
            pe.wait_ge(s5_sig, 5)
            for lo, w in ((0, TP), (TP, TS)):
                for c in range(4):
                    ins = mm(flat(0)[:, lo:lo + w], ones[:, :], s_gl[:, c, lo:lo + w], start=c == 0, stop=c == 3)
            ins.then_inc(s5_sum, 1)

            pe.wait_ge(s5_mix, 3)
            pe.wait_ge(hn_out, 12)
            base = fills("out")
            with pe.Fori(0, 4) as i:
                for s in range(2):
                    pe.wait_ge(ring_in[s], i * 16 + 16 * (base[s] + 1))
                    for m in range(2):
                        pe.wait_ge(prod_out, i * 4 + (34 + 2 * s + m - 1 + 4))
                        product(s, m, m, True).then_inc(prod_made, 1)

            sum_squares(sq2, 1, 3)

            pe.wait_ge(h_hi_made, 1)
            pe.wait_ge(h_lo_made, 1)
            pe.wait_ge(keys_in, 16)

            def block_product(n, k, between=None):
                pe.wait_ge(blk_lo_made, n + 1)
                pe.wait_ge(blk_out, n + 1)
                hi = blk_hi[k][:, :].rearrange("p (c n) -> p c n", n=P)
                lo = blk_lo[k][:, :].rearrange("p (c n) -> p c n", n=P)
                for x in range(2):
                    cols = slice(HALF * x, HALF * x + HALF)
                    for c in range(KC):
                        mm(split(k)[:, x], hi[:, c], h_part[0][:, c, cols], start=c == 0, stop=False)
                        mm(split(k)[:, x], hi[:, c], h_part[1][:, c, cols], start=False, stop=False)
                        ins = mm(split(k)[:, x], lo[:, c], h_part[0][:, c, cols], start=False, stop=c == KC - 1)
                        if x == 1 and c == KC - 1:
                            ins.then_inc(blk_made, 1)
                        if between:
                            between(KC * x + c)

            def scores(c, k):
                pe.wait_ge(blk_out, c + 4)
                pe.wait_ge(sc_out, c * 2 + 2)
                keys = p_keys[:, c] if isinstance(c, int) else p_keys[:, bass.ds(c, 1), :].rearrange("p c k -> p (c k)")
                for n in range(NT):
                    nr = P if n < 4 else TS
                    ins = mm(bank(6, P * n, NK) if n < 4 else bank(7, 0, NK, TS), p_qT[:, k, P * n:P * n + nr], keys,
                             start=True, stop=True)
                ins.then_inc(sc_made, 1)

            def turn_selection(n):
                pe.wait_ge(sel_made, n + 1)
                pe.wait_ge(sc_out, 4 * PH + 2)
                for r in range(3):
                    ins = pe.transpose(bank(6, P * r, P), p_sel[:, r], ident[:, :])
                ins.then_inc(sel_tr, 1)

            block_product(0, 0)
            with pe.Fori(0, NQ // 3) as i:
                for k in range(3):
                    block_product(i * 3 + (k + 1), (k + 1) % 3)
                    scores(i * 3 + k, k)
            block_product(NQ, NQ % 3)
            scores(NQ - 1, (NQ - 1) % 3)
            block_product(NQ + 1, (NQ + 1) % 3)
            with pe.Fori(0, NT) as t:
                for b in range(TB):
                    block_product(t * TB + (NQ + 2 + b), (NQ + 2 + b) % 3)
                turn_selection(t)

            pe.wait_ge(sel_out, NT)
            with pe.Fori(0, GL) as w:
                def gate_products(x, b):
                    at_ = 2 * KC * b + x
                    if at_ % 6 != 5:
                        return
                    u = at_ // 6
                    pe.wait_ge(oh_made, w * 16 + u + 1)
                    pe.wait_ge(g_out, w * 16 + u + 1)
                    for t in range(4):
                        ins = mm(bank(6 + u % 2, P * t, P), o_j[u % 2][:, t], o_i[u % 2][:, t], start=True, stop=True)
                    ins.then_inc(g_made, 1)

                for b in range(3):
                    block_product(w * 3 + (GB + b), (GB + b) % 3, lambda x: gate_products(x, b))

            n0 = GB + 3 * GL
            with pe.Fori(0, (NB_ALL - n0) // 3) as i:
                for k in range(3):
                    block_product(i * 3 + (n0 + k), (n0 + k) % 3)
            assert (NB_ALL - n0) % 3 == 0

            with pe.Fori(0, ROUNDS // 2) as i:
                for p in range(2):
                    r = i * 2 + p
                    pe.wait_ge(ev_lo_made, r * GRP + GRP)
                    pe.wait_ge(co_lo_made, r + 1)
                    for c in range(KC):
                        pe.wait_ge(acc_made, r * KC + c + 1)
                        for x in range(2):
                            out = split(c % 4)[:, x]
                            for b in range(GRP):
                                w = slice(D * b + P * c, D * b + P * c + P)
                                m = slice(T * b + HALF * x, T * b + HALF * x + HALF)
                                mm(out, ev_hi[p][:, w], co_hi[p][:, m], start=b == 0, stop=False)
                                mm(out, ev_hi[p][:, w], co_lo[p][:, m], start=False, stop=False)
                                ins = mm(out, ev_lo[p][:, w], co_hi[p][:, m], start=False, stop=b == GRP - 1)
                        ins.then_inc(vp_made, 1)

            sum_squares(sqf, 2, 3)



def kernel(**inputs):
    from concourse import bacc
    from concourse.bass_utils import run_bass_kernel_spmd

    g = {k: np.ascontiguousarray(v) for k, v in inputs.items()}
    g = {k: v[0] if k not in ("x_prompt", "x_sample", "c_prompt", "c_sample", "final_gain") else v for k, v in g.items()}

    def chunks(w, rows_last=False):
        return w.reshape(-1, P, *w.shape[1:]).swapaxes(0, 1)

    def tiles(w):
        return w.reshape(KC, P, -1, WT).transpose(2, 1, 0, 3).reshape(-1, P, KC * WT)

    def vecs(*vs):
        return np.concatenate([chunks(v.reshape(-1)) for v in vs], axis=1)

    w_in = g["w_in"]
    c = np.concatenate([g["c_prompt"], g["c_sample"]])
    x = np.concatenate([g["x_prompt"].reshape(TP, D), g["x_sample"].reshape(TS, D)])
    ins = {
        "cT": chunks(c.T).reshape(P, -1),
        "xT": chunks(x.T),
        "vecs": vecs(g["norm_gain"][0], g["norm_gain"][1], g["final_gain"], g["b_ada"], g["gla_norm_gain"],
                     g["ml_norm_gain"], g["s5_norm_gain"], g["s5_b_glu"], g["s5_d"], g["gla_b_gate"],
                     g["s5_lambda_re"], g["s5_lambda_im"], np.repeat(g["s5_log_dt"], S5P)),
        "gate_bias": np.stack([g["ml_b_igate"], g["ml_b_fgate"]], axis=1),
        "m0": g["state_mlstm_m"].T,
        "w_ada": tiles(g["w_ada"]),
        "w_f": tiles(np.concatenate([w_in[:, lo:hi] for lo, hi in (
            (1536, 2304), (4624, 5392), (5404, 5916), (0, 384), (384, 768), (2320, 3088), (3088, 3856))], axis=1)),
        "w_v": tiles(np.concatenate([w_in[:, 768:1536], w_in[:, 3856:4624]], axis=1)),
        "w_s": chunks(np.concatenate([w_in[:, 2304:2320], w_in[:, 5392:5404]], axis=1)).reshape(P, -1),
        "w_gate_up": g["gla_w_gate_up"],
        "state_gla": g["state_gla"].reshape(NSEQ, HEADS * GDK, MDH),
        "state_c": g["state_mlstm_c"],
        "state_n": g["state_mlstm_n"].transpose(1, 2, 0),
        "s5_b": np.stack([g[k].reshape(S5C, 2, S5P, S5CH).transpose(1, 2, 0, 3) for k in ("s5_b_re", "s5_b_im")]),
        "s5_c": np.stack([g[k].reshape(S5C, 2, S5CH, S5P).transpose(1, 3, 0, 2) for k in ("s5_c_re", "s5_c_im")]),
        "s5_h0": np.stack([g[k].reshape(NSEQ, S5C, P).transpose(2, 1, 0) for k in ("state_s5_re", "state_s5_im")], axis=1),
        "w_glu": chunks(g["s5_w_glu"]).reshape(P, -1),
        "w_out": tiles(g["w_out"]),
        "w_q": g["peer_w_q"].reshape(KC, P, KC, P).transpose(2, 1, 0, 3).reshape(KC, P, D),
        "keysT": g["peer_sub_keys"].transpose(3, 0, 1, 2).reshape(P, -1),
        "peer_ut": g["peer_u"].reshape(NK, NK, KC, P).transpose(0, 3, 2, 1).reshape(NK, P, D),
        "peer_v": g["peer_v"].reshape(NK, P, D),
    }
    outs = {
        "yT": (P, KC, T), "gla_p": (HEADS * GDK, MDH), "gla_s": (NSEQ, HEADS * GDK, MDH),
        "c_p": (HEADS, P, P), "n_p": (P, HEADS), "c_s": (NSEQ, HEADS, P, P), "n_s": (HEADS, P, NSEQ),
        "m_p": (HEADS, 1), "m_s": (HEADS, NSEQ), "s5_s": (P, 2, S5C, NSEQ), "s5_p": (P, 2, S5C),
    }
    nc = bacc.Bacc("TRN2", target_bir_lowering=False, num_devices=1)
    arrays = {f"in_{k}": np.ascontiguousarray(v) for k, v in ins.items()}
    a = {k: nc.dram_tensor(f"in_{k}", arrays[f"in_{k}"].shape, F32, kind="ExternalInput").ap() for k in ins}
    o = {k: nc.dram_tensor(f"out_{k}", s, F32, kind="ExternalOutput").ap() for k, s in outs.items()}
    build(nc, a, o)
    r = run_bass_kernel_spmd(nc, [arrays], core_ids=[0]).results[0]
    r = {k: np.asarray(r[f"out_{k}"]) for k in outs}

    y = r["yT"].transpose(2, 1, 0).reshape(T, D)
    s5_s = r["s5_s"].transpose(1, 3, 2, 0).reshape(2, 1, NSEQ, 2 * S5C, S5P)
    s5_p = r["s5_p"].transpose(1, 2, 0).reshape(2, 1, 1, 2 * S5C, S5P)
    return (y[:TP].reshape(1, TP, D), y[TP:].reshape(NSEQ, SLEN, D),
            r["gla_p"].reshape(1, 1, HEADS, GDK, MDH), r["gla_s"].reshape(1, NSEQ, HEADS, GDK, MDH),
            r["c_p"].reshape(1, 1, HEADS, P, P), r["c_s"].reshape(1, NSEQ, HEADS, P, P),
            r["n_p"].T.reshape(1, 1, HEADS, P), r["n_s"].transpose(2, 0, 1).reshape(1, NSEQ, HEADS, P),
            r["m_p"].reshape(1, 1, HEADS), r["m_s"].T.reshape(1, NSEQ, HEADS),
            s5_p[0], s5_s[0], s5_p[1], s5_s[1])
```
